# Optimizing a Trainium2 kernel written in Bass

```python
import math
import jax, jax.numpy as jnp
from jax import lax
import numpy as np

D_MODEL = 1024
BATCH = 1
SEQ = 512
DEPTH = 1

MIX_WIDTH = D_MODEL
SSM_WIDTH = MIX_WIDTH // 2
ATTN_WIDTH = MIX_WIDTH - SSM_WIDTH
SSM_GROUP = 16
SSM_GROUPS = SSM_WIDTH // SSM_GROUP
SSM_STATE = 64
HEAD_DIM = 64
N_HEADS = ATTN_WIDTH // HEAD_DIM
IDX_HEADS = 8
IDX_DIM = 64
TOPK_MAX = 256
QBLOCK = 32
NUM_BUCKETS = 32
MAX_DISTANCE = 128
EPS = 1e-6
DT_MIN = 1e-3
DT_MAX = 1e-1
SPLITS = (SSM_WIDTH, SSM_WIDTH, ATTN_WIDTH, ATTN_WIDTH, ATTN_WIDTH, ATTN_WIDTH,
          IDX_HEADS * IDX_DIM, IDX_DIM, IDX_HEADS)
IN_WIDTH = 2 * SSM_WIDTH + 4 * ATTN_WIDTH + IDX_HEADS * IDX_DIM + IDX_DIM + IDX_HEADS


def rms_norm(x, g):
    xf = x.astype(jnp.float32)
    xf = xf * lax.rsqrt(jnp.mean(xf * xf, axis=-1, keepdims=True) + EPS)
    return (xf * g.astype(jnp.float32)).astype(x.dtype)

def t5_causal_bucket(dist):
    max_exact = NUM_BUCKETS // 2
    is_small = dist < max_exact
    d = jnp.maximum(dist, 1).astype(jnp.float32)
    large = max_exact + (jnp.log(d / max_exact) / math.log(MAX_DISTANCE / max_exact)
                         * (NUM_BUCKETS - max_exact)).astype(jnp.int32)
    large = jnp.minimum(large, NUM_BUCKETS - 1)
    return jnp.where(is_small, dist, large)

def _ssm_combine(e1, e2):
    a1, b1 = e1
    a2, b2 = e2
    return a1 * a2, a2 * b1 + b2

def s5_mixer(u, a_re, a_im, log_dt, b_re, b_im, c_re, c_im, d_skip, w_glu, b_glu):
    bsz, seq, _ = u.shape
    uf = u.astype(jnp.float32)
    ug = uf.reshape(bsz, seq, SSM_GROUPS, SSM_GROUP)
    lam = lax.complex(a_re.astype(jnp.float32), a_im.astype(jnp.float32))
    dt = jnp.exp(log_dt.astype(jnp.float32))[:, None]
    lam_bar = jnp.exp(lam * dt)
    b_mat = lax.complex(b_re.astype(jnp.float32), b_im.astype(jnp.float32))
    b_bar = ((lam_bar - 1.0) / lam)[..., None] * b_mat
    bu = jnp.einsum('gpc,bsgc->bsgp', b_bar, ug.astype(jnp.complex64))
    a_seq = jnp.broadcast_to(lam_bar, (1, seq) + lam_bar.shape)
    _, states = lax.associative_scan(_ssm_combine, (a_seq, bu), axis=1)
    c_mat = lax.complex(c_re.astype(jnp.float32), c_im.astype(jnp.float32))
    y = jnp.einsum('gcp,bsgp->bsgc', c_mat, states).real.reshape(bsz, seq, SSM_WIDTH)
    y = y + d_skip.astype(jnp.float32) * uf
    z = jax.nn.gelu(y)
    z = z * jax.nn.sigmoid(z @ w_glu.astype(jnp.float32) + b_glu.astype(jnp.float32))
    return z.astype(u.dtype)

def dsa_mixer(q, k, v, q_idx, k_idx, w_idx, q_gain, k_gain, rel_bias):
    bsz, seq = q.shape[0], q.shape[1]
    topk = min(TOPK_MAX, seq // 4)
    nb = seq // QBLOCK
    scale = HEAD_DIM ** -0.5
    q = rms_norm(q.reshape(bsz, seq, N_HEADS, HEAD_DIM), q_gain)
    k = rms_norm(k.reshape(bsz, seq, N_HEADS, HEAD_DIM), k_gain)
    v = v.reshape(bsz, seq, N_HEADS, HEAD_DIM)
    q_idx = q_idx.reshape(bsz, seq, IDX_HEADS, IDX_DIM)
    w_idx = w_idx * (IDX_HEADS ** -0.5)
    key_pos = jnp.arange(seq, dtype=jnp.int32)

    def to_blocks(t):
        return jnp.moveaxis(t.reshape((bsz, nb, QBLOCK) + t.shape[2:]), 1, 0)

    gather = jax.vmap(lambda src, idx: src[idx])

    def block(args):
        qb, qib, wib, pos = args
        rel = jnp.einsum('bqhd,bsd->bqhs', qib, k_idx)
        score = jnp.einsum('bqh,bqhs->bqs', wib, jax.nn.relu(rel)).astype(jnp.float32)
        causal = key_pos[None, :] <= pos[:, None]
        score = jnp.where(causal[None], score, -jnp.inf)
        _, sel = lax.top_k(score, topk)
        k_sel = gather(k, sel)
        v_sel = gather(v, sel)
        logits = jnp.einsum('bqhd,bqkhd->bqhk', qb, k_sel).astype(jnp.float32) * scale
        dist = pos[None, :, None] - sel
        bias = rel_bias[t5_causal_bucket(jnp.maximum(dist, 0))]
        logits = logits + jnp.transpose(bias, (0, 1, 3, 2)).astype(jnp.float32)
        logits = jnp.where((dist >= 0)[:, :, None, :], logits, -jnp.inf)
        p = jax.nn.softmax(logits, axis=-1).astype(v.dtype)
        return jnp.einsum('bqhk,bqkhd->bqhd', p, v_sel)

    out = lax.map(block, (to_blocks(q), to_blocks(q_idx), to_blocks(w_idx),
                          key_pos.reshape(nb, QBLOCK)))
    return jnp.moveaxis(out, 0, 1).reshape(bsz, seq, ATTN_WIDTH)

def first_inputs(seed: int = 0) -> dict:
    key = jax.random.key(seed)
    ks = jax.random.split(key, 24)
    f32 = jnp.float32
    x = jax.random.normal(ks[0], (BATCH, SEQ, D_MODEL), f32)
    c = jax.random.normal(ks[1], (BATCH, D_MODEL), f32)
    rel_bias = 0.5 * jax.random.normal(ks[2], (NUM_BUCKETS, N_HEADS), f32)
    norm_g = 1.0 + 0.05 * jax.random.normal(ks[3], (DEPTH, D_MODEL), f32)
    w_ada = 0.5 * D_MODEL ** -0.5 * jax.random.normal(ks[4], (DEPTH, D_MODEL, 3 * D_MODEL), f32)
    b_ada = 0.01 * jax.random.normal(ks[5], (DEPTH, 3 * D_MODEL), f32)
    w_in = D_MODEL ** -0.5 * jax.random.normal(ks[6], (DEPTH, D_MODEL, IN_WIDTH), f32)
    q_gain = 1.0 + 0.05 * jax.random.normal(ks[7], (DEPTH, HEAD_DIM), f32)
    k_gain = 1.0 + 0.05 * jax.random.normal(ks[8], (DEPTH, HEAD_DIM), f32)
    n = jnp.arange(SSM_STATE, dtype=f32)
    a_re = -0.5 + 0.01 * jax.random.normal(ks[9], (DEPTH, SSM_GROUPS, SSM_STATE), f32)
    a_im = math.pi * n + 0.01 * jax.random.normal(ks[10], (DEPTH, SSM_GROUPS, SSM_STATE), f32)
    log_dt = jax.random.uniform(ks[11], (DEPTH, SSM_GROUPS), f32,
                                minval=math.log(DT_MIN), maxval=math.log(DT_MAX))
    b_re = (2 * SSM_GROUP) ** -0.5 * jax.random.normal(ks[12], (DEPTH, SSM_GROUPS, SSM_STATE, SSM_GROUP), f32)
    b_im = (2 * SSM_GROUP) ** -0.5 * jax.random.normal(ks[13], (DEPTH, SSM_GROUPS, SSM_STATE, SSM_GROUP), f32)
    c_re = (2 * SSM_STATE) ** -0.5 * jax.random.normal(ks[14], (DEPTH, SSM_GROUPS, SSM_GROUP, SSM_STATE), f32)
    c_im = (2 * SSM_STATE) ** -0.5 * jax.random.normal(ks[15], (DEPTH, SSM_GROUPS, SSM_GROUP, SSM_STATE), f32)
    d_skip = jax.random.normal(ks[16], (DEPTH, SSM_WIDTH), f32)
    w_glu = SSM_WIDTH ** -0.5 * jax.random.normal(ks[17], (DEPTH, SSM_WIDTH, SSM_WIDTH), f32)
    b_glu = 0.01 * jax.random.normal(ks[18], (DEPTH, SSM_WIDTH), f32)
    w_out = MIX_WIDTH ** -0.5 * jax.random.normal(ks[19], (DEPTH, MIX_WIDTH, D_MODEL), f32)
    return {"x": x, "c": c, "rel_bias": rel_bias, "norm_g": norm_g, "w_ada": w_ada,
            "b_ada": b_ada, "w_in": w_in, "q_gain": q_gain, "k_gain": k_gain,
            "a_re": a_re, "a_im": a_im, "log_dt": log_dt, "b_re": b_re, "b_im": b_im,
            "c_re": c_re, "c_im": c_im, "d_skip": d_skip, "w_glu": w_glu, "b_glu": b_glu,
            "w_out": w_out}

def first_block(x, c, rel_bias, norm_g, w_ada, b_ada, w_in, q_gain, k_gain, a_re, a_im,
              log_dt, b_re, b_im, c_re, c_im, d_skip, w_glu, b_glu, w_out):
    split_points = np.cumsum(SPLITS)[:-1].tolist()
    cond = jax.nn.silu(c)
    for l in range(DEPTH):
        mod = cond @ w_ada[l] + b_ada[l]
        shift, scale, gate = jnp.split(mod, 3, axis=-1)
        h = rms_norm(x, norm_g[l]) * (1.0 + scale[:, None, :]) + shift[:, None, :]
        proj = h @ w_in[l]
        ssm_u, ssm_z, q, k, v, attn_z, q_idx, k_idx, w_idx = jnp.split(proj, split_points, axis=-1)
        y_ssm = s5_mixer(ssm_u, a_re[l], a_im[l], log_dt[l], b_re[l], b_im[l], c_re[l], c_im[l],
                         d_skip[l], w_glu[l], b_glu[l]) * jax.nn.silu(ssm_z)
        y_attn = dsa_mixer(q, k, v, q_idx, k_idx, w_idx, q_gain[l], k_gain[l], rel_bias) * jax.nn.silu(attn_z)
        y = jnp.concatenate([y_ssm, y_attn], axis=-1) @ w_out[l]
        x = x + gate[:, None, :] * y
    return x


RET_HEADS = 4
RET_DK = 128
RET_DV = 256
RET_CHUNK = 128
GLA_HEADS = 4
GLA_DK = 128
GLA_DV = 256
GLA_RANK = 16
GLA_TAU = 16.0
GLA_LOG_GATE_MIN = -1.0
GLA_CHUNK = 64
SWA_Q_HEADS = 16
SWA_KV_HEADS = 4
SWA_HEAD_DIM = 64
SWA_WINDOW = 128
N_BRANCH = 3
BRANCH_WIDTH = RET_HEADS * RET_DV
D_FF = -(-8 * D_MODEL // (3 * 256)) * 256
NORM_EPS = 1e-6
GN_EPS = 1e-5

IN_SPLITS = (
    RET_HEADS * RET_DK, RET_HEADS * RET_DK, RET_HEADS * RET_DV, RET_HEADS * RET_DV,
    GLA_HEADS * GLA_DK, GLA_HEADS * GLA_DK, GLA_HEADS * GLA_DV, GLA_HEADS * GLA_DV, GLA_RANK,
    SWA_Q_HEADS * SWA_HEAD_DIM, SWA_KV_HEADS * SWA_HEAD_DIM, SWA_KV_HEADS * SWA_HEAD_DIM,
    N_BRANCH * D_MODEL,
)
D_IN = sum(IN_SPLITS)


def _split_points():
    return [int(o) for o in np.cumsum(IN_SPLITS)[:-1]]

def rmsnorm(x, w):
    xf = x.astype(jnp.float32)
    y = xf * lax.rsqrt(jnp.mean(xf * xf, axis=-1, keepdims=True) + NORM_EPS)
    return (y * w.astype(jnp.float32)).astype(x.dtype)

def head_groupnorm(o, w, b):
    B, S, H, dv = o.shape
    of = o.astype(jnp.float32)
    mu = jnp.mean(of, axis=-1, keepdims=True)
    var = jnp.mean(jnp.square(of - mu), axis=-1, keepdims=True)
    y = ((of - mu) * lax.rsqrt(var + GN_EPS)).reshape(B, S, H * dv)
    return y * w.astype(jnp.float32) + b.astype(jnp.float32)

def head_rmsnorm(o, w):
    B, S, H, dv = o.shape
    of = o.astype(jnp.float32)
    y = of * lax.rsqrt(jnp.mean(of * of, axis=-1, keepdims=True) + NORM_EPS)
    return y.reshape(B, S, H * dv) * w.astype(jnp.float32)

def retention(q, k, v):
    B, S, H, dk = q.shape
    dv = v.shape[-1]
    C = RET_CHUNK
    N = S // C
    log_g = jnp.log1p(-jnp.exp2(-5.0 - jnp.arange(H, dtype=jnp.float32)))
    q = (q * dk ** -0.5).reshape(B, N, C, H, dk)
    k = k.reshape(B, N, C, H, dk)
    v = v.reshape(B, N, C, H, dv)
    pos = jnp.arange(C, dtype=jnp.float32)
    rel = pos[:, None] - pos[None, :]
    decay = jnp.exp(jnp.where((rel >= 0)[None], rel[None] * log_g[:, None, None], -jnp.inf))
    scores = jnp.einsum('bnihd,bnjhd->bnhij', q, k) * decay
    intra = jnp.einsum('bnhij,bnjhe->bnihe', scores, v)
    zeta = jnp.exp((C - 1 - pos)[None, :] * log_g[:, None])
    kv = jnp.einsum('bnjhd,bnjhe,hj->nbhde', k, v, zeta)
    gamma_c = jnp.exp(C * log_g)[None, :, None, None]

    def step(R, kv_n):
        return gamma_c * R + kv_n, R

    _, states = lax.scan(step, jnp.zeros(kv.shape[1:], kv.dtype), kv)
    xi = jnp.exp((pos + 1.0)[:, None] * log_g[None, :])
    inter = jnp.einsum('bnihd,nbhde->bnihe', q * xi[:, :, None], states)
    return (intra + inter).reshape(B, S, H, dv)

def gla(q, k, v, log_a):
    B, S, H, dk = q.shape
    dv = v.shape[-1]
    C = GLA_CHUNK
    N = S // C
    q = (q * dk ** -0.5).reshape(B, N, C, H, dk)
    k = k.reshape(B, N, C, H, dk)
    v = v.reshape(B, N, C, H, dv)
    b = jnp.cumsum(log_a.reshape(B, N, C, H, dk), axis=2)
    b_last = b[:, :, -1:]
    q_dec = q * jnp.exp(b)
    k_inv = k * jnp.exp(-b)
    causal = jnp.tril(jnp.ones((C, C), dtype=bool))
    A = jnp.where(causal, jnp.einsum('bnihd,bnjhd->bnhij', q_dec, k_inv), 0.0)
    intra = jnp.einsum('bnhij,bnjhe->bnihe', A, v)
    kv = jnp.einsum('bnjhd,bnjhe->nbhde', k * jnp.exp(b_last - b), v)
    chunk_decay = jnp.moveaxis(jnp.exp(b_last[:, :, 0]), 1, 0)

    def step(St, inp):
        kv_n, a_n = inp
        return a_n[..., None] * St + kv_n, St

    _, states = lax.scan(step, jnp.zeros(kv.shape[1:], kv.dtype), (kv, chunk_decay))
    inter = jnp.einsum('bnihd,nbhde->bnihe', q_dec, states)
    return (intra + inter).reshape(B, S, H, dv)

def swa_sinks(q, k, v, sinks):
    B, S, Hq, dh = q.shape
    Hkv = k.shape[2]
    G = Hq // Hkv
    W = SWA_WINDOW
    N = S // W
    slopes = jnp.exp2(-8.0 * jnp.arange(1, Hq + 1, dtype=jnp.float32) / Hq).reshape(Hkv, G)
    qb = q.reshape(B, N, W, Hkv, G, dh)
    kb = k.reshape(B, N, W, Hkv, dh)
    vb = v.reshape(B, N, W, Hkv, dh)

    def with_prev(t):
        prev = jnp.pad(t[:, :-1], ((0, 0), (1, 0), (0, 0), (0, 0), (0, 0)))
        return jnp.concatenate([prev, t], axis=2)

    kk, vv = with_prev(kb), with_prev(vb)
    scores = jnp.einsum('bnqhgd,bnkhd->bnhgqk', qb, kk).astype(jnp.float32) * dh ** -0.5
    qpos = W + jnp.arange(W)
    kpos = jnp.arange(2 * W)
    dist = qpos[:, None] - kpos[None, :]
    blk = jnp.arange(N)
    valid = ((dist >= 0) & (dist < W))[None] & ((blk[:, None, None] > 0) | (kpos[None, None, :] >= W))
    logits = scores - slopes[:, :, None, None] * dist.astype(jnp.float32)
    logits = jnp.where(valid[None, :, None, None], logits, -jnp.inf)
    sink = sinks.astype(jnp.float32).reshape(Hkv, G)[:, :, None, None]
    m = jnp.maximum(jnp.max(logits, axis=-1, keepdims=True), sink)
    p = jnp.exp(logits - m)
    probs = p / (jnp.sum(p, axis=-1, keepdims=True) + jnp.exp(sink - m))
    out = jnp.einsum('bnhgqk,bnkhd->bnqhgd', probs.astype(v.dtype), vv)
    return out.reshape(B, S, Hq * dh)

def second_inputs(seed: int = 0) -> dict:
    key = jax.random.key(seed)
    ks = jax.random.split(key, 17)
    f32 = jnp.float32

    def nrm(k, shape, scale):
        return jax.random.normal(k, shape, f32) * scale

    def gain(k, n):
        return 1.0 + nrm(k, (DEPTH, n), 0.05)

    return {
        'x': nrm(ks[0], (BATCH, SEQ, D_MODEL), 1.0),
        'norm_mix_pre': gain(ks[1], D_MODEL),
        'norm_mix_post': gain(ks[2], D_MODEL),
        'w_in': nrm(ks[3], (DEPTH, D_MODEL, D_IN), D_MODEL ** -0.5),
        'ret_norm_w': gain(ks[4], RET_HEADS * RET_DV),
        'ret_norm_b': nrm(ks[5], (DEPTH, RET_HEADS * RET_DV), 0.02),
        'gla_w_alpha2': nrm(ks[6], (DEPTH, GLA_RANK, GLA_HEADS * GLA_DK), GLA_RANK ** -0.5),
        'gla_b_alpha': nrm(ks[7], (DEPTH, GLA_HEADS * GLA_DK), 0.1),
        'gla_norm_w': gain(ks[8], GLA_HEADS * GLA_DV),
        'attn_sinks': nrm(ks[9], (DEPTH, SWA_Q_HEADS), 0.5),
        'w_branch': nrm(ks[10], (DEPTH, N_BRANCH, BRANCH_WIDTH, D_MODEL), BRANCH_WIDTH ** -0.5),
        'w_out': nrm(ks[11], (DEPTH, D_MODEL, D_MODEL), D_MODEL ** -0.5),
        'norm_ffn_pre': gain(ks[12], D_MODEL),
        'norm_ffn_post': gain(ks[13], D_MODEL),
        'ffn_w_gate': nrm(ks[14], (DEPTH, D_MODEL, D_FF), D_MODEL ** -0.5),
        'ffn_w_up': nrm(ks[15], (DEPTH, D_MODEL, D_FF), D_MODEL ** -0.5),
        'ffn_w_down': nrm(ks[16], (DEPTH, D_FF, D_MODEL), D_FF ** -0.5),
    }

def second_block(x, norm_mix_pre, norm_mix_post, w_in, ret_norm_w, ret_norm_b, gla_w_alpha2,
              gla_b_alpha, gla_norm_w, attn_sinks, w_branch, w_out, norm_ffn_pre, norm_ffn_post,
              ffn_w_gate, ffn_w_up, ffn_w_down):
    B, S, _ = x.shape
    split_points = _split_points()
    for l in range(DEPTH):
        h = rmsnorm(x, norm_mix_pre[l])
        proj = h @ w_in[l]
        (rq, rk, rv, rg, gq, gk, gv, gg, ga, sq, sk, sv, gate_logits) = jnp.split(proj, split_points, axis=-1)

        o_ret = retention(rq.reshape(B, S, RET_HEADS, RET_DK), rk.reshape(B, S, RET_HEADS, RET_DK),
                          rv.reshape(B, S, RET_HEADS, RET_DV))
        o_ret = (head_groupnorm(o_ret, ret_norm_w[l], ret_norm_b[l]) * jax.nn.silu(rg)).astype(x.dtype)

        z = (ga @ gla_w_alpha2[l] + gla_b_alpha[l]).astype(jnp.float32)
        log_a = jnp.maximum(jax.nn.log_sigmoid(z) / GLA_TAU, GLA_LOG_GATE_MIN)
        o_gla = gla(gq.reshape(B, S, GLA_HEADS, GLA_DK), gk.reshape(B, S, GLA_HEADS, GLA_DK),
                    gv.reshape(B, S, GLA_HEADS, GLA_DV), log_a.reshape(B, S, GLA_HEADS, GLA_DK))
        o_gla = (head_rmsnorm(o_gla, gla_norm_w[l]) * jax.nn.silu(gg)).astype(x.dtype)

        o_swa = swa_sinks(sq.reshape(B, S, SWA_Q_HEADS, SWA_HEAD_DIM),
                          sk.reshape(B, S, SWA_KV_HEADS, SWA_HEAD_DIM),
                          sv.reshape(B, S, SWA_KV_HEADS, SWA_HEAD_DIM), attn_sinks[l]).astype(x.dtype)

        branches = jnp.stack([o_ret, o_gla, o_swa], axis=2)
        projected = jnp.einsum('bsnc,ncd->bsnd', branches, w_branch[l])
        gates = jax.nn.sigmoid(gate_logits.reshape(B, S, N_BRANCH, D_MODEL))
        merged = jnp.sum(gates * projected, axis=2)
        x = x + rmsnorm(merged @ w_out[l], norm_mix_post[l])

        h = rmsnorm(x, norm_ffn_pre[l])
        f = (jax.nn.silu(h @ ffn_w_gate[l]) * (h @ ffn_w_up[l])) @ ffn_w_down[l]
        x = x + rmsnorm(f, norm_ffn_post[l])
    return x


def setup_inputs(seed=0):
    out = dict(first_inputs(seed))
    for name, value in second_inputs(seed + 1).items():
        if name != "x":
            out[name + "_2"] = value
    return out


def reference(
    x, c, rel_bias, norm_g, w_ada, b_ada, w_in, q_gain, k_gain, a_re, a_im, log_dt, b_re, b_im,
    c_re, c_im, d_skip, w_glu, b_glu, w_out, norm_mix_pre_2, norm_mix_post_2, w_in_2,
    ret_norm_w_2, ret_norm_b_2, gla_w_alpha2_2, gla_b_alpha_2, gla_norm_w_2, attn_sinks_2,
    w_branch_2, w_out_2, norm_ffn_pre_2, norm_ffn_post_2, ffn_w_gate_2, ffn_w_up_2,
    ffn_w_down_2,
):
    x = first_block(
        x, c, rel_bias, norm_g, w_ada, b_ada, w_in, q_gain, k_gain, a_re, a_im, log_dt, b_re,
        b_im, c_re, c_im, d_skip, w_glu, b_glu, w_out,
    )
    return second_block(
        x, norm_mix_pre_2, norm_mix_post_2, w_in_2, ret_norm_w_2, ret_norm_b_2, gla_w_alpha2_2,
        gla_b_alpha_2, gla_norm_w_2, attn_sinks_2, w_branch_2, w_out_2, norm_ffn_pre_2,
        norm_ffn_post_2, ffn_w_gate_2, ffn_w_up_2, ffn_w_down_2,
    )


_drawn_inputs = setup_inputs


def setup_inputs(seed=0):
    import zlib

    import numpy as np

    out = dict(_drawn_inputs(seed))
    spreads = {}
    factors = {'rel_bias': 2.826,
     'norm_g': 4.743,
     'b_ada': 7.967,
     'q_gain': 8.0,
     'k_gain': 8.0,
     'a_re': 64.0,
     'a_im': 64.0,
     'log_dt': 64.0,
     'b_re': 64.0,
     'b_im': 64.0,
     'c_re': 64.0,
     'c_im': 64.0,
     'b_glu': 64.0,
     'ret_norm_b_2': 18.232,
     'attn_sinks_2': 51.139,
     'norm_mix_post_2': 4.848,
     'ret_norm_w_2': 7.289,
     'gla_w_alpha2_2': 3.169,
     'gla_b_alpha_2': 8.0,
     'gla_norm_w_2': 6.835,
     'norm_ffn_pre_2': 3.573,
     'norm_ffn_post_2': 4.953}
    for name, (base, spread) in spreads.items():
        noise = np.random.default_rng([zlib.crc32(name.encode()), seed]).standard_normal(out[name].shape)
        drawn = base * np.exp(spread * noise) if base else spread * noise
        out[name] = __import__('jax').numpy.asarray(drawn.astype(out[name].dtype))
    for name, factor in factors.items():
        out[name] = (out[name] * factor).astype(out[name].dtype)
    return out
```

```python
from contextlib import ExitStack

import numpy as np

import concourse.bass as bass
from concourse import mybir

P = 128
SEQ = 512
D = 1024
KT = D // P
TT = SEQ // P
WC = 256
EPS_RMS = 1e-6
EPS_GN = 1e-5
GROUPS, GCH, NSTATE = 32, 16, 64
PAIRS = GROUPS // 2
STEPS = 8
CHUNKS = SEQ // STEPS
HEADS = 8
TOPK = 128
BUCKET_STARTS = [0, 1, 2, 3, 4, 5, 6, 7, 8, 9, 10, 11, 12, 13, 14, 15, 16, 19, 21, 24, 27, 31, 35,
                 40, 46, 52, 59, 67, 77, 87, 99, 113]
BIAS_LEN = 640
D_FF = 2816
FT = D_FF // P
NEG_MASKED, NEG_TAKEN, NEG_BETWEEN, NEG_LOGIT = -2e38, -3e38, -2.5e38, -1e30
GLA_CHUNK = 64

VEC_SIZES = [("c", 8), ("norm_g", 8), ("b_ada", 24), ("q_gain", 1), ("k_gain", 1), ("b_glu", 4),
             ("norm_mix_pre", 8), ("norm_mix_post", 8), ("ret_w", 8), ("ret_b", 8), ("gla_b", 4),
             ("gla_w", 8), ("norm_ffn_pre", 8), ("norm_ffn_post", 8), ("sinks", 16)]
VEC = {}
_at = 0
for _name, _n in VEC_SIZES:
    VEC[_name] = (_at, _at + _n)
    _at += _n
VECS = _at

def _cols(name, c0, n, kt=KT, row0=0):
    return [(name, row0, kt, [(c0 + i * WC, WC)]) for i in range(n // WC)]

KV2 = 7184
STAGES = [
    ("ada_shift_scale", _cols("w_ada", 0, 2048)),
    ("ssm_u", _cols("w_in", 0, 512)),
    ("ssm_z", _cols("w_in", 512, 512)),
    ("glu", _cols("w_glu", 0, 512, kt=4)),
    ("q_idx", _cols("w_in", 3072, 512)),
    ("k_idx", [("w_in", 0, KT, [(3584, 64), (3584, 64), (3648, 8)])]),
    ("q", _cols("w_in", 1024, 512)),
    ("k", _cols("w_in", 1536, 512)),
    ("v", _cols("w_in", 2048, 512)),
    ("attn_z", _cols("w_in", 2560, 512)),
    ("ada_gate", _cols("w_ada", 2048, 1024)),
    ("out1", _cols("w_out", 0, 1024)),
    ("ret_q", _cols("w_in2", 0, 512)),
    ("ret_k", _cols("w_in2", 512, 512)),
    ("ret_v", _cols("w_in2", 1024, 1024)),
    ("ret_g", _cols("w_in2", 2048, 1024)),
    ("merge0", [t for p in range(4) for t in _cols("w_in2", 7696 + p * WC, WC)
                + _cols("w_branch0", p * WC, WC)]),
    ("gla_q", _cols("w_in2", 3072, 512)),
    ("gla_k", _cols("w_in2", 3584, 512)),
    ("gla_v", _cols("w_in2", 4096, 1024)),
    ("gla_a", [("w_in2", 0, KT, [(6144, 16)])]),
    ("gla_g", _cols("w_in2", 5120, 1024)),
    ("merge1", [t for p in range(4) for t in _cols("w_in2", 8720 + p * WC, WC)
                + _cols("w_branch1", p * WC, WC)]),
    ("swa_k", _cols("w_in2", KV2, 256)),
    ("swa_v", _cols("w_in2", KV2 + 256, 256)),
    ("swa_q", _cols("w_in2", 6160, 1024)),
    ("merge2", [t for p in range(4) for t in _cols("w_in2", 9744 + p * WC, WC)
                + _cols("w_branch2", p * WC, WC)]),
    ("out2", _cols("w_out2", 0, 1024)),
    ("ffn_up", [t for p in range(D_FF // WC) for t in _cols("w_gate", p * WC, WC)
                + _cols("w_up", p * WC, WC)]),
    ("ffn_down", [("w_down", k * D, min(KT, FT - k * KT), [(c * WC, WC)])
                  for c in range(4) for k in range(3)]),
]
RAW_STAGES = ("ada_shift_scale", "ada_gate")
TILES = [t for _, ts in STAGES for t in ts]
TILES_PER_GROUP = {"ffn_down": 3}
RAW_SLOTS = 2

ACT_TILES = [("norm0", 8), ("z", 4), ("y_ssm", 4), ("y_attn", 4), ("norm1", 8), ("y0", 8),
             ("y1", 8), ("y2", 8), ("merged", 8), ("norm2", 8), ("f", FT)]
AT = {}
_at = 0
for _name, _n in ACT_TILES:
    AT[_name] = _at
    _at += _n


class Group:

    def __init__(self, index, kts, split0):
        self.g = index
        self.kts = kts
        self.s = split0


def plan():
    groups, tiles = {}, []
    g = s = raw = 0
    for name, ts in STAGES:
        groups[name] = []
        if name in RAW_STAGES:
            for t in ts:
                tiles.append(("raw", raw, t))
                groups[name].append((len(tiles) - 1, raw))
                raw += 1
            continue
        per = TILES_PER_GROUP.get(name, 1)
        for i in range(0, len(ts), per):
            groups[name].append(Group(g, [t[2] for t in ts[i:i + per]], s))
            for t in ts[i:i + per]:
                tiles.append(("split", s, t))
                s += 1
            g += 1
    return groups, tiles


def hybrid_blocks(nc, wstream, xT, vecs, consts, onehot, rel_bias, ssm_vec, ssm_b, ssm_c, d_skip,
                  alpha2, decay, reset, outT):
    f32, f32r, i32 = mybir.dt.float32, mybir.dt.float32r, mybir.dt.int32
    ALU, ACT, AX = mybir.AluOpType, mybir.ActivationFunctionType, mybir.AxisListType
    G, STREAM = plan()
    SPLIT_TILES = sum(kind == "split" for kind, _, _ in STREAM)
    SPLIT_AT = [i for i, (kind, _, _) in enumerate(STREAM) if kind == "split"]

    bias_dram = nc.dram_tensor("bias_table", (HEADS, BIAS_LEN), f32, kind="Internal")
    bias_rows = nc.dram_tensor("bias_rows", (P, HEADS * BIAS_LEN), f32, kind="Internal")
    x1_dram = nc.dram_tensor("x1_saved", (P, KT * SEQ), f32, kind="Internal").ap()

    ctx = ExitStack()
    with ctx:
        def sb(name, shape, dt=f32):
            return ctx.enter_context(nc.sbuf_tensor(name, shape, dt))

        def views(hold, *sets):
            made = []
            for tensors in sets:
                with ExitStack() as phase:
                    made.append([phase.enter_context(nc.sbuf_tensor(n, s, dt)) for n, s, dt in tensors])
            for n, s, dt in hold:
                ctx.enter_context(nc.sbuf_tensor(n, s, dt))
            return made

        def sem(name):
            return ctx.enter_context(nc.semaphore(name))

        vec = sb("vec", [P, VECS])
        cst = sb("cst", [P, 768])
        ident = cst[:, 0:128]
        causal = cst[:, 128:256]
        gla_mask = cst[:, 256:384]
        swa_dist = cst[:, 384:640]
        head_ones = cst[:, 640:768]
        ones = sb("ones", [P, P])
        eps = sb("eps", [P, 2])
        modv = sb("modv", [P, 24])
        gs = sb("gs", [P, 8])
        silu_c = sb("silu_c", [P, 8])
        qg = sb("qg", [P, 1])
        rho = sb("rho", [P, PAIRS])
        small = sb("small", [P, 64])

        w_raw = sb("w_raw", [P, RAW_SLOTS, KT, WC])
        w_hi = sb("w_hi", [P, 2, KT, WC], f32r)
        w_lo = sb("w_lo", [P, 2, KT, WC], f32r)
        tval = sb("tval", [P, 2, SEQ])
        sqb = sb("sqb", [P, 2, SEQ])
        sgb = sb("sgb", [P, 2, SEQ])
        root = sb("root", [P, SEQ])
        rstd = sb("rstd", [P, SEQ])

        ((h_hi, h_lo), (win_re, win_im, sv, b_re, b_im, c_re, c_im, bb_re, bb_im, pw_re, pw_im,
                        tmp, btab), (down,)) = views(
            [("room_h", [P, 2 * KT * SEQ], f32)],
            [("h_hi", [P, KT, SEQ], f32r), ("h_lo", [P, KT, SEQ], f32r)],
            [("win_re", [P, PAIRS, P], f32), ("win_im", [P, PAIRS, P], f32),
             ("sv", [P, 24, PAIRS], f32)] +
            [(n, [P, PAIRS, GCH], f32) for n in ("b_re", "b_im", "c_re", "c_im", "bb_re", "bb_im")] +
            [(n, [P, STEPS + 1, PAIRS], f32) for n in ("pw_re", "pw_im")] +
            [("tmp", [P, 1152], f32), ("btab", [HEADS, BIAS_LEN], f32)],
            [("down", [P, KT, SEQ], f32)])
        ((xr,), (xa, xb, ga_, gb_), (bias,), (merged,)) = views(
            [("room_x", [P, KT * SEQ], f32)],
            [("xr", [P, KT, SEQ], f32)],
            [(n, [P, PAIRS, CHUNKS], f32) for n in ("xa", "xb", "ga_", "gb_")],
            [("bias", [P, HEADS, SEQ], f32)],
            [("merged", [P, KT, SEQ], f32)])
        A = [
            [("y_hi", [P, KT, SEQ], f32r), ("y_lo", [P, KT, SEQ], f32r)],
            [("toep", [P, GROUPS, P], f32), ("wint_re", [P, PAIRS, P], f32),
             ("wint_im", [P, PAIRS, P], f32)],
            [("pad_on", [P, KT, SEQ], f32), ("on", [P, KT, SEQ], f32)],
            [("f_hi", [P, FT, SEQ], f32r), ("f_lo", [P, FT, SEQ], f32r)],
        ]
        pad = ("pad", [P, 2 * KT * SEQ], f32)

        def arena(*t):
            A.append([(pad[0] + str(len(A)), pad[1], pad[2])] + list(t))

        arena(("sz", [P, 4, SEQ], f32), ("ut", [P, GROUPS, CHUNKS], f32),
              ("cl_re", [P, PAIRS, 2, (STEPS + 1) * GCH], f32),
              ("cl_im", [P, PAIRS, 2, (STEPS + 1) * GCH], f32), ("sin_t", [P, PAIRS, CHUNKS], f32))
        arena(("strip", [GCH, GROUPS, P], f32))
        arena(("q32", [P, 4, SEQ], f32), ("k32", [P, 4, SEQ], f32), ("v32", [P, TT, SEQ], f32),
              ("qi", [P, 4, SEQ], f32), ("score", [P, TT, SEQ], f32), ("az", [P, 4, SEQ], f32),
              ("ki", [P, SEQ], f32), ("pT", [P, 2, TT, P], f32), ("wi", [P, TT, HEADS], f32),
              ("stat", [P, 4, 32], f32))
        arena(("rq", [P, 4, SEQ], f32), ("rk", [P, 4, SEQ], f32), ("rv", [P, TT, D], f32),
              ("ra", [P, 2, SEQ], f32), ("dec", [P, 4, SEQ], f32), ("o32", [P, 2, SEQ], f32),
              ("oc", [P, 2, SEQ], f32))
        arena(("gq", [P, 4, SEQ], f32), ("gk", [P, 4, SEQ], f32), ("gv", [P, TT, D], f32),
              ("la", [P, SEQ], f32), ("lb", [P, SEQ], f32), ("eb", [P, SEQ], f32),
              ("kd", [P, SEQ], f32), ("kdT", [P, TT, P], f32), ("am", [P, TT, P], f32),
              ("st", [P, 7, 256], f32), ("ga", [GCH, SEQ], f32), ("al2", [GCH, SEQ], f32),
              ("rst", [P, SEQ], f32))
        arena(("sq", [P, KT, SEQ], f32), ("sk", [P, 4, SEQ], f32), ("svd", [P, TT, 4, P], f32),
              ("lg", [P, 2, 4, 256], f32), ("spT", [P, 2, SEQ], f32), ("yb", [P, 2, SEQ], f32),
              ("sst", [P, 8, 64], f32))
        arena(("mo", [P, KT, SEQ], f32),)
        arena(("u4", [P, GROUPS, STEPS // 2, GCH], f32))
        A.append([("pad_u", [P, GROUPS, P], f32), ("u", [64, STEPS, GROUPS * GCH], f32)])
        arena(("pad_sz", [P, 4, SEQ], f32), ("z32", [P, 4, SEQ], f32))
        made = views([("room_f", [P, 23040], f32)], *A)
        (y_hi, y_lo), (toep, wint_re, wint_im), (_, on), (f_hi, f_lo) = made[0:4]
        _, sz, ut, cl_re, cl_im, sin_t = made[4]
        _, strip = made[5]
        z32 = made[13][2]
        u = made[12][1]
        cos_t = sgb[:, :, :].rearrange("p a (j k) -> p (a j) k", k=CHUNKS)
        u4 = made[11][1]
        _, q32, k32, v32, qi, score, az, ki, pT, wi, stat = made[6]
        _, rq, rk, rv, ra, dec, o32, oc = made[7]
        _, gq, gk, gv, la, lb, eb, kd, kdT, am, st, ga, al2, rst = made[8]
        _, sq, sk, svd, lg, spT, yb, sst = made[9]
        _, mo = made[10]
        flat = tval[:, :, :].rearrange("p a n -> p (a n)")
        oh, rb, dsk = flat[0:32, 0:BIAS_LEN], flat[0:32, 640:640 + HEADS], small[0:GCH, 32:32 + GROUPS]

        bank = [ctx.enter_context(nc.psum_tensor(f"bank{i}", [P, SEQ], f32)) for i in range(8)]

        raw_loaded = [sem(f"raw_loaded{i}") for i in range(RAW_SLOTS)]
        raw_used = sem("raw_used")
        w_high = sem("w_high")
        w_low = sem("w_low")
        w_used = sem("w_used")
        group_done = sem("group_done")
        bank_free = [sem(f"bank_free{i}") for i in range(4)]
        act_val, act_high, act_low = sem("act_val"), sem("act_high"), sem("act_low")
        sq_ready, sq_used = sem("sq_ready"), sem("sq_used")
        root_ready, rstd_ready = sem("root_ready"), sem("rstd_ready")
        dve_step, act_step, pool_step = sem("dve_step"), sem("act_step"), sem("pool_step")
        in_small, in_x, in_ssm, consts_set = sem("in_small"), sem("in_x"), sem("in_ssm"), sem("consts_set")
        cl_zero, bias_spread = sem("cl_zero"), sem("bias_spread")
        c_ready, ada_done, mod_ready = sem("c_ready"), sem("ada_done"), sem("mod_ready")
        setup_trig, trig_ready = sem("setup_trig"), sem("trig_ready")
        win_ready, wint_psum, wint_act, wint_dve = sem("win_ready"), sem("wint_psum"), sem("wint_act"), sem("wint_dve")
        cl_ready, strip_psum, strip_act, strip_dve = sem("cl_ready"), sem("strip_psum"), sem("strip_act"), sem("strip_dve")
        strip_ready, toep_zero, toep_loaded = sem("strip_ready"), sem("toep_zero"), sem("toep_loaded")
        bias_psum, bias_copied, bias_stored, bias_loaded = sem("bias_psum"), sem("bias_copied"), sem("bias_stored"), sem("bias_loaded")
        u_act, u_dve, ut_psum, ut_act, ut_dve = sem("u_act"), sem("u_dve"), sem("ut_psum"), sem("ut_act"), sem("ut_dve")
        x_psum, state_ready, y_psum, y_act, y_dve = sem("x_psum"), sem("state_ready"), sem("y_psum"), sem("y_act"), sem("y_dve")
        zt_psum, z_ready, sig_ready, sig_used = sem("zt_psum"), sem("z_ready"), sem("sig_ready"), sem("sig_used")
        copied_act, copied_dve = sem("copied_act"), sem("copied_dve")
        rel_psum, relu_ready, rel_used = sem("rel_psum"), sem("relu_ready"), sem("rel_used")
        lg_psum, lg_ready, p_exp, p_norm = sem("lg_psum"), sem("lg_ready"), sem("p_exp"), sem("p_norm")
        lg_read, pt_psum, pt_ready, pv_psum, pv_read = sem("lg_read"), sem("pt_psum"), sem("pt_ready"), sem("pv_psum"), sem("pv_read")
        x_reload, x1_done, x1_stored, x1_back = sem("x_reload"), sem("x1_done"), sem("x1_stored"), sem("x1_back")
        sc_psum, a_ready, o_psum, o_copied = sem("sc_psum"), sem("a_ready"), sem("o_psum"), sem("o_copied")
        mean_psum, oc_ready, on_ready, dec_loaded = sem("mean_psum"), sem("oc_ready"), sem("on_ready"), sem("dec_loaded")
        gz_psum, gz_ready, gsp_ready, gb_ready, gexp_ready = sem("gz_psum"), sem("gz_ready"), sem("gsp_ready"), sem("gb_ready"), sem("gexp_ready")
        gkd_ready, gkdT_psum, gkdT_ready, gla_loaded = sem("gkd_ready"), sem("gkdT_psum"), sem("gkdT_ready"), sem("gla_loaded")
        kv_psum, kv_read = sem("kv_psum"), sem("kv_read")
        merged_ready, mo_ready, x2_ready, dn_ready = sem("merged_ready"), sem("mo_ready"), sem("x2_ready"), sem("dn_ready")
        y_tile, out_ready, out_stored = sem("y_tile"), sem("out_ready"), sem("out_stored")
        block = ctx.enter_context(nc.Block())

        STATS = ["norm0"] + [f"qk{i}" for i in range(8)] + ["norm1"] + \
            [f"ret{h}" for h in range(4)] + [f"gla{h}" for h in range(4)] + ["post1", "norm2", "post2"]
        sizes = {"norm0": 8, "norm1": 8, "norm2": 8, "post1": 8, "post2": 8}
        sizes.update({f"qk{i}": 1 for i in range(8)})
        sizes.update({f"{b}{h}": 2 for b in ("ret", "gla") for h in range(4)})
        SQ0, ROOT = {}, {}
        for i, name in enumerate(STATS):
            SQ0[name] = sum(sizes[n] for n in STATS[:i])
            ROOT[name] = i

        def v(name, m):
            a, _ = VEC[name]
            return vec[:, a + m:a + m + 1]

        def done(name, i, b=2):
            return 2 * G[name][i].g + b

        def pbanks(gr):
            return 2 * (gr.g % 2), 2 * (gr.g % 2) + 1

        def all_groups():
            for name, _ in STAGES:
                if name not in RAW_STAGES:
                    for gr in G[name]:
                        yield gr

        def tile_used(s):
            inner = 0
            for gr in all_groups():
                n = len(gr.kts)
                if gr.s + n - 1 == s:
                    return group_done, 2 * gr.g + 2
                if gr.s <= s:
                    if s < gr.s + n - 1:
                        return w_used, inner + s - gr.s + 1
                inner += n - 1

        SIG, n_sig = {}, 0
        for name, n in (("glu", 4), ("ret_g", 8), ("merge0", 8), ("gla_g", 8), ("merge1", 8),
                        ("merge2", 8), ("ffn_up", FT)):
            SIG[name] = n_sig
            n_sig += n
        PT_END = [32 + sum(1 if m % TT == 0 else 2 for m in range(n + 1)) for n in range(16)]

        @block.sync
        def _(sp):
            for t, src in ((vec[:, :], vecs), (cst[:, :], consts), (oh[:, :], onehot),
                           (rb[:, :], rel_bias), (dsk[:, :], d_skip)):
                sp.dma_start(t, src).then_inc(in_small, 16)
            for t, src in ((sv[:, 0:3, :], ssm_vec), (b_re[:, :, :], ssm_b[0]), (b_im[:, :, :], ssm_b[1]),
                           (c_re[:, :, :], ssm_c[0]), (c_im[:, :, :], ssm_c[1])):
                sp.dma_start(t, src).then_inc(in_ssm, 16)
            sp.dma_start(xr[:, :, :], xT).then_inc(in_x, 16)

            def aside(i):
                kind, n, _ = STREAM[i]
                if i == 10:
                    sp.wait_ge(strip_ready, 1)
                    sp.wait_ge(toep_zero, 1)
                    for s in range(STEPS):
                        r = (STEPS - 1 - s) * GCH
                        sp.dma_start(toep[r:r + GCH, :, s * GCH:P],
                                     strip[:, :, 0:P - s * GCH]).then_inc(toep_loaded, 16)

            for i, (kind, n, (_, _, kt, _)) in enumerate(STREAM):
                aside(i)
                if kind == "split" and n == G["out1"][1].s:
                    sp.wait_ge(lg_ready, 32)
                    sp.dma_start(xr[:, :, :], xT).then_inc(x_reload, 16)
                if i >= RAW_SLOTS:
                    was, k, _ = STREAM[i - RAW_SLOTS]
                    if was == "split":
                        sp.wait_ge(w_low, k + 1)
                    else:
                        sp.wait_ge(raw_used, k + 1)
                sp.dma_start(w_raw[:, i % RAW_SLOTS, 0:kt, :],
                             wstream[i][:, 0:kt * WC].rearrange("p (t c) -> p t c", c=WC)
                             ).then_inc(raw_loaded[i % RAW_SLOTS], 16)
            sp.wait_ge(toep_loaded, 16 * STEPS)
            sp.wait_ge(x1_stored, 16)
            for m in range(KT):
                sp.wait_ge(out_ready, m + 1)
                sp.dma_start(outT[:, m, :], down[:, m, :]).then_inc(out_stored, 16)
            sp.wait_ge(out_stored, 16 * KT)

        @block.gpsimd
        def _(pool):
            pool.memset(ones[:, :], 1.0).then_inc(consts_set, 1)
            pool.memset(eps[:, 0:1], EPS_RMS).then_inc(consts_set, 1)
            pool.memset(eps[:, 1:2], EPS_GN).then_inc(consts_set, 1)
            pool.memset(cl_re[:, :, :, :], 0.0).then_inc(cl_zero, 1)
            pool.memset(cl_im[:, :, :, :], 0.0).then_inc(cl_zero, 1)
            pool.memset(toep[:, :, :], 0.0).then_inc(toep_zero, 1)
            pool.wait_ge(bias_copied, 1)
            pool.dma_start(bias_dram.ap(), btab[:, :]).then_inc(bias_stored, 16)
            pool.wait_ge(bias_stored, 16)
            pool.dma_start(bias_rows.ap(), bass.AP(bias_dram, 0, [[0, P], [1, HEADS * BIAS_LEN]])
                           ).then_inc(bias_spread, 16)
            pool.wait_ge(bias_spread, 16)
            pool.wait_ge(y_psum, 8)
            pool.dma_start(bias[:, :, :], bass.AP(
                bias_rows, P - 1, [[HEADS * BIAS_LEN - 1, P], [BIAS_LEN, HEADS], [1, SEQ]])
                           ).then_inc(bias_loaded, 16)
            for h in range(4):
                if h == 0:
                    pool.wait_ge(pv_read, 4)
                    pool.wait_ge(act_low, AT["y_attn"] + 4)
                    pool.dma_start(dec[:, :, :], decay).then_inc(dec_loaded, 16)
            pool.wait_ge(x1_done, KT)
            pool.dma_start(x1_dram, xr[:, :, :].rearrange("p t n -> p (t n)")).then_inc(x1_stored, 16)
            pool.wait_ge(on_ready, 8)
            pool.wait_ge(o_psum, 8)
            pool.dma_start(rst[:, :], reset).then_inc(gla_loaded, 16)
            pool.dma_start(al2[:, :], alpha2).then_inc(gla_loaded, 16)
            pool.wait_ge(x1_stored, 16)
            pool.wait_ge(act_low, AT["merged"] + 8)
            pool.dma_start(xr[:, :, :].rearrange("p t n -> p (t n)"), x1_dram).then_inc(x1_back, 16)
            pool.wait_ge(x1_back, 16)

        @block.tensor
        def _(pe):
            def mm(out, lhsT, rhs, start, stop):
                return pe.matmul(out, lhsT, rhs, start=start, stop=stop)

            def gemm(gr, kind, hi, lo, k0=0, cols=WC, permuted=False):
                b = pbanks(gr)
                if gr.g >= 2:
                    for x in b:
                        pe.wait_ge(bank_free[x], gr.g // 2)
                n_tiles = len(gr.kts)
                k_all = sum(gr.kts)
                k_at = 0
                for j, kt in enumerate(gr.kts):
                    s = gr.s + j
                    pe.wait_ge(w_low, s + 1)
                    wh, wl = w_hi[:, s % 2], w_lo[:, s % 2]
                    for half in range(2):
                        if kind == "fm":
                            c = slice(half * P, half * P + P)
                            out = bank[b[half]][:, :]
                            for k in range(kt):
                                a = k0 + k_at + k
                                first, last = k_at + k == 0, k_at + k == k_all - 1
                                mm(out, wh[:, k, c], hi[:, a, :], first, False)
                                mm(out, wh[:, k, c], lo[:, a, :], False, False)
                                ins = mm(out, wl[:, k, c], hi[:, a, :], False, last)
                        else:
                            for t in (2 * half, 2 * half + 1):
                                out = bank[b[half]][:, (t % 2) * WC:(t % 2) * WC + cols]
                                for k in range(kt):
                                    a = k0 + k
                                    if permuted:
                                        ah, al = (x[:, a, t:SEQ:4] for x in (hi, lo))
                                    else:
                                        ah, al = (x[:, a, t * P:t * P + P] for x in (hi, lo))
                                    mm(out, ah, wh[:, k, 0:cols], k == 0, False)
                                    mm(out, ah, wl[:, k, 0:cols], False, False)
                                    ins = mm(out, al, wh[:, k, 0:cols], False, k == kt - 1)
                        if j == n_tiles - 1:
                            ins.then_inc(group_done, 1)
                        elif half == 1:
                            ins.then_inc(w_used, 1)
                    k_at += kt

            def ada(name, m0):
                for i, (tile, raw) in enumerate(G[name]):
                    pe.wait_ge(raw_loaded[tile % RAW_SLOTS], 16 * (tile // RAW_SLOTS + 1))
                    for half in range(2):
                        m = m0 + 2 * i + half
                        for k in range(KT):
                            ins = mm(bank[7][:, m:m + 1],
                                     w_raw[:, tile % RAW_SLOTS, k, half * P:half * P + P],
                                     silu_c[:, k:k + 1], k == 0, k == KT - 1)
                    ins.then_inc(raw_used, 1)
                pe.wait_ge(raw_used, G[name][-1][1] + 1)
                pe.nop().then_inc(ada_done, 1)

            def stats(name, lhsT):
                n, s0, r = sizes[name], SQ0[name], ROOT[name]
                if r:
                    pe.wait_ge(root_ready, r)
                for m in range(n):
                    pe.wait_ge(sq_ready, s0 + m + 1)
                    mm(bank[4][:, :], lhsT, sqb[:, (s0 + m) % 2, :], m == 0, m == n - 1).then_inc(sq_used, 1)

            pe.wait_ge(in_small, 80)
            pe.wait_ge(consts_set, 3)
            mm(bank[4][0:HEADS, 0:320], rb[:, :], oh[:, 0:320], True, True)
            mm(bank[5][0:HEADS, 0:320], rb[:, :], oh[:, 320:640], True, True).then_inc(bias_psum, 1)
            pe.wait_ge(c_ready, 1)
            ada("ada_shift_scale", 0)
            pe.wait_ge(win_ready, 1)
            pe.wait_ge(bias_copied, 1)
            for b in range(8):
                src = (win_re, win_im)[b // 4]
                if b >= 2:
                    pe.wait_ge(wint_act if b % 2 == 0 else wint_dve, b // 2)
                for i in range(4):
                    ins = pe.transpose(bank[4 + b % 2][:, i * P:i * P + P],
                                       src[:, 4 * (b % 4) + i, :], ident)
                ins.then_inc(wint_psum, 1)
            pe.wait_ge(cl_ready, 1)
            pe.wait_ge(wint_act, 4)
            pe.wait_ge(wint_dve, 4)
            for b in range(8):
                if b >= 2:
                    pe.wait_ge(strip_act if b % 2 == 0 else strip_dve, b // 2)
                for i in range(2):
                    j = 2 * b + i
                    out = bank[4 + b % 2][0:GCH, i * 2 * P:(i + 1) * 2 * P]
                    mm(out, bb_re[:, j, :], cl_re[:, j, :, 0:P], True, False)
                    ins = mm(out, bb_im[:, j, :], cl_im[:, j, :, 0:P], False, True)
                ins.then_inc(strip_psum, 1)
            pe.wait_ge(strip_act, 4)
            pe.wait_ge(strip_dve, 4)

            stats("norm0", ones[:, :])
            pe.wait_ge(act_low, AT["norm0"] + 8)
            for gr in G["ssm_u"]:
                gemm(gr, "tm", h_hi, h_lo, permuted=True)
            pe.wait_ge(u_act, 4)
            pe.wait_ge(u_dve, 4)
            pe.wait_ge(root_ready, 1)
            pe.wait_ge(mod_ready, 1)
            for b in range(8):
                if b >= 4:
                    pe.wait_ge(ut_act if b % 2 == 0 else ut_dve, (b - 4) // 2 + 1)
                for i in range(4):
                    ins = pe.transpose(bank[4 + b % 4][0:64, i * P:i * P + P], u4[:, 4 * b + i, :, :], ident)
                ins.then_inc(ut_psum, 1)
            pe.wait_ge(ut_act, 4)
            pe.wait_ge(ut_dve, 4)
            for half in range(2):
                for w, bk in ((wint_re, 4 + half), (wint_im, 6 + half)):
                    for j in range(8 * half, 8 * half + 8):
                        for gp in range(2):
                            ins = mm(bank[bk][gp * 64:gp * 64 + 64, (j % 8) * CHUNKS:(j % 8 + 1) * CHUNKS],
                                     w[:, j, gp * 64:gp * 64 + 64], ut[:, 2 * j + gp, :], True, True)
                    ins.then_inc(x_psum, 1)
            for gr in G["ssm_z"]:
                gemm(gr, "fm", h_hi, h_lo)
            pe.wait_ge(state_ready, 1)
            pe.wait_ge(toep_loaded, 16 * STEPS)
            for b in range(8):
                if b >= 4:
                    pe.wait_ge(y_act if b % 2 == 0 else y_dve, (b - 4) // 2 + 1)
                for i in range(2):
                    j = 2 * b + i
                    c = i * 2 * P
                    out = bank[4 + b % 4][0:64, c:c + 2 * P]
                    mm(out, ga_[:, j, :], cl_re[:, j, :, GCH:GCH + P], True, False)
                    mm(out, gb_[:, j, :], cl_im[:, j, :, GCH:GCH + P], False, False)
                    mm(out[:, 0:P], ut[:, 2 * j, :], toep[:, 2 * j, :], False, False)
                    ins = mm(out[:, P:2 * P], ut[:, 2 * j + 1, :], toep[:, 2 * j + 1, :], False, True)
                ins.then_inc(y_psum, 1)
            pe.wait_ge(y_act, 4)
            pe.wait_ge(y_dve, 4)
            for ct in range(4):
                for t in range(STEPS):
                    ins = pe.transpose(bank[4 + ct][:, t * CHUNKS:(t + 1) * CHUNKS],
                                       u[:, t, ct * P:ct * P + P], ident[0:64, 0:64])
                ins.then_inc(zt_psum, 1)
            pe.wait_ge(act_low, AT["z"] + 4)
            for gr in G["glu"]:
                gemm(gr, "fm", y_hi, y_lo, k0=4)
            for gr in G["q_idx"]:
                gemm(gr, "fm", h_hi, h_lo)
            gr = G["k_idx"][0]
            b = pbanks(gr)
            for x in b:
                pe.wait_ge(bank_free[x], gr.g // 2)
            pe.wait_ge(w_low, gr.s + 1)
            wh, wl = w_hi[:, gr.s % 2], w_lo[:, gr.s % 2]
            for k in range(KT):
                mm(bank[b[0]][:, :], wh[:, k, 0:P], h_hi[:, k, :], k == 0, False)
                mm(bank[b[0]][:, :], wh[:, k, 0:P], h_lo[:, k, :], False, False)
                ins = mm(bank[b[0]][:, :], wl[:, k, 0:P], h_hi[:, k, :], False, k == KT - 1)
            ins.then_inc(group_done, 1)
            for t in range(TT):
                out = bank[b[1]][:, t * HEADS:(t + 1) * HEADS]
                for k in range(KT):
                    ah, al = h_hi[:, k, t * P:t * P + P], h_lo[:, k, t * P:t * P + P]
                    mm(out, ah, wh[:, k, P:P + HEADS], k == 0, False)
                    mm(out, ah, wl[:, k, P:P + HEADS], False, False)
                    ins = mm(out, al, wh[:, k, P:P + HEADS], False, k == KT - 1)
            ins.then_inc(group_done, 1)
            pe.wait_ge(copied_act, 1)
            pe.wait_ge(copied_dve, 1)
            for i in range(32):
                qt, h = i // 8, i % 8
                hp = slice((h % 2) * 64, (h % 2) * 64 + 64)
                if i >= 3:
                    pe.wait_ge(relu_ready, i - 2)
                mm(bank[5 + i % 3][:, 0:P * (qt + 1)], qi[hp, h // 2, qt * P:qt * P + P],
                   ki[hp, 0:P * (qt + 1)], True, True).then_inc(rel_psum, 1)
            for i in range(8):
                if i % 2 == 0:
                    gemm(G["q" if i < 4 else "k"][(i % 4) // 2], "fm", h_hi, h_lo)
                stats(f"qk{i}", head_ones)
            for gr in G["v"]:
                gemm(gr, "tm", h_hi, h_lo)
            for gr in G["attn_z"]:
                gemm(gr, "fm", h_hi, h_lo)
            pe.wait_ge(relu_ready, 32)
            ada("ada_gate", 16)
            pe.wait_ge(mod_ready, 2)
            pe.wait_ge(copied_act, 3)
            pe.wait_ge(copied_dve, 3)
            pe.wait_ge(root_ready, ROOT["qk7"] + 1)

            def logits(i):
                h, qt = i // TT, i % TT
                hp = slice((h % 2) * 64, (h % 2) * 64 + 64)
                if i >= 2:
                    pe.wait_ge(lg_read, i - 1)
                mm(bank[4 + i % 2][:, 0:P * (qt + 1)], q32[hp, h // 2, qt * P:qt * P + P],
                   k32[hp, h // 2, 0:P * (qt + 1)], True, True).then_inc(lg_psum, 1)

            logits(0)
            for i in range(32):
                h, qt = i // TT, i % TT
                if i + 1 < 32:
                    logits(i + 1)
                pe.wait_ge(p_norm, i + 1)
                if i >= 1:
                    pe.wait_ge(pt_ready, i)
                for s in range(qt + 1):
                    ins = pe.transpose(bank[6][:, s * P:s * P + P], sgb[:, i % 2, s * P:s * P + P], ident)
                ins.then_inc(pt_psum, 1)
                pe.wait_ge(pt_ready, i + 1)
                if h % 2 == 0 and qt == 0 and h:
                    pe.wait_ge(pv_read, h // 2)
                out = bank[7][(h % 2) * 64:(h % 2) * 64 + 64, qt * P:qt * P + P]
                for s in range(qt + 1):
                    ins = mm(out, v32[:, s, h * 64:h * 64 + 64], pT[:, i % 2, s, :], s == 0, s == qt)
                ins.then_inc(pv_psum, 1)
            pe.wait_ge(act_low, AT["y_attn"] + 4)
            for gr in G["out1"]:
                gemm(gr, "fm", y_hi, y_lo)
            stats("norm1", ones[:, :])
            pe.wait_ge(act_low, AT["norm1"] + 8)

            for name in ("ret_q", "ret_k"):
                for gr in G[name]:
                    gemm(gr, "fm", h_hi, h_lo)
            for gr in G["ret_v"]:
                gemm(gr, "tm", h_hi, h_lo)
            pe.wait_ge(copied_act, 5)
            pe.wait_ge(copied_dve, 5)
            for h in range(4):
                for jb in range(TT):
                    i = 4 * h + jb
                    if i >= 1:
                        pe.wait_ge(a_ready, i)
                    mm(bank[5][:, P * jb:SEQ], rk[:, h, P * jb:P * jb + P], rq[:, h, P * jb:SEQ],
                       True, True).then_inc(sc_psum, 1)
                    pe.wait_ge(a_ready, i + 1)
                    if jb == 0 and h:
                        pe.wait_ge(o_copied, 2 * h)
                    for e in range(2):
                        c = h * 256 + e * P
                        ins = mm(bank[6 + e][:, P * jb:SEQ], rv[:, jb, c:c + P],
                                 ra[:, i % 2, 0:SEQ - P * jb], jb == 0, jb == TT - 1)
                        if jb == TT - 1:
                            ins.then_inc(o_psum, 1)
                pe.wait_ge(o_copied, 2 * h + 2)
                pe.wait_ge(root_ready, ROOT[f"ret{h}"])
                mm(bank[4][:, :], ones[:, :], o32[:, 0, :], True, False)
                mm(bank[4][:, :], ones[:, :], o32[:, 1, :], False, True).then_inc(mean_psum, 1)
                pe.wait_ge(oc_ready, 2 * h + 2)
                stats(f"ret{h}", ones[:, :])
            for gr in G["ret_g"]:
                gemm(gr, "fm", h_hi, h_lo)

            def merge(n):
                pe.wait_ge(act_low, AT[f"y{n}"] + 8)
                for i, gr in enumerate(G[f"merge{n}"]):
                    if i % 2 == 0:
                        gemm(gr, "fm", h_hi, h_lo)
                    else:
                        gemm(gr, "fm", y_hi, y_lo)

            merge(0)
            for name in ("gla_q", "gla_k"):
                for gr in G[name]:
                    gemm(gr, "fm", h_hi, h_lo)
            for gr in G["gla_v"]:
                gemm(gr, "tm", h_hi, h_lo)
            gemm(G["gla_a"][0], "fm", h_hi, h_lo)
            pe.wait_ge(copied_act, 7)
            pe.wait_ge(copied_dve, 7)
            pe.wait_ge(gla_loaded, 32)
            kv = 0
            for h in range(4):
                pe.wait_ge(root_ready, ROOT[f"gla{h}"])
                mm(bank[4][:, :], al2[:, h * P:h * P + P], ga[:, :], True, True).then_inc(gz_psum, 1)
                pe.wait_ge(gkd_ready, h + 1)
                for t in range(TT):
                    ins = pe.transpose(bank[5][:, t * P:t * P + P], kd[:, t * P:t * P + P], ident)
                ins.then_inc(gkdT_psum, 1)
                for t in range(TT):
                    ins = mm(bank[4][:, t * P:t * P + P], gk[:, h, t * P:t * P + P],
                             gq[:, h, t * P:t * P + P], True, True)
                ins.then_inc(sc_psum, 1)
                pe.wait_ge(gkdT_ready, h + 1)
                pe.wait_ge(a_ready, 16 + h + 1)
                for n in range(7):
                    if kv >= 2:
                        pe.wait_ge(kv_read, kv - 1)
                    pr = slice((n % 2) * 64, (n % 2) * 64 + 64)
                    mm(bank[4 + kv % 2][:, 0:256], kdT[pr, n // 2, :],
                       gv[pr, n // 2, h * 256:h * 256 + 256], True, True).then_inc(kv_psum, 1)
                    kv += 1
                pe.wait_ge(kv_read, kv)
                pe.wait_ge(o_copied, 8 + 2 * h)
                for e in range(2):
                    c = h * 256 + e * P
                    for t in range(TT):
                        mm(bank[6 + e][:, t * P:t * P + P], gv[:, t, c:c + P], am[:, t, :], t == 0, False)
                    for n in range(7):
                        ins = mm(bank[6 + e][:, (n + 1) * 64:(n + 2) * 64], st[:, n, e * P:e * P + P],
                                 gq[:, h, (n + 1) * 64:(n + 2) * 64], False, n == 6)
                    ins.then_inc(o_psum, 1)
                stats(f"gla{h}", ones[:, :])
            for gr in G["gla_g"]:
                gemm(gr, "fm", h_hi, h_lo)
            merge(1)
            gemm(G["swa_k"][0], "fm", h_hi, h_lo)
            gemm(G["swa_v"][0], "tm", h_hi, h_lo)
            for gr in G["swa_q"]:
                gemm(gr, "fm", h_hi, h_lo)
            pe.wait_ge(copied_act, 9)
            pe.wait_ge(copied_dve, 9)
            pe.wait_ge(root_ready, ROOT["gla3"] + 1)
            pe.wait_ge(o_copied, 16)

            def swa_logits(n):
                kvh, qb = n // TT, n % TT
                if n >= 1:
                    pe.wait_ge(lg_read, 32 + 4 * n)
                k0 = max(qb - 1, 0) * P
                w = (qb + 1) * P - k0
                for i in range(4):
                    hp = slice((i % 2) * 64, (i % 2) * 64 + 64)
                    ins = mm(bank[4 + i % 2][:, (i // 2) * 256:(i // 2) * 256 + w],
                             sq[hp, 2 * kvh + i // 2, qb * P:qb * P + P], sk[hp, kvh, k0:k0 + w],
                             True, True)
                ins.then_inc(lg_psum, 1)

            swa_logits(0)
            pt = 0
            for n in range(16):
                kvh, qb = n // TT, n % TT
                if n + 1 < 16:
                    swa_logits(n + 1)
                pe.wait_ge(p_norm, 32 + n + 1)
                blocks = 1 if qb == 0 else 2
                for kb in range(blocks):
                    if pt:
                        pe.wait_ge(pt_ready, 32 + pt)
                    for i in range(4):
                        ins = pe.transpose(bank[6][:, i * P:i * P + P],
                                           lg[:, n % 2, i, kb * P:kb * P + P], ident)
                    ins.then_inc(pt_psum, 1)
                    pt += 1
                    pe.wait_ge(pt_ready, 32 + pt)
                    if kb == 0 and n:
                        pe.wait_ge(pv_read, 4 + n)
                    ins = mm(bank[7][:, :], svd[:, qb - blocks + 1 + kb, kvh, :],
                             spT[:, (pt - 1) % 2, :], kb == 0, kb == blocks - 1)
                    ins.then_inc(pv_psum, 1)
            merge(2)
            pe.wait_ge(act_low, AT["merged"] + 8)
            for gr in G["out2"]:
                gemm(gr, "fm", h_hi, h_lo)
            pe.wait_ge(pv_read, 4 + 16)
            stats("post1", ones[:, :])
            stats("norm2", ones[:, :])
            pe.wait_ge(act_low, AT["norm2"] + 8)
            for gr in G["ffn_up"]:
                gemm(gr, "fm", h_hi, h_lo)
            pe.wait_ge(act_low, AT["f"] + FT)
            for gr in G["ffn_down"]:
                gemm(gr, "fm", f_hi, f_lo)
            stats("post2", ones[:, :])

        @block.scalar
        def _(act):
            steps = 0

            def settle(ins):
                nonlocal steps
                steps += 1
                ins.then_inc(act_step, 1)
                act.wait_ge(act_step, steps)

            def split_high(s):
                if s >= SPLIT_TILES:
                    return
                i = SPLIT_AT[s]
                kt = STREAM[i][2][2]
                act.wait_ge(raw_loaded[i % RAW_SLOTS], 16 * (i // RAW_SLOTS + 1))
                if s >= 2:
                    act.wait_ge(*tile_used(s - 2))
                act.copy(w_hi[:, s % 2, 0:kt, :], w_raw[:, i % RAW_SLOTS, 0:kt, :]).then_inc(w_high, 1)

            def ahead(gr):
                for j in range(len(gr.kts)):
                    split_high(gr.s + j + 1)

            def high(a, dst, src=None):
                act.wait_ge(act_val, a + 1)
                act.copy(dst, tval[:, a % 2, :] if src is None else src).then_inc(act_high, 1)

            def square(name, m, src):
                i = SQ0[name] + m
                if i >= 2:
                    act.wait_ge(sq_used, i - 1)
                act.activation(sqb[:, i % 2, :], src, ACT.Square).then_inc(sq_ready, 1)

            def root_of(name, n, e=0):
                act.wait_ge(sq_used, SQ0[name] + sizes[name])
                if ROOT[name]:
                    act.wait_ge(rstd_ready, ROOT[name])
                act.activation(root[:, :], bank[4][:, :], ACT.Sqrt, bias=eps[:, e:e + 1],
                               scale=1.0 / n).then_inc(root_ready, 1)

            def norm(name, src, ready=None, ready0=0):
                for m in range(KT):
                    if ready is not None:
                        act.wait_ge(ready, ready0 + m + 1)
                    square(name, m, src[:, m, :])
                root_of(name, D)

            act.wait_ge(in_small, 80)
            act.activation(silu_c[:, :], vec[:, VEC["c"][0]:VEC["c"][1]], ACT.Silu).then_inc(c_ready, 1)
            act.wait_ge(bias_psum, 1)
            settle(act.copy(btab[:, 0:320], bank[4][0:HEADS, 0:320]))
            act.copy(btab[:, 320:640], bank[5][0:HEADS, 0:320]).then_inc(bias_copied, 1)
            act.wait_ge(setup_trig, 1)
            act.activation(sv[:, 10, :], sv[:, 9, :], ACT.Sin).then_inc(trig_ready, 1)
            act.activation(sv[:, 11, :], sv[:, 9, :], ACT.Sin, scale=0.5).then_inc(trig_ready, 1)
            for b in range(0, 8, 2):
                act.wait_ge(wint_psum, b + 1)
                dst = (wint_re, wint_im)[b // 4]
                act.copy(dst[:, 4 * (b % 4):4 * (b % 4) + 4, :],
                         bank[4][:, :].rearrange("p (i c) -> p i c", c=P)).then_inc(wint_act, 1)
            for b in range(0, 8, 2):
                act.wait_ge(strip_psum, b + 1)
                act.copy(strip[:, 4 * b:4 * b + 4, :],
                         bank[4][0:GCH, :].rearrange("p (i c) -> p i c", c=P)).then_inc(strip_act, 1)
            act.wait_ge(in_x, 16)
            act.wait_ge(consts_set, 3)
            norm("norm0", xr)
            split_high(0)
            act.wait_ge(strip_psum, 8)
            act.wait_ge(bias_stored, 16)
            for m in range(KT):
                high(AT["norm0"] + m, h_hi[:, m, :])
            for w, gr in enumerate(G["ssm_u"]):
                ahead(gr)
                act.wait_ge(group_done, 2 * gr.g + 1)
                act.wait_ge(toep_loaded, 16 * STEPS)
                for t in range(2):
                    act.copy(u4[:, 16 * w:16 * w + 16, 3 - t, :],
                             bank[pbanks(gr)[0]][:, t * WC:(t + 1) * WC]
                             .rearrange("p (g c) -> p g c", c=GCH)).then_inc(u_act, 1)
                act.wait_ge(u_act, 2 * w + 2)
                act.nop().then_inc(bank_free[pbanks(gr)[0]], 1)
            for b in range(0, 8, 2):
                act.wait_ge(ut_psum, b + 1)
                x = bank[4 + b % 4][0:64, :].rearrange("p (i k r) -> p i r k", i=4, r=2)
                settle(act.copy(ut[0:64, 4 * b:4 * b + 4, :], x[:, :, 1, :]))
                act.copy(ut[64:128, 4 * b:4 * b + 4, :], x[:, :, 0, :]).then_inc(ut_act, 1)
            for w, gr in enumerate(G["ssm_z"]):
                ahead(gr)
                for half in range(2):
                    act.wait_ge(group_done, 2 * gr.g + half + 1)
                    bk = pbanks(gr)[half]
                    act.activation(sz[:, 2 * w + half, :], bank[bk][:, :], ACT.Silu).then_inc(bank_free[bk], 1)
            for b in range(0, 8, 2):
                act.wait_ge(y_psum, b + 1)
                if b == 0:
                    act.wait_ge(ut_psum, 8)
                act.copy(u[:, :, 64 * b:64 * b + 64].rearrange("p t (i c) -> p i t c", c=GCH),
                         bank[4 + b % 4][0:64, :].rearrange("p (i t c) -> p i t c", i=4, t=STEPS)).then_inc(y_act, 1)
            for ct in range(4):
                act.wait_ge(zt_psum, ct + 1)
                act.activation(z32[:, ct, :].rearrange("p (k t) -> p k t", t=STEPS),
                               bank[4 + ct][:, :].rearrange("p (t k) -> p k t", t=STEPS),
                               ACT.Gelu_apprx_tanh).then_inc(z_ready, 1)
            for m in range(4):
                act.wait_ge(z_ready, m + 1)
                act.copy(y_hi[:, 4 + m, :], z32[:, m, :]).then_inc(act_high, 1)
            for w, gr in enumerate(G["glu"]):
                ahead(gr)
                for half in range(2):
                    m = 2 * w + half
                    bk = pbanks(gr)[half]
                    act.wait_ge(group_done, 2 * gr.g + half + 1)
                    if m >= 2:
                        act.wait_ge(sig_used, m - 1)
                    settle(act.activation(sgb[:, m % 2, :], bank[bk][:, :], ACT.Sigmoid, bias=v("b_glu", m)))
                    act.nop().then_inc(sig_ready, 1)
                    act.nop().then_inc(bank_free[bk], 1)
                for half in range(2):
                    m = 2 * w + half
                    high(AT["y_ssm"] + m, y_hi[:, m, :])
            for w, gr in enumerate(G["q_idx"]):
                ahead(gr)
                for half in range(2):
                    act.wait_ge(group_done, 2 * gr.g + half + 1)
                    bk = pbanks(gr)[half]
                    act.copy(qi[:, 2 * w + half, :], bank[bk][:, :]).then_inc(bank_free[bk], 1)
                    act.wait_ge(bank_free[bk], gr.g // 2 + 1)
            gr = G["k_idx"][0]
            ahead(gr)
            act.wait_ge(group_done, 2 * gr.g + 1)
            act.copy(ki[:, :], bank[pbanks(gr)[0]][:, :]).then_inc(bank_free[pbanks(gr)[0]], 1)
            act.wait_ge(bank_free[pbanks(gr)[0]], gr.g // 2 + 1)
            act.nop().then_inc(copied_act, 1)
            for i in range(32):
                qt = i // 8
                act.wait_ge(rel_psum, i + 1)
                if i >= 2:
                    act.wait_ge(rel_used, i - 1)
                else:
                    act.wait_ge(sig_used, 4)
                act.activation(sgb[:, i % 2, 0:P * (qt + 1)], bank[5 + i % 3][:, 0:P * (qt + 1)],
                               ACT.Relu).then_inc(relu_ready, 1)
            for i in range(8):
                name, m = ("q", i) if i < 4 else ("k", i - 4)
                gr = G[name][m // 2]
                if i % 2 == 0:
                    ahead(gr)
                bk = pbanks(gr)[m % 2]
                act.wait_ge(group_done, 2 * gr.g + m % 2 + 1)
                settle(act.copy((q32 if i < 4 else k32)[:, m, :], bank[bk][:, :]))
                square(f"qk{i}", 0, bank[bk][:, :])
                act.wait_ge(sq_ready, SQ0[f"qk{i}"] + 1)
                act.nop().then_inc(bank_free[bk], 1)
                root_of(f"qk{i}", 64)
            for w, gr in enumerate(G["v"]):
                ahead(gr)
                bk = pbanks(gr)[0]
                act.wait_ge(group_done, 2 * gr.g + 1)
                settle(act.copy(v32[:, 0:2, w * WC:(w + 1) * WC],
                                bank[bk][:, :].rearrange("p (t c) -> p t c", c=WC)))
                act.nop().then_inc(bank_free[bk], 1)
            act.nop().then_inc(copied_act, 1)
            for w, gr in enumerate(G["attn_z"]):
                ahead(gr)
                for half in range(2):
                    act.wait_ge(group_done, 2 * gr.g + half + 1)
                    bk = pbanks(gr)[half]
                    settle(act.activation(az[:, 2 * w + half, :], bank[bk][:, :], ACT.Silu))
                    act.nop().then_inc(bank_free[bk], 1)
            act.nop().then_inc(copied_act, 1)
            for i in range(33):
                if i < 32:
                    qt = i % TT
                    act.wait_ge(lg_ready, i + 1)
                    act.activation(sgb[:, i % 2, 0:P * (qt + 1)], sgb[:, i % 2, 0:P * (qt + 1)], ACT.Exp,
                                   bias=stat[:, 1, i:i + 1], accum_out=stat[:, 2, i:i + 1]).then_inc(p_exp, 1)
                if i >= 1:
                    j = i - 1
                    qt = j % TT
                    act.wait_ge(pt_psum, j + 1)
                    if j >= 2:
                        act.wait_ge(pv_psum, j - 1)
                    act.copy(pT[:, j % 2, 0:qt + 1, :],
                             bank[6][:, 0:P * (qt + 1)].rearrange("p (s c) -> p s c", c=P)).then_inc(pt_ready, 1)
                    if j % 8 == 7:
                        high(AT["y_attn"] + j // 8, y_hi[:, 4 + j // 8, :])
            for gr in G["out1"]:
                ahead(gr)
            norm("norm1", xr, x1_done)
            act.wait_ge(group_done, done("out1", 3))
            for m in range(KT):
                high(AT["norm1"] + m, h_hi[:, m, :])

            def copies(name, dst, scale=None):
                for w, gr in enumerate(G[name]):
                    ahead(gr)
                    bk = pbanks(gr)[0]
                    act.wait_ge(group_done, 2 * gr.g + 1)
                    act.activation(dst[:, 2 * w, :], bank[bk][:, :], ACT.Copy, scale=scale or 1.0)\
                       .then_inc(bank_free[bk], 1)
                    act.wait_ge(bank_free[bk], gr.g // 2 + 1)

            def copies_tm(name, dst):
                for w, gr in enumerate(G[name]):
                    ahead(gr)
                    bk = pbanks(gr)[0]
                    act.wait_ge(group_done, 2 * gr.g + 1)
                    act.copy(dst[:, 0:2, w * WC:(w + 1) * WC],
                             bank[bk][:, :].rearrange("p (t c) -> p t c", c=WC)).then_inc(bank_free[bk], 1)
                    act.wait_ge(bank_free[bk], gr.g // 2 + 1)

            def head_outputs(h, base, dst):
                if base + h:
                    act.wait_ge(on_ready, base + 2 * h)
                if base and h == 0:
                    act.wait_ge(sig_used, SIG["gla_g"])
                for e in range(2):
                    act.wait_ge(o_psum, base + 2 * h + e + 1)
                    act.copy(dst[:, e, :], bank[6 + e][:, :]).then_inc(o_copied, 1)

            def gated(name, n):
                act.wait_ge(on_ready, 8 * (n + 1))
                for w, gr in enumerate(G[name]):
                    ahead(gr)
                    for half in range(2):
                        m = 2 * w + half
                        bk = pbanks(gr)[half]
                        act.wait_ge(group_done, 2 * gr.g + half + 1)
                        act.wait_ge(sig_used, SIG[name] + m - 1)
                        act.activation(sgb[:, m % 2, :], bank[bk][:, :], ACT.Silu).then_inc(bank_free[bk], 1)
                        act.wait_ge(bank_free[bk], gr.g // 2 + 1)
                        act.nop().then_inc(sig_ready, 1)
                    for half in range(2):
                        m = 2 * w + half
                        high(AT[f"y{n}"] + m, y_hi[:, m, :])

            def merge(n):
                for i, gr in enumerate(G[f"merge{n}"]):
                    ahead(gr)
                    if i % 2 == 0:
                        for half in range(2):
                            m = i + half
                            bk = pbanks(gr)[half]
                            act.wait_ge(group_done, 2 * gr.g + half + 1)
                            act.wait_ge(sig_used, SIG[f"merge{n}"] + m - 1)
                            act.activation(sgb[:, m % 2, :], bank[bk][:, :], ACT.Sigmoid)\
                               .then_inc(bank_free[bk], 1)
                            act.wait_ge(bank_free[bk], gr.g // 2 + 1)
                            act.nop().then_inc(sig_ready, 1)

            copies("ret_q", rq)
            copies("ret_k", rk)
            copies_tm("ret_v", rv)
            act.nop().then_inc(copied_act, 2)
            for h in range(4):
                head_outputs(h, 0, o32)
                for e in range(2):
                    act.wait_ge(oc_ready, 2 * h + e + 1)
                    square(f"ret{h}", e, oc[:, e, :])
                root_of(f"ret{h}", 256, e=1)
            gated("ret_g", 0)
            merge(0)
            copies("gla_q", gq)
            copies("gla_k", gk)
            copies_tm("gla_v", gv)
            gr = G["gla_a"][0]
            ahead(gr)
            bk = pbanks(gr)
            act.wait_ge(group_done, 2 * gr.g + 1)
            settle(act.copy(ga[:, :], bank[bk[0]][0:GCH, :]))
            act.wait_ge(group_done, 2 * gr.g + 2)
            act.nop().then_inc(bank_free[bk[0]], 1)
            act.nop().then_inc(bank_free[bk[1]], 1)
            act.nop().then_inc(copied_act, 2)
            for h in range(4):
                act.wait_ge(gz_ready, h + 1)
                settle(act.activation(lb[:, :], la[:, :], ACT.Abs))
                settle(act.activation(lb[:, :], lb[:, :], ACT.Exp, scale=-1.0))
                act.activation(lb[:, :], lb[:, :], ACT.Ln, bias=1.0).then_inc(gsp_ready, 1)
                act.wait_ge(gb_ready, h + 1)
                act.activation(eb[:, :], lb[:, :], ACT.Exp).then_inc(gexp_ready, 1)
                act.activation(la[:, :], lb[:, :], ACT.Exp, scale=-1.0).then_inc(gexp_ready, 1)
                act.wait_ge(gkdT_psum, h + 1)
                act.copy(kdT[:, :, :], bank[5][:, :].rearrange("p (t c) -> p t c", c=P)).then_inc(gkdT_ready, 1)
                head_outputs(h, 8, sgb)
                for e in range(2):
                    act.wait_ge(o_copied, 8 + 2 * h + e + 1)
                    square(f"gla{h}", e, sgb[:, e, :])
                root_of(f"gla{h}", 256)
            gated("gla_g", 1)
            merge(1)
            gr = G["swa_k"][0]
            ahead(gr)
            for half in range(2):
                bk = pbanks(gr)[half]
                act.wait_ge(group_done, 2 * gr.g + half + 1)
                settle(act.copy(sk[0:64, 2 * half, :], bank[bk][0:64, :]))
                settle(act.copy(sk[64:128, 2 * half, :], bank[bk][0:64, :]))
                settle(act.copy(sk[0:64, 2 * half + 1, :], bank[bk][64:128, :]))
                settle(act.copy(sk[64:128, 2 * half + 1, :], bank[bk][64:128, :]))
                act.nop().then_inc(bank_free[bk], 1)
            ahead(G["swa_v"][0])
            copies("swa_q", sq, 0.125)
            act.nop().then_inc(copied_act, 2)

            def window_copies(n, pt):
                kvh, qb = n // TT, n % TT
                for _ in range(1 if qb == 0 else 2):
                    act.wait_ge(pt_psum, 32 + pt + 1)
                    if pt >= 2:
                        act.wait_ge(pv_psum, 32 + pt - 1)
                    act.copy(spT[:, pt % 2, :], bank[6][:, :]).then_inc(pt_ready, 1)
                    pt += 1
                if qb == TT - 1:
                    for i in range(2):
                        high(AT["y2"] + 2 * kvh + i, y_hi[:, 2 * kvh + i, :], yb[:, i, :])
                return pt

            pt = 0
            for n in range(17):
                if n == 16:
                    pt = window_copies(15, pt)
                    break
                kvh, qb = n // TT, n % TT
                blocks = 1 if qb == 0 else 2
                w = blocks * P
                c = 4 * n
                act.wait_ge(lg_ready, 32 + n + 1)
                for i in range(4):
                    ins = act.activation(lg[:, n % 2, i, 0:w], lg[:, n % 2, i, 0:w], ACT.Exp,
                                         bias=sst[:, 1, c + i:c + i + 1], accum_out=sst[:, 2, c + i:c + i + 1])
                settle(ins)
                settle(act.activation(sst[:, 4, c:c + 4], sst[:, 3, c:c + 4], ACT.Exp))
                act.nop().then_inc(p_exp, 1)
                if n:
                    pt = window_copies(n - 1, pt)
            merge(2)
            for m in range(KT):
                act.wait_ge(group_done, done("merge2", 7))
                act.wait_ge(merged_ready, m + 1)
                act.copy(h_hi[:, m, :], merged[:, m, :]).then_inc(act_high, 1)
            for w, gr in enumerate(G["out2"]):
                ahead(gr)
                bk = pbanks(gr)[0]
                act.wait_ge(group_done, 2 * gr.g + 1)
                act.copy(mo[:, 2 * w, :], bank[bk][:, :]).then_inc(bank_free[bk], 1)
                act.wait_ge(bank_free[bk], gr.g // 2 + 1)
            for m in range(KT):
                if m % 2:
                    act.wait_ge(mo_ready, m // 2 + 1)
                square("post1", m, mo[:, m, :])
            root_of("post1", D)
            norm("norm2", xr, x2_ready)
            act.wait_ge(group_done, done("out2", 3))
            for m in range(KT):
                high(AT["norm2"] + m, h_hi[:, m, :])
            for i, gr in enumerate(G["ffn_up"]):
                ahead(gr)
                if i % 2 == 0:
                    for half in range(2):
                        m = i + half
                        bk = pbanks(gr)[half]
                        act.wait_ge(group_done, 2 * gr.g + half + 1)
                        act.wait_ge(sig_used, SIG["ffn_up"] + m - 1)
                        act.activation(sgb[:, m % 2, :], bank[bk][:, :], ACT.Silu).then_inc(bank_free[bk], 1)
                        act.wait_ge(bank_free[bk], gr.g // 2 + 1)
                        act.nop().then_inc(sig_ready, 1)
                else:
                    for half in range(2):
                        high(AT["f"] + i - 1 + half, f_hi[:, i - 1 + half, :])
            for w, gr in enumerate(G["ffn_down"]):
                ahead(gr)
                bk = pbanks(gr)[0]
                act.wait_ge(group_done, 2 * gr.g + 1)
                act.copy(down[:, 2 * w, :], bank[bk][:, :]).then_inc(bank_free[bk], 1)
                act.wait_ge(bank_free[bk], gr.g // 2 + 1)
            for m in range(KT):
                if m % 2:
                    act.wait_ge(dn_ready, m // 2 + 1)
                square("post2", m, down[:, m, :])
            root_of("post2", D)

        @block.vector
        def _(dve):
            steps = 0

            def settle(ins):
                nonlocal steps
                steps += 1
                ins.then_inc(dve_step, 1)
                dve.wait_ge(dve_step, steps)

            def tt(out, a, b, op):
                settle(dve.tensor_tensor(out, a, b, op))

            def ts(out, a, s1, s2, op0, op1=None):
                settle(dve.tensor_scalar(out, a, s1, s2, op0, op1) if op1 is not None
                       else dve.tensor_scalar(out, a, s1, None, op0))

            def stt(out, a, s, b, op0, op1):
                settle(dve.scalar_tensor_tensor(out=out, in0=a, scalar=s, in1=b, op0=op0, op1=op1))

            def cmul(o, a, b, t, negative=False):
                tt(o[0], a[0], b[0], ALU.mult)
                tt(t, a[1], b[1], ALU.mult)
                tt(o[0], o[0], t, ALU.subtract)
                tt(t, a[0], b[1], ALU.mult)
                tt(o[1], a[1], b[0], ALU.mult)
                if negative:
                    stt(o[1], t, -1.0, o[1], ALU.mult, ALU.subtract)
                else:
                    tt(o[1], o[1], t, ALU.add)

            def exponential(out, x, t):
                n, f, p = sv[:, t, :], sv[:, t + 1, :], sv[:, t + 2, :]
                ts(out, x, -87.0, 88.0, ALU.max, ALU.min)
                ts(n, out, 1.4426950408889634, 12582912.0, ALU.mult, ALU.add)
                ts(n, n, 12582912.0, None, ALU.subtract)
                stt(f, n, -0.693359375, out, ALU.mult, ALU.add)
                stt(f, n, 2.12194440e-4, f, ALU.mult, ALU.add)
                ts(p, f, 1.0 / 40320, None, ALU.mult)
                for c in (1.0 / 5040, 1.0 / 720, 1.0 / 120, 1.0 / 24, 1.0 / 6, 0.5, 1.0):
                    stt(p, p, c, f, ALU.add, ALU.mult)
                ts(p, p, 1.0, None, ALU.add)
                ts(f.bitcast(i32), n, 127.0, None, ALU.add)
                ts(f.bitcast(i32), f.bitcast(i32), 23, None, ALU.logical_shift_left)
                tt(out, p, f, ALU.mult)

            def split_low(s):
                if s >= SPLIT_TILES:
                    return
                i = SPLIT_AT[s]
                kt = STREAM[i][2][2]
                dve.wait_ge(w_high, s + 1)
                dve.tensor_tensor(w_lo[:, s % 2, 0:kt, :], w_raw[:, i % RAW_SLOTS, 0:kt, :],
                                  w_hi[:, s % 2, 0:kt, :].bitcast(f32), ALU.subtract).then_inc(w_low, 1)

            def ahead(gr):
                for j in range(len(gr.kts)):
                    split_low(gr.s + j + 1)

            def new_val(a):
                if a >= 2:
                    dve.wait_ge(act_low, a - 1)
                return tval[:, a % 2, :]

            def low(a, dst, hi, src=None):
                dve.wait_ge(act_high, a + 1)
                dve.tensor_tensor(dst, tval[:, a % 2, :] if src is None else src, hi.bitcast(f32),
                                  ALU.subtract).then_inc(act_low, 1)

            def rstd_of(name):
                dve.wait_ge(root_ready, ROOT[name] + 1)
                dve.reciprocal(rstd[:, :], root[:, :]).then_inc(rstd_ready, 1)
                dve.wait_ge(rstd_ready, ROOT[name] + 1)

            def norm(name, src, gain, shift=None):
                rstd_of(name)
                for m in range(KT + 1):
                    if m < KT:
                        a = AT[name] + m
                        t = new_val(a)
                        if shift is None:
                            dve.scalar_tensor_tensor(out=t, in0=src[:, m, :], scalar=gain(m), in1=rstd[:, :],
                                                     op0=ALU.mult, op1=ALU.mult).then_inc(act_val, 1)
                        else:
                            stt(t, src[:, m, :], gain(m), rstd[:, :], ALU.mult, ALU.mult)
                            dve.tensor_scalar(t, t, shift(m), None, ALU.add).then_inc(act_val, 1)
                    if m:
                        low(AT[name] + m - 1, h_lo[:, m - 1, :], h_hi[:, m - 1, :])

            dve.wait_ge(in_ssm, 80)
            log_dt, are, aim = sv[:, 0, :], sv[:, 1, :], sv[:, 2, :]
            dt, arg = sv[:, 3, :], sv[:, 9, :]
            exponential(dt, log_dt, 4)
            re, im, mag = sv[:, 12, :], sv[:, 13, :], sv[:, 14, :]
            tt(re, are, dt, ALU.mult)
            tt(im, aim, dt, ALU.mult)
            exponential(mag, re, 4)
            turns = sv[:, 4, :]
            ts(turns, im, 0.15915494309189535, 12582912.0, ALU.mult, ALU.add)
            ts(turns, turns, 12582912.0, None, ALU.subtract)
            stt(arg, turns, -6.28125, im, ALU.mult, ALU.add)
            stt(arg, turns, -1.9350051879882812e-3, arg, ALU.mult, ALU.add)
            stt(arg, turns, -3.0199159819e-7, arg, ALU.mult, ALU.add)
            ts(arg, arg, -3.1415925, 3.1415925, ALU.max, ALU.min)
            dve.nop().then_inc(setup_trig, 1)
            dve.wait_ge(trig_ready, 2)
            sin, half_sin, cos = sv[:, 10, :], sv[:, 11, :], sv[:, 15, :]
            tt(cos, half_sin, half_sin, ALU.mult)
            ts(cos, cos, -2.0, 1.0, ALU.mult, ALU.add)
            lre, lim = sv[:, 16, :], sv[:, 17, :]
            tt(lre, mag, cos, ALU.mult)
            tt(lim, mag, sin, ALU.mult)
            lm1, den, fre, fim, t0 = (sv[:, i, :] for i in (18, 19, 20, 21, 5))
            ts(lm1, lre, 1.0, None, ALU.subtract)
            tt(den, are, are, ALU.mult)
            tt(t0, aim, aim, ALU.mult)
            tt(den, den, t0, ALU.add)
            settle(dve.reciprocal(den, den))
            tt(fre, lm1, are, ALU.mult)
            tt(t0, lim, aim, ALU.mult)
            tt(fre, fre, t0, ALU.add)
            tt(fim, lim, are, ALU.mult)
            tt(t0, lm1, aim, ALU.mult)
            tt(fim, fim, t0, ALU.subtract)
            tt(fre, fre, den, ALU.mult)
            tt(fim, fim, den, ALU.mult)

            def over_c(x):
                return x[:, :, None].to_broadcast([P, PAIRS, GCH])

            tb = tmp[:, 0:PAIRS * GCH].rearrange("p (j c) -> p j c", c=GCH)
            cmul((bb_re[:, :, :], bb_im[:, :, :]), (over_c(fre), over_c(fim)),
                 (b_re[:, :, :], b_im[:, :, :]), tb)
            settle(dve.memset(pw_re[:, 0, :], 1.0))
            settle(dve.memset(pw_im[:, 0, :], 0.0))
            settle(dve.tensor_copy(pw_re[:, 1, :], lre))
            settle(dve.tensor_copy(pw_im[:, 1, :], lim))
            n = 1
            while n < STEPS:
                top = (pw_re[:, n:n + 1, :].to_broadcast([P, n, PAIRS]),
                       pw_im[:, n:n + 1, :].to_broadcast([P, n, PAIRS]))
                cmul((pw_re[:, n + 1:2 * n + 1, :], pw_im[:, n + 1:2 * n + 1, :]),
                     (pw_re[:, 1:n + 1, :], pw_im[:, 1:n + 1, :]), top,
                     tmp[:, 0:n * PAIRS].rearrange("p (t j) -> p t j", j=PAIRS))
                n *= 2
            for half in range(2):
                js = slice(8 * half, 8 * half + 8)
                shape = [P, 8, STEPS, GCH]
                tw = tmp[:, 0:1024].rearrange("p (j t c) -> p j t c", j=8, t=STEPS)

                def power(x, t0, t1, n):
                    return x[:, t0:t1, js].rearrange("p t j -> p j t")[:, :, :, None]\
                        .to_broadcast([P, 8, n, GCH])

                cmul(tuple(w[:, js, :].rearrange("p j (t c) -> p j t c", c=GCH) for w in (win_re, win_im)),
                     tuple(x[:, js, None, :].to_broadcast(shape) for x in (bb_re, bb_im)),
                     (power(pw_re, 0, STEPS, STEPS), power(pw_im, 0, STEPS, STEPS)), tw)
            dve.nop().then_inc(win_ready, 1)
            n = STEPS + 1
            dve.wait_ge(cl_zero, 2)
            for q in range(4):
                js = slice(4 * q, 4 * q + 4)
                sh = "p (j t c) -> p j t c"
                p1 = tmp[:, 0:576].rearrange(sh, j=4, t=n)
                p2 = tmp[:, 576:1152].rearrange(sh, j=4, t=n)
                ca, cb = (x[:, js, None, :].to_broadcast([P, 4, n, GCH]) for x in (c_re, c_im))
                wa, wb = (x[:, :, js].rearrange("p t j -> p j t")[:, :, :, None].to_broadcast([P, 4, n, GCH])
                          for x in (pw_re, pw_im))
                for out, x, y, z, w, op in ((cl_re, ca, wa, cb, wb, ALU.subtract),
                                            (cl_im, ca, wb, cb, wa, ALU.add)):
                    tt(p1, x, y, ALU.mult)
                    tt(p2, z, w, ALU.mult)
                    for r in range(2):
                        rows = slice(64 * r, 64 * r + 64)
                        o = out[rows, js, r, :].rearrange("p j (t c) -> p j t c", c=GCH)
                        if op == ALU.add:
                            ts(p1[rows], p1[rows], -1.0, None, ALU.mult)
                            tt(o, p1[rows], p2[rows], ALU.subtract)
                        else:
                            tt(o, p1[rows], p2[rows], ALU.subtract)
            dve.nop().then_inc(cl_ready, 1)
            for b in range(1, 8, 2):
                dve.wait_ge(wint_psum, b + 1)
                dst = (wint_re, wint_im)[b // 4]
                dve.tensor_copy(dst[:, 4 * (b % 4):4 * (b % 4) + 4, :],
                                bank[5][:, :].rearrange("p (i c) -> p i c", c=P)).then_inc(wint_dve, 1)
            pa, pb_ = [(sv[:, 4, :], sv[:, 5, :]), (sv[:, 6, :], sv[:, 7, :])], sv[:, 8, :]
            cmul(pa[0], (cos, sin), (cos, sin), pb_)
            cmul(pa[1], pa[0], pa[0], pb_)
            cmul(pa[0], pa[1], pa[1], pb_)
            tt(rho[:, :], mag, mag, ALU.mult)
            tt(rho[:, :], rho[:, :], rho[:, :], ALU.mult)
            tt(rho[:, :], rho[:, :], rho[:, :], ALU.mult)
            settle(dve.memset(cos_t[:, :, 0:1], 1.0))
            settle(dve.memset(sin_t[:, :, 0:1], 0.0))
            n, at = 1, 0
            while n < CHUNKS:
                by = tuple(x[:, :, None].to_broadcast([P, PAIRS, n]) for x in pa[at])
                cmul((cos_t[:, :, n:2 * n], sin_t[:, :, n:2 * n]), (cos_t[:, :, 0:n], sin_t[:, :, 0:n]), by,
                     tmp[:, 0:n * PAIRS].rearrange("p (j k) -> p j k", j=PAIRS))
                n *= 2
                if n < CHUNKS:
                    cmul(pa[1 - at], pa[at], pa[at], pb_)
                    at = 1 - at
            for b in range(1, 8, 2):
                dve.wait_ge(strip_psum, b + 1)
                dve.tensor_copy(strip[:, 4 * b:4 * b + 4, :],
                                bank[5][0:GCH, :].rearrange("p (i c) -> p i c", c=P)).then_inc(strip_dve, 1)
            dve.wait_ge(strip_act, 4)
            dve.wait_ge(strip_dve, 4)
            diag = tmp[0:GCH, 0:GROUPS * GCH].rearrange("p (g c) -> p g c", c=GCH)
            tt(diag, ident[0:GCH, None, 0:GCH].to_broadcast([GCH, GROUPS, GCH]),
               dsk[:, :, None].to_broadcast([GCH, GROUPS, GCH]), ALU.mult)
            dve.tensor_tensor(strip[:, :, 0:GCH], strip[:, :, 0:GCH], diag, ALU.add).then_inc(strip_ready, 1)
            a0 = VEC["b_ada"][0]
            dve.wait_ge(ada_done, 1)
            tt(modv[:, 0:16], bank[7][:, 0:16], vec[:, a0:a0 + 16], ALU.add)
            g0 = VEC["norm_g"][0]
            dve.scalar_tensor_tensor(out=gs[:, :], in0=modv[:, 8:16], scalar=1.0, in1=vec[:, g0:g0 + 8],
                                     op0=ALU.add, op1=ALU.mult).then_inc(mod_ready, 1)
            dve.wait_ge(mod_ready, 1)
            norm("norm0", xr, lambda m: gs[:, m:m + 1], lambda m: modv[:, m:m + 1])
            split_low(0)
            for w, gr in enumerate(G["ssm_u"]):
                ahead(gr)
                dve.wait_ge(group_done, 2 * gr.g + 2)
                dve.wait_ge(toep_loaded, 16 * STEPS)
                for t in range(2):
                    dve.tensor_copy(u4[:, 16 * w:16 * w + 16, 1 - t, :],
                                    bank[pbanks(gr)[1]][:, t * WC:(t + 1) * WC]
                                    .rearrange("p (g c) -> p g c", c=GCH)).then_inc(u_dve, 1)
                dve.wait_ge(u_dve, 2 * w + 2)
                dve.nop().then_inc(bank_free[pbanks(gr)[1]], 1)
            for b in range(1, 8, 2):
                dve.wait_ge(ut_psum, b + 1)
                x = bank[4 + b % 4][0:64, :].rearrange("p (i k r) -> p i r k", i=4, r=2)
                settle(dve.tensor_copy(ut[0:64, 4 * b:4 * b + 4, :], x[:, :, 1, :]))
                dve.tensor_copy(ut[64:128, 4 * b:4 * b + 4, :], x[:, :, 0, :]).then_inc(ut_dve, 1)
            t1 = tval[:, 0, :].rearrange("p (j k) -> p j k", k=CHUNKS)
            t2 = tval[:, 1, :].rearrange("p (j k) -> p j k", k=CHUNKS)
            for half in range(2):
                js = slice(8 * half, 8 * half + 8)
                dve.wait_ge(x_psum, 2 * half + 2)
                zr = bank[4 + half][:, :].rearrange("p (j k) -> p j k", k=CHUNKS)
                zi = bank[6 + half][:, :].rearrange("p (j k) -> p j k", k=CHUNKS)
                tt(t1, zr, cos_t[:, js, :], ALU.mult)
                tt(t2, zi, sin_t[:, js, :], ALU.mult)
                tt(xa[:, js, :], t1, t2, ALU.add)
                tt(t1, zi, cos_t[:, js, :], ALU.mult)
                tt(t2, zr, sin_t[:, js, :], ALU.mult)
                tt(xb[:, js, :], t1, t2, ALU.subtract)
                for j in range(8 * half, 8 * half + 8):
                    for x in (xa, xb):
                        ins = dve.tensor_tensor_scan(x[:, j, :], rho[:, j:j + 1].to_broadcast([P, CHUNKS]),
                                                     x[:, j, :], 0.0, ALU.mult, ALU.add)
                settle(ins)
                a, b, n = xa[:, js, 0:CHUNKS - 1], xb[:, js, 0:CHUNKS - 1], CHUNKS - 1
                cs, sn = cos_t[:, js, 0:n], sin_t[:, js, 0:n]
                cmul((ga_[:, js, 1:CHUNKS], gb_[:, js, 1:CHUNKS]), (a, b), (cs, sn), t1[:, :, 0:n])
            settle(dve.memset(ga_[:, :, 0:1], 0.0))
            dve.memset(gb_[:, :, 0:1], 0.0).then_inc(state_ready, 1)
            for gr in G["ssm_z"]:
                ahead(gr)
            for b in range(1, 8, 2):
                dve.wait_ge(y_psum, b + 1)
                dve.tensor_copy(u[:, :, 64 * b:64 * b + 64].rearrange("p t (i c) -> p i t c", c=GCH),
                                bank[4 + b % 4][0:64, :].rearrange("p (i t c) -> p i t c", i=4, t=STEPS))\
                   .then_inc(y_dve, 1)
            for m in range(4):
                dve.wait_ge(z_ready, m + 1)
                dve.nop().then_inc(act_val, 1)
                low(AT["z"] + m, y_lo[:, 4 + m, :], y_hi[:, 4 + m, :], z32[:, m, :])
            for w, gr in enumerate(G["glu"]):
                ahead(gr)
                for half in range(2):
                    m = 2 * w + half
                    dve.wait_ge(sig_ready, m + 1)
                    tt(sgb[:, m % 2, :], sgb[:, m % 2, :], z32[:, m, :], ALU.mult)
                    a = AT["y_ssm"] + m
                    dve.tensor_tensor(new_val(a), sgb[:, m % 2, :], sz[:, m, :], ALU.mult).then_inc(act_val, 1)
                    dve.wait_ge(act_val, a + 1)
                    dve.nop().then_inc(sig_used, 1)
                for half in range(2):
                    m = 2 * w + half
                    low(AT["y_ssm"] + m, y_lo[:, m, :], y_hi[:, m, :])
            for gr in G["q_idx"]:
                ahead(gr)
            gr = G["k_idx"][0]
            ahead(gr)
            bk = pbanks(gr)[1]
            dve.wait_ge(group_done, 2 * gr.g + 2)
            ts(wi[:, :, :], bank[bk][:, 0:TT * HEADS].rearrange("p (t h) -> p t h", h=HEADS),
               float(HEADS) ** -0.5, None, ALU.mult)
            dve.nop().then_inc(bank_free[bk], 1)
            dve.nop().then_inc(copied_dve, 1)
            for i in range(32):
                qt, h = i // 8, i % 8
                w = P * (qt + 1)
                dve.wait_ge(relu_ready, i + 1)
                if h == 0:
                    dve.tensor_scalar(score[:, qt, 0:w], sgb[:, i % 2, 0:w], wi[:, qt, h:h + 1], None,
                                      ALU.mult).then_inc(rel_used, 1)
                else:
                    dve.scalar_tensor_tensor(out=score[:, qt, 0:w], in0=sgb[:, i % 2, 0:w],
                                             scalar=wi[:, qt, h:h + 1], in1=score[:, qt, 0:w],
                                             op0=ALU.mult, op1=ALU.add).then_inc(rel_used, 1)
                dve.wait_ge(rel_used, i + 1)
                if h == 7 and qt:
                    tt(score[:, qt, qt * P:w], score[:, qt, qt * P:w], causal, ALU.add)
            ts(score[:, 0, 0:P], causal, NEG_BETWEEN / 2, NEG_LOGIT, ALU.is_lt, ALU.mult)
            m8 = small[:, 0:8]
            rounds = 0

            def select_keys(n):
                nonlocal rounds
                for _ in range(n):
                    qt = 1 + rounds // (TOPK // 8)
                    if qt >= TT:
                        return
                    s = score[:, qt, 0:P * (qt + 1)]
                    settle(dve.max(m8, s))
                    settle(dve.match_replace(s, m8, s, NEG_TAKEN))
                    rounds += 1
                    if rounds % (TOPK // 8) == 0:
                        ts(s, s, NEG_BETWEEN, NEG_LOGIT, ALU.is_ge, ALU.mult)

            ts(qg[:, :], v("q_gain", 0), 0.125, None, ALU.mult)
            for i in range(8):
                name, m = ("q", i) if i < 4 else ("k", i - 4)
                if i % 2 == 0:
                    ahead(G[name][m // 2])
                rstd_of(f"qk{i}")
                x = (q32 if i < 4 else k32)[:, m, :]
                stt(x, x, qg[:, 0:1] if i < 4 else v("k_gain", 0), rstd[:, :], ALU.mult, ALU.mult)
                select_keys(4)
            for w, gr in enumerate(G["v"]):
                ahead(gr)
                bk = pbanks(gr)[1]
                dve.wait_ge(group_done, 2 * gr.g + 2)
                settle(dve.tensor_copy(v32[:, 2:4, w * WC:(w + 1) * WC],
                                       bank[bk][:, :].rearrange("p (t c) -> p t c", c=WC)))
                dve.nop().then_inc(bank_free[bk], 1)
                select_keys(4)
            for gr in G["attn_z"]:
                ahead(gr)
                select_keys(4)
            dve.wait_ge(ada_done, 2)
            dve.tensor_tensor(modv[:, 16:24], bank[7][:, 16:24], vec[:, a0 + 16:a0 + 24], ALU.add)\
               .then_inc(mod_ready, 1)
            dve.wait_ge(mod_ready, 2)
            dve.nop().then_inc(copied_dve, 2)
            dve.wait_ge(bias_loaded, 16)

            def masked_logits(i):
                h, qt = i // TT, i % TT
                w = P * (qt + 1)
                s = sgb[:, i % 2, 0:w]
                dve.wait_ge(lg_psum, i + 1)
                if i >= 2:
                    dve.wait_ge(pt_psum, i - 1)
                dve.tensor_tensor(s, bank[4 + i % 2][:, 0:w], bias[:, h, SEQ - w:SEQ], ALU.add)\
                   .then_inc(lg_read, 1)
                dve.wait_ge(lg_read, i + 1)
                settle(dve.tensor_tensor_reduce(s, s, score[:, qt, 0:w], 1.0, -3e38, ALU.add, ALU.max,
                                                stat[:, 0, i:i + 1]))
                dve.tensor_scalar(stat[:, 1, i:i + 1], stat[:, 0, i:i + 1], -1.0, None, ALU.mult)\
                   .then_inc(lg_ready, 1)

            def attn_out(j):
                m = j // 8
                a = AT["y_attn"] + m
                dve.wait_ge(pv_psum, j + 1)
                dve.tensor_tensor(new_val(a), bank[7][:, :], az[:, m, :], ALU.mult).then_inc(act_val, 1)
                dve.wait_ge(act_val, a + 1)
                dve.nop().then_inc(pv_read, 1)
                low(a, y_lo[:, 4 + m, :], y_hi[:, 4 + m, :])

            masked_logits(0)
            for i in range(32):
                if i + 1 < 32:
                    masked_logits(i + 1)
                w = P * (i % TT + 1)
                dve.wait_ge(p_exp, i + 1)
                settle(dve.reciprocal(stat[:, 3, i:i + 1], stat[:, 2, i:i + 1]))
                dve.tensor_scalar(sgb[:, i % 2, 0:w], sgb[:, i % 2, 0:w], stat[:, 3, i:i + 1], None,
                                  ALU.mult).then_inc(p_norm, 1)
                if i >= 1 and (i - 1) % 8 == 7:
                    attn_out(i - 1)
            attn_out(31)
            dve.wait_ge(x_reload, 16)
            for w, gr in enumerate(G["out1"]):
                ahead(gr)
                for half in range(2):
                    m = 2 * w + half
                    bk = pbanks(gr)[half]
                    dve.wait_ge(group_done, 2 * gr.g + half + 1)
                    dve.scalar_tensor_tensor(out=xr[:, m, :], in0=bank[bk][:, :], scalar=modv[:, 16 + m:17 + m],
                                             in1=xr[:, m, :], op0=ALU.mult, op1=ALU.add).then_inc(x1_done, 1)
                    dve.wait_ge(x1_done, m + 1)
                    dve.nop().then_inc(bank_free[bk], 1)
            norm("norm1", xr, lambda m: v("norm_mix_pre", m))

            def copies(name, dst, signal=None, scale=None):
                for w, gr in enumerate(G[name]):
                    ahead(gr)
                    bk = pbanks(gr)[1]
                    dve.wait_ge(group_done, 2 * gr.g + 2)
                    if scale is None:
                        ins = dve.tensor_copy(dst[:, 2 * w + 1, :], bank[bk][:, :])
                    else:
                        ins = dve.tensor_scalar(dst[:, 2 * w + 1, :], bank[bk][:, :], scale, None, ALU.mult)
                    ins.then_inc(bank_free[bk], 1)
                    dve.wait_ge(bank_free[bk], gr.g // 2 + 1)
                    if signal is not None:
                        dve.nop().then_inc(signal, 1)

            def copies_tm(name, dst):
                for w, gr in enumerate(G[name]):
                    ahead(gr)
                    bk = pbanks(gr)[1]
                    dve.wait_ge(group_done, 2 * gr.g + 2)
                    dve.tensor_copy(dst[:, 2:4, w * WC:(w + 1) * WC],
                                    bank[bk][:, :].rearrange("p (t c) -> p t c", c=WC)).then_inc(bank_free[bk], 1)
                    dve.wait_ge(bank_free[bk], gr.g // 2 + 1)

            def gated(name, n, bias_name=None):
                for w, gr in enumerate(G[name]):
                    ahead(gr)
                    for half in range(2):
                        m = 2 * w + half
                        a = AT[f"y{n}"] + m
                        t = new_val(a)
                        dve.wait_ge(sig_ready, SIG[name] + m + 1)
                        if bias_name:
                            ins = dve.scalar_tensor_tensor(out=t, in0=on[:, m, :], scalar=v(bias_name, m),
                                                           in1=sgb[:, m % 2, :], op0=ALU.add, op1=ALU.mult)
                        else:
                            ins = dve.tensor_tensor(t, on[:, m, :], sgb[:, m % 2, :], ALU.mult)
                        ins.then_inc(act_val, 1)
                        dve.wait_ge(act_val, a + 1)
                        dve.nop().then_inc(sig_used, 1)
                    for half in range(2):
                        m = 2 * w + half
                        low(AT[f"y{n}"] + m, y_lo[:, m, :], y_hi[:, m, :])

            def merge(n):
                for i, gr in enumerate(G[f"merge{n}"]):
                    ahead(gr)
                    if i % 2 == 0:
                        continue
                    for half in range(2):
                        m = i - 1 + half
                        bk = pbanks(gr)[half]
                        dve.wait_ge(sig_ready, SIG[f"merge{n}"] + m + 1)
                        dve.wait_ge(group_done, 2 * gr.g + half + 1)
                        g = sgb[:, m % 2, :]
                        if n == 0:
                            tt(merged[:, m, :], g, bank[bk][:, :], ALU.mult)
                        else:
                            tt(g, g, bank[bk][:, :], ALU.mult)
                            tt(merged[:, m, :], merged[:, m, :], g, ALU.add)
                        dve.nop().then_inc(bank_free[bk], 1)
                        dve.nop().then_inc(sig_used, 1)
                        if n == 2:
                            dve.nop().then_inc(merged_ready, 1)

            copies("ret_q", rq)
            copies("ret_k", rk)
            copies_tm("ret_v", rv)
            dve.nop().then_inc(copied_dve, 2)
            dve.wait_ge(dec_loaded, 16)
            dve.wait_ge(group_done, done("out1", 3))
            for h in range(4):
                for jb in range(TT):
                    i = 4 * h + jb
                    dve.wait_ge(sc_psum, i + 1)
                    dve.tensor_tensor(ra[:, i % 2, 0:SEQ - P * jb], bank[5][:, P * jb:SEQ],
                                      dec[:, h, 0:SEQ - P * jb], ALU.mult).then_inc(a_ready, 1)
                dve.wait_ge(mean_psum, h + 1)
                for e in range(2):
                    dve.scalar_tensor_tensor(out=oc[:, e, :], in0=bank[4][:, :], scalar=-1.0 / 256,
                                             in1=o32[:, e, :], op0=ALU.mult, op1=ALU.add).then_inc(oc_ready, 1)
                dve.wait_ge(oc_ready, 2 * h + 2)
                rstd_of(f"ret{h}")
                for e in range(2):
                    dve.scalar_tensor_tensor(out=on[:, 2 * h + e, :], in0=oc[:, e, :],
                                             scalar=v("ret_w", 2 * h + e), in1=rstd[:, :],
                                             op0=ALU.mult, op1=ALU.mult).then_inc(on_ready, 1)
                dve.wait_ge(on_ready, 2 * h + 2)
            gated("ret_g", 0, "ret_b")
            dve.wait_ge(x1_stored, 16)
            merge(0)
            copies("gla_q", gq)
            copies("gla_k", gk)
            copies_tm("gla_v", gv)
            ahead(G["gla_a"][0])
            dve.nop().then_inc(copied_dve, 2)
            dve.wait_ge(gla_loaded, 32)
            dve.wait_ge(group_done, done("merge0", 7))
            kv = 0
            for h in range(4):
                dve.wait_ge(gz_psum, h + 1)
                dve.tensor_scalar(la[:, :], bank[4][:, :], v("gla_b", h), None, ALU.add).then_inc(gz_ready, 1)
                dve.wait_ge(gsp_ready, h + 1)
                stt(la[:, :], la[:, :], 0.0, lb[:, :], ALU.min, ALU.subtract)
                ts(la[:, :], la[:, :], 1.0 / 16, -1.0, ALU.mult, ALU.max)
                dve.tensor_tensor_scan(lb[:, :], rst[:, :], la[:, :], 0.0, ALU.mult, ALU.add).then_inc(gb_ready, 1)
                dve.wait_ge(gexp_ready, 2 * h + 2)
                stt(gq[:, h, :], gq[:, h, :], float(P) ** -0.5, eb[:, :], ALU.mult, ALU.mult)
                tt(gk[:, h, :], gk[:, h, :], la[:, :], ALU.mult)
                chunks = "p (n c) -> p n c"
                dve.tensor_tensor(kd[:, :].rearrange(chunks, c=GLA_CHUNK),
                                  gk[:, h, :].rearrange(chunks, c=GLA_CHUNK),
                                  eb[:, :].rearrange(chunks, c=GLA_CHUNK)[:, :, GLA_CHUNK - 1:GLA_CHUNK]
                                  .to_broadcast([P, SEQ // GLA_CHUNK, GLA_CHUNK]), ALU.mult).then_inc(gkd_ready, 1)
                dve.wait_ge(sc_psum, 16 + h + 1)
                dve.tensor_tensor(am[:, :, :], bank[4][:, :].rearrange("p (t c) -> p t c", c=P),
                                  gla_mask[:, None, :].to_broadcast([P, TT, P]), ALU.mult).then_inc(a_ready, 1)
                for n in range(7):
                    dve.wait_ge(kv_psum, kv + 1)
                    if n == 0:
                        ins = dve.tensor_copy(st[:, 0, :], bank[4 + kv % 2][:, 0:256])
                    else:
                        last = (n + 1) * GLA_CHUNK - 1
                        ins = dve.scalar_tensor_tensor(out=st[:, n, :], in0=st[:, n - 1, :],
                                                       scalar=eb[:, last:last + 1], in1=bank[4 + kv % 2][:, 0:256],
                                                       op0=ALU.mult, op1=ALU.add)
                    ins.then_inc(kv_read, 1)
                    kv += 1
                    dve.wait_ge(kv_read, kv)
                rstd_of(f"gla{h}")
                for e in range(2):
                    dve.scalar_tensor_tensor(out=on[:, 2 * h + e, :], in0=sgb[:, e, :],
                                             scalar=v("gla_w", 2 * h + e), in1=rstd[:, :],
                                             op0=ALU.mult, op1=ALU.mult).then_inc(on_ready, 1)
                dve.wait_ge(on_ready, 8 + 2 * h + 2)
            gated("gla_g", 1)
            merge(1)
            ahead(G["swa_k"][0])
            gr = G["swa_v"][0]
            ahead(gr)
            for half in range(2):
                bk = pbanks(gr)[half]
                dve.wait_ge(group_done, 2 * gr.g + half + 1)
                for t in range(2):
                    settle(dve.tensor_copy(
                        svd[:, 2 * half + t, :, :].rearrange("p k (r c) -> p k r c", r=2),
                        bank[bk][:, t * WC:(t + 1) * WC].rearrange("p (k c) -> p k c", c=64)
                        [:, :, None, :].to_broadcast([P, 4, 2, 64])))
                dve.nop().then_inc(bank_free[bk], 1)
            copies("swa_q", sq, scale=0.125)
            dve.nop().then_inc(copied_dve, 2)

            def window_logits(n):
                kvh, qb = n // TT, n % TT
                w = P if qb == 0 else 2 * P
                c = 4 * n
                dve.wait_ge(lg_psum, 32 + n + 1)
                if n >= 2:
                    dve.wait_ge(pt_psum, PT_END[n - 2])
                for i in range(4):
                    slope = float(np.float32(2.0 ** (-8.0 * (4 * kvh + i + 1) / 16)))
                    dve.scalar_tensor_tensor(out=lg[:, n % 2, i, 0:w], in0=swa_dist[:, 256 - w:256], scalar=-slope,
                                             in1=bank[4 + i % 2][:, (i // 2) * 256:(i // 2) * 256 + w],
                                             op0=ALU.mult, op1=ALU.add).then_inc(lg_read, 1)
                dve.wait_ge(lg_read, 32 + 4 * n + 4)
                mx, nmx, dsink = sst[:, 0, c:c + 4], sst[:, 1, c:c + 4], sst[:, 3, c:c + 4]
                s0 = VEC["sinks"][0] + 4 * kvh
                settle(dve.tensor_reduce(mx, lg[:, n % 2, :, 0:w], AX.X, ALU.max))
                tt(mx, mx, vec[:, s0:s0 + 4], ALU.max)
                ts(nmx, mx, -1.0, None, ALU.mult)
                dve.tensor_tensor(dsink, vec[:, s0:s0 + 4], mx, ALU.subtract).then_inc(lg_ready, 1)

            def window_norm(n):
                w = P if n % TT == 0 else 2 * P
                c = 4 * n
                dve.wait_ge(p_exp, 32 + n + 1)
                tt(sst[:, 5, c:c + 4], sst[:, 2, c:c + 4], sst[:, 4, c:c + 4], ALU.add)
                settle(dve.reciprocal(sst[:, 6, c:c + 4], sst[:, 5, c:c + 4]))
                dve.tensor_tensor(lg[:, n % 2, :, 0:w], lg[:, n % 2, :, 0:w],
                                  sst[:, 6, c:c + 4][:, :, None].to_broadcast([P, 4, w]), ALU.mult)\
                   .then_inc(p_norm, 1)

            def window_out(n):
                kvh, qb = n // TT, n % TT
                dve.wait_ge(pv_psum, PT_END[n])
                o = bank[7][:, :].rearrange("p (m r q) -> p m r q", m=2, r=2)
                for r in range(2):
                    rows = slice(64 * r, 64 * r + 64)
                    settle(dve.tensor_copy(yb[rows, :, qb * P:qb * P + P], o[rows, :, r, :]))
                dve.nop().then_inc(pv_read, 1)
                if qb == TT - 1:
                    dve.nop().then_inc(act_val, 2)
                    for i in range(2):
                        m = 2 * kvh + i
                        low(AT["y2"] + m, y_lo[:, m, :], y_hi[:, m, :], yb[:, i, :])
                    dve.wait_ge(act_low, AT["y2"] + 2 * kvh + 2)

            window_logits(0)
            for n in range(16):
                if n + 1 < 16:
                    window_logits(n + 1)
                window_norm(n)
                if n:
                    window_out(n - 1)
            window_out(15)
            merge(2)
            for m in range(KT):
                dve.nop().then_inc(act_val, 1)
                low(AT["merged"] + m, h_lo[:, m, :], h_hi[:, m, :], merged[:, m, :])
            copies("out2", mo, signal=mo_ready)
            rstd_of("post1")
            dve.wait_ge(x1_back, 16)
            for m in range(KT):
                stt(sgb[:, m % 2, :], mo[:, m, :], v("norm_mix_post", m), rstd[:, :], ALU.mult, ALU.mult)
                dve.tensor_tensor(xr[:, m, :], xr[:, m, :], sgb[:, m % 2, :], ALU.add).then_inc(x2_ready, 1)
            dve.wait_ge(x2_ready, KT)
            norm("norm2", xr, lambda m: v("norm_ffn_pre", m))
            for i, gr in enumerate(G["ffn_up"]):
                ahead(gr)
                if i % 2 == 0:
                    continue
                for half in range(2):
                    m = i - 1 + half
                    bk = pbanks(gr)[half]
                    a = AT["f"] + m
                    t = new_val(a)
                    dve.wait_ge(sig_ready, SIG["ffn_up"] + m + 1)
                    dve.wait_ge(group_done, 2 * gr.g + half + 1)
                    dve.tensor_tensor(t, sgb[:, m % 2, :], bank[bk][:, :], ALU.mult).then_inc(act_val, 1)
                    dve.wait_ge(act_val, a + 1)
                    dve.nop().then_inc(bank_free[bk], 1)
                    dve.nop().then_inc(sig_used, 1)
                for half in range(2):
                    m = i - 1 + half
                    low(AT["f"] + m, f_lo[:, m, :], f_hi[:, m, :])
            copies("ffn_down", down, signal=dn_ready)
            rstd_of("post2")
            for m in range(KT):
                stt(sgb[:, m % 2, :], down[:, m, :], v("norm_ffn_post", m), rstd[:, :], ALU.mult, ALU.mult)
                dve.tensor_tensor(down[:, m, :], xr[:, m, :], sgb[:, m % 2, :], ALU.add).then_inc(out_ready, 1)


def shape_constants():
    q, s = np.arange(P)[:, None], np.arange(P)[None, :]
    k2 = np.arange(256)[None, :]
    dist = P + q - k2
    cst = np.concatenate([
        np.eye(P), np.where(s <= q, 0.0, NEG_MASKED),
        (s >= q) & (s // GLA_CHUNK == q // GLA_CHUNK),
        np.where((dist >= 0) & (dist < P), dist, 1e30),
        q // 64 == s // 64], axis=1).astype(np.float32)
    m = np.arange(BIAS_LEN)
    bucket = np.searchsorted(np.array(BUCKET_STARTS), np.maximum(SEQ - 1 - m, 0), side="right") - 1
    onehot = (np.arange(32)[:, None] == bucket[None, :]).astype(np.float32)
    log_g = np.log1p(-np.exp2(-5.0 - np.arange(4)))
    rel = np.arange(SEQ)[None, :] - np.arange(P)[:, None]
    decay = np.exp(np.maximum(rel, 0)[:, None, :] * log_g[None, :, None]) * (rel >= 0)[:, None, :] * P ** -0.5
    reset = np.broadcast_to((np.arange(SEQ) % GLA_CHUNK != 0), (P, SEQ)).astype(np.float32)
    return cst, onehot, decay.astype(np.float32), np.ascontiguousarray(reset)


def lay_out(inputs):
    a = {k: np.asarray(x) for k, x in inputs.items()}
    mats = {"w_ada": a["w_ada"][0], "w_in": a["w_in"][0], "w_glu": a["w_glu"][0], "w_out": a["w_out"][0],
            "w_in2": a["w_in_2"][0], "w_out2": a["w_out_2"][0], "w_gate": a["ffn_w_gate_2"][0],
            "w_up": a["ffn_w_up_2"][0], "w_down": a["ffn_w_down_2"][0]}
    for n in range(3):
        mats[f"w_branch{n}"] = a["w_branch_2"][0, n]
    ws = np.zeros((len(TILES), P, KT, WC), np.float32)
    for i, (name, row0, kt, cols) in enumerate(TILES):
        at = 0
        for c0, n in cols:
            ws[i, :, 0:kt, at:at + n] = mats[name][row0:row0 + kt * P, c0:c0 + n].reshape(kt, P, n).transpose(1, 0, 2)
            at += n

    def col(x):
        return x.reshape(-1, P).T

    vecs = np.concatenate([
        col(a["c"]), col(a["norm_g"]), col(a["b_ada"]), np.tile(a["q_gain"].reshape(64, 1), (2, 1)),
        np.tile(a["k_gain"].reshape(64, 1), (2, 1)), col(a["b_glu"]), col(a["norm_mix_pre_2"]),
        col(a["norm_mix_post_2"]), col(a["ret_norm_w_2"]), col(a["ret_norm_b_2"]),
        col(a["gla_b_alpha_2"]), col(a["gla_norm_w_2"]), col(a["norm_ffn_pre_2"]),
        col(a["norm_ffn_post_2"]), np.broadcast_to(a["attn_sinks_2"].reshape(1, 16), (P, 16))], axis=1)

    def states(x):
        x = x.reshape((PAIRS, 2) + x.shape[1:])
        return np.moveaxis(x, 0, 2).reshape((P, PAIRS) + x.shape[3:])

    log_dt = np.broadcast_to(a["log_dt"][0][:, None], (GROUPS, NSTATE))
    ssm_vec = np.stack([states(x) for x in (log_dt, a["a_re"][0], a["a_im"][0])], axis=1)
    ssm_b = np.stack([states(a["b_re"][0]), states(a["b_im"][0])])
    ssm_c = np.stack([states(a[n][0].transpose(0, 2, 1)) for n in ("c_re", "c_im")])
    cst, onehot, decay, reset = shape_constants()
    return {
        "wstream": ws.reshape(len(TILES), P, KT * WC),
        "xT": a["x"][0].T.reshape(KT, P, SEQ).transpose(1, 0, 2),
        "vecs": vecs, "consts": cst, "onehot": onehot, "rel_bias": a["rel_bias"],
        "ssm_vec": ssm_vec, "ssm_b": ssm_b, "ssm_c": ssm_c,
        "d_skip": a["d_skip"][0].reshape(GROUPS, GCH).T, "alpha2": a["gla_w_alpha2_2"][0],
        "decay": decay, "reset": reset,
    }


def kernel(**inputs):
    import concourse.bacc as bacc
    from concourse.bass_utils import run_bass_kernel_spmd

    nc = bacc.Bacc("TRN2", target_bir_lowering=False, num_devices=1)
    arrays = {n: np.ascontiguousarray(x) for n, x in lay_out(inputs).items()}
    args = [nc.dram_tensor(n, x.shape, mybir.dt.from_np(x.dtype), kind="ExternalInput").ap()
            for n, x in arrays.items()]
    outT = nc.dram_tensor("outT", (P, KT, SEQ), mybir.dt.float32, kind="ExternalOutput").ap()
    hybrid_blocks(nc, *args, outT)
    r = run_bass_kernel_spmd(nc, [arrays], core_ids=[0])
    got = np.asarray(r.results[0]["outT"])
    return np.ascontiguousarray(got.transpose(1, 0, 2).reshape(D, SEQ).T[None])
```

```python
from contextlib import ExitStack

import numpy as np

import concourse.bass as bass
from concourse import mybir

P = 128
SEQ = 512
D = 1024
KT = D // P
TT = SEQ // P
WC = 256
EPS_RMS = 1e-6
EPS_GN = 1e-5
GROUPS, GCH, NSTATE = 32, 16, 64
PAIRS = GROUPS // 2
STEPS = 8
CHUNKS = SEQ // STEPS
HEADS = 8
TOPK = 128
BUCKET_STARTS = [0, 1, 2, 3, 4, 5, 6, 7, 8, 9, 10, 11, 12, 13, 14, 15, 16, 19, 21, 24, 27, 31, 35,
                 40, 46, 52, 59, 67, 77, 87, 99, 113]
BIAS_LEN = 640
D_FF = 2816
FT = D_FF // P
NEG_MASKED, NEG_TAKEN, NEG_BETWEEN, NEG_LOGIT = -2e38, -3e38, -2.5e38, -1e30
GLA_CHUNK = 64

VEC_SIZES = [("c", 8), ("norm_g", 8), ("b_ada", 24), ("q_gain", 1), ("k_gain", 1), ("b_glu", 4),
             ("norm_mix_pre", 8), ("norm_mix_post", 8), ("ret_w", 8), ("ret_b", 8), ("gla_b", 4),
             ("gla_w", 8), ("norm_ffn_pre", 8), ("norm_ffn_post", 8), ("sinks", 16)]
VEC = {}
_at = 0
for _name, _n in VEC_SIZES:
    VEC[_name] = (_at, _at + _n)
    _at += _n
VECS = _at

def _cols(name, c0, n, kt=KT, row0=0):
    return [(name, row0, kt, [(c0 + i * WC, WC)]) for i in range(n // WC)]

KV2 = 7184
STAGES = [
    ("ada_shift_scale", _cols("w_ada", 0, 2048)),
    ("ssm_u", _cols("w_in", 0, 512)),
    ("ssm_z", _cols("w_in", 512, 512)),
    ("glu", _cols("w_glu", 0, 512, kt=4)),
    ("q_idx", _cols("w_in", 3072, 512)),
    ("k_idx", [("w_in", 0, KT, [(3584, 64), (3584, 64), (3648, 8)])]),
    ("q", _cols("w_in", 1024, 512)),
    ("ada_gate0", _cols("w_ada", 2048, WC)),
    ("k", _cols("w_in", 1536, 512)),
    ("ada_gate1", _cols("w_ada", 2048 + WC, WC)),
    ("v", _cols("w_in", 2048, 512)),
    ("ada_gate2", _cols("w_ada", 2048 + 2 * WC, WC)),
    ("attn_z", _cols("w_in", 2560, 512)),
    ("ada_gate3", _cols("w_ada", 2048 + 3 * WC, WC)),
    ("out1", _cols("w_out", 0, 1024)),
    ("ret_q", _cols("w_in2", 0, 512)),
    ("ret_k", _cols("w_in2", 512, 512)),
    ("ret_v", _cols("w_in2", 1024, 1024)),
    ("ret_g", _cols("w_in2", 2048, 1024)),
    ("merge0", [t for p in range(4) for t in _cols("w_in2", 7696 + p * WC, WC)
                + _cols("w_branch0", p * WC, WC)]),
    ("gla_q", _cols("w_in2", 3072, 512)),
    ("gla_k", _cols("w_in2", 3584, 512)),
    ("gla_a", [("w_in2", 0, KT, [(6144, 16)])]),
    ("gla_v", _cols("w_in2", 4096, 1024)),
    ("gla_g", _cols("w_in2", 5120, 1024)),
    ("merge1", [t for p in range(4) for t in _cols("w_in2", 8720 + p * WC, WC)
                + _cols("w_branch1", p * WC, WC)]),
    ("swa_k", _cols("w_in2", KV2, 256)),
    ("swa_v", _cols("w_in2", KV2 + 256, 256)),
    ("swa_q", _cols("w_in2", 6160, 1024)),
    ("merge2", [t for p in range(4) for t in _cols("w_in2", 9744 + p * WC, WC)
                + _cols("w_branch2", p * WC, WC)]),
    ("out2", _cols("w_out2", 0, 1024)),
    ("ffn_up", [t for p in range(D_FF // WC) for t in _cols("w_gate", p * WC, WC)
                + _cols("w_up", p * WC, WC)]),
    ("ffn_down", [("w_down", k * D, min(KT, FT - k * KT), [(c * WC, WC)])
                  for c in range(4) for k in range(3)]),
]
RAW_STAGES = ("ada_shift_scale", "ada_gate0", "ada_gate1", "ada_gate2", "ada_gate3")
TILES = [t for _, ts in STAGES for t in ts]
TILES_PER_GROUP = {"ffn_down": 3}
RAW_SLOTS = 2

ACT_TILES = [("norm0", 8), ("z", 4), ("y_ssm", 4), ("y_attn", 4), ("norm1", 8), ("y0", 8),
             ("y1", 8), ("y2", 8), ("merged", 8), ("norm2", 8), ("f", FT)]
AT = {}
_at = 0
for _name, _n in ACT_TILES:
    AT[_name] = _at
    _at += _n


class Group:

    def __init__(self, index, kts, split0):
        self.g = index
        self.kts = kts
        self.s = split0


def plan():
    groups, tiles = {}, []
    g = s = raw = 0
    for name, ts in STAGES:
        groups[name] = []
        if name in RAW_STAGES:
            for t in ts:
                tiles.append(("raw", raw, t))
                groups[name].append((len(tiles) - 1, raw))
                raw += 1
            continue
        per = TILES_PER_GROUP.get(name, 1)
        for i in range(0, len(ts), per):
            groups[name].append(Group(g, [t[2] for t in ts[i:i + per]], s))
            for t in ts[i:i + per]:
                tiles.append(("split", s, t))
                s += 1
            g += 1
    return groups, tiles


def hybrid_blocks(nc, wstream, xT, vecs, consts, onehot, rel_bias, ssm_vec, ssm_b, ssm_c, d_skip,
                  alpha2, decay, reset, outT):
    f32, f32r, i32 = mybir.dt.float32, mybir.dt.float32r, mybir.dt.int32
    ALU, ACT, AX = mybir.AluOpType, mybir.ActivationFunctionType, mybir.AxisListType
    G, STREAM = plan()
    SPLIT_TILES = sum(kind == "split" for kind, _, _ in STREAM)
    SPLIT_AT = [i for i, (kind, _, _) in enumerate(STREAM) if kind == "split"]

    bias_dram = nc.dram_tensor("bias_table", (HEADS, BIAS_LEN), f32, kind="Internal")
    bias_rows = nc.dram_tensor("bias_rows", (P, HEADS * BIAS_LEN), f32, kind="Internal")
    x1_dram = nc.dram_tensor("x1_saved", (P, KT * SEQ), f32, kind="Internal").ap()

    ctx = ExitStack()
    with ctx:
        def sb(name, shape, dt=f32):
            return ctx.enter_context(nc.sbuf_tensor(name, shape, dt))

        def views(hold, *sets):
            made = []
            for tensors in sets:
                with ExitStack() as phase:
                    made.append([phase.enter_context(nc.sbuf_tensor(n, s, dt)) for n, s, dt in tensors])
            for n, s, dt in hold:
                ctx.enter_context(nc.sbuf_tensor(n, s, dt))
            return made

        def sem(name):
            return ctx.enter_context(nc.semaphore(name))

        vec = sb("vec", [P, VECS])
        cst = sb("cst", [P, 768])
        ident = cst[:, 0:128]
        causal = cst[:, 128:256]
        gla_mask = cst[:, 256:384]
        swa_dist = cst[:, 384:640]
        head_ones = cst[:, 640:768]
        ones = sb("ones", [P, P])
        eps = sb("eps", [P, 2])
        modv = sb("modv", [P, 24])
        gs = sb("gs", [P, 8])
        silu_c = sb("silu_c", [P, 8])
        qg = sb("qg", [P, 1])
        rho = sb("rho", [P, PAIRS])
        small = sb("small", [P, 64])

        w_raw = sb("w_raw", [P, RAW_SLOTS, KT, WC])
        w_hi = sb("w_hi", [P, 2, KT, WC], f32r)
        w_lo = sb("w_lo", [P, 2, KT, WC], f32r)
        tval = sb("tval", [P, 2, SEQ])
        sqb = sb("sqb", [P, 2, SEQ])
        sgb = sb("sgb", [P, 2, SEQ])
        root = sb("root", [P, SEQ])
        rstd = sb("rstd", [P, SEQ])

        ((h_hi, h_lo), (win_re, win_im, sv, b_re, b_im, c_re, c_im, bb_re, bb_im, pw_re, pw_im,
                        tmp, btab), (down,)) = views(
            [("room_h", [P, 2 * KT * SEQ], f32)],
            [("h_hi", [P, KT, SEQ], f32r), ("h_lo", [P, KT, SEQ], f32r)],
            [("win_re", [P, PAIRS, P], f32), ("win_im", [P, PAIRS, P], f32),
             ("sv", [P, 24, PAIRS], f32)] +
            [(n, [P, PAIRS, GCH], f32) for n in ("b_re", "b_im", "c_re", "c_im", "bb_re", "bb_im")] +
            [(n, [P, STEPS + 1, PAIRS], f32) for n in ("pw_re", "pw_im")] +
            [("tmp", [P, 1152], f32), ("btab", [HEADS, BIAS_LEN], f32)],
            [("down", [P, KT, SEQ], f32)])
        ((xr,), (xa, xb, ga_, gb_), (bias,), (merged,)) = views(
            [("room_x", [P, KT * SEQ], f32)],
            [("xr", [P, KT, SEQ], f32)],
            [(n, [P, PAIRS, CHUNKS], f32) for n in ("xa", "xb", "ga_", "gb_")],
            [("bias", [P, HEADS, SEQ], f32)],
            [("merged", [P, KT, SEQ], f32)])
        A = [
            [("y_hi", [P, KT, SEQ], f32r), ("y_lo", [P, KT, SEQ], f32r)],
            [("toep", [P, GROUPS, P], f32), ("wint_re", [P, PAIRS, P], f32),
             ("wint_im", [P, PAIRS, P], f32)],
            [("pad_on", [P, KT, SEQ], f32), ("on", [P, KT, SEQ], f32)],
            [("f_hi", [P, FT, SEQ], f32r), ("f_lo", [P, FT, SEQ], f32r)],
        ]
        pad = ("pad", [P, 2 * KT * SEQ], f32)

        def arena(*t):
            A.append([(pad[0] + str(len(A)), pad[1], pad[2])] + list(t))

        arena(("sz", [P, 4, SEQ], f32), ("ut", [P, GROUPS, CHUNKS], f32),
              ("cl_re", [P, PAIRS, 2, (STEPS + 1) * GCH], f32),
              ("cl_im", [P, PAIRS, 2, (STEPS + 1) * GCH], f32), ("sin_t", [P, PAIRS, CHUNKS], f32))
        arena(("strip", [GCH, GROUPS, P], f32))
        arena(("q32", [P, 4, SEQ], f32), ("k32", [P, 4, SEQ], f32), ("v32", [P, TT, SEQ], f32),
              ("qi", [P, 4, SEQ], f32), ("score", [P, TT, SEQ], f32), ("az", [P, 4, SEQ], f32),
              ("ki", [P, SEQ], f32), ("pT", [P, 2, TT, P], f32), ("wi", [P, TT, HEADS], f32),
              ("stat", [P, 4, 32], f32))
        arena(("rq", [P, 4, SEQ], f32), ("rk", [P, 4, SEQ], f32), ("rv", [P, TT, D], f32),
              ("ra", [P, 4, SEQ], f32), ("dec", [P, 4, SEQ], f32), ("o32", [P, 2, SEQ], f32),
              ("oc", [P, 2, SEQ], f32))
        gla_kept = [("gq", [P, 4, SEQ], f32), ("gk", [P, 4, SEQ], f32), ("gv", [P, TT, D], f32),
                    ("kdT", [P, 4 * TT, P], f32), ("ebl", [P, 4, SEQ // GLA_CHUNK], f32)]
        arena(*gla_kept, ("la", [P, SEQ], f32), ("lb", [P, SEQ], f32), ("eb", [P, SEQ], f32),
              ("kd", [P, SEQ], f32), ("ga", [GCH, SEQ], f32), ("al2", [GCH, SEQ], f32),
              ("rst", [P, SEQ], f32))
        arena(("sq", [P, KT, SEQ], f32), ("sk", [P, 4, SEQ], f32), ("svd", [P, TT, 4, P], f32),
              ("lg", [P, 3, 4, 256], f32), ("spT", [P, 4, SEQ], f32), ("yb", [P, 2, SEQ], f32),
              ("sst", [P, 8, 64], f32))
        arena(("mo", [P, KT, SEQ], f32),)
        arena(("u4", [P, GROUPS, STEPS // 2, GCH], f32))
        A.append([("pad_u", [P, GROUPS, P], f32), ("u", [64, STEPS, GROUPS * GCH], f32)])
        arena(("pad_sz", [P, 4, SEQ], f32), ("z32", [P, 4, SEQ], f32))
        arena(("gla_pad", [P, 2 * 4 * SEQ + TT * D + 4 * SEQ + 32], f32), ("am", [P, TT, P], f32),
              ("st", [P, 7, 256], f32), ("og", [P, 2, SEQ], f32))
        made = views([("room_f", [P, 23040], f32)], *A)
        (y_hi, y_lo), (toep, wint_re, wint_im), (_, on), (f_hi, f_lo) = made[0:4]
        _, sz, ut, cl_re, cl_im, sin_t = made[4]
        _, strip = made[5]
        z32 = made[13][2]
        u = made[12][1]
        cos_t = sgb[:, :, :].rearrange("p a (j k) -> p (a j) k", k=CHUNKS)
        u4 = made[11][1]
        _, q32, k32, v32, qi, score, az, ki, pT, wi, stat = made[6]
        _, rq, rk, rv, ra, dec, o32, oc = made[7]
        _, gq, gk, gv, kdT, ebl, la, lb, eb, kd, ga, al2, rst = made[8]
        _, _, am, st, og = made[14]
        _, sq, sk, svd, lg, spT, yb, sst = made[9]
        _, mo = made[10]
        flat = tval[:, :, :].rearrange("p a n -> p (a n)")
        oh, rb, dsk = flat[0:32, 0:BIAS_LEN], flat[0:32, 640:640 + HEADS], small[0:GCH, 32:32 + GROUPS]

        bank = [ctx.enter_context(nc.psum_tensor(f"bank{i}", [P, SEQ], f32)) for i in range(8)]

        raw_loaded = [sem(f"raw_loaded{i}") for i in range(RAW_SLOTS)]
        raw_used = sem("raw_used")
        w_high = sem("w_high")
        w_low = sem("w_low")
        w_used = sem("w_used")
        group_done = sem("group_done")
        bank_free = [sem(f"bank_free{i}") for i in range(4)]
        act_val, act_high, act_low = sem("act_val"), sem("act_high"), sem("act_low")
        sq_ready, sq_used = sem("sq_ready"), sem("sq_used")
        root_ready, rstd_ready = sem("root_ready"), sem("rstd_ready")
        dve_step, act_step, pool_step = sem("dve_step"), sem("act_step"), sem("pool_step")
        in_small, in_x, in_ssm, consts_set = sem("in_small"), sem("in_x"), sem("in_ssm"), sem("consts_set")
        cl_zero, bias_spread = sem("cl_zero"), sem("bias_spread")
        c_ready, ada_done, mod_ready = sem("c_ready"), sem("ada_done"), sem("mod_ready")
        setup_trig, trig_ready = sem("setup_trig"), sem("trig_ready")
        win_ready, wint_psum, wint_act, wint_dve = sem("win_ready"), sem("wint_psum"), sem("wint_act"), sem("wint_dve")
        cl_ready, strip_psum, strip_act, strip_dve = sem("cl_ready"), sem("strip_psum"), sem("strip_act"), sem("strip_dve")
        strip_ready, toep_zero, toep_loaded = sem("strip_ready"), sem("toep_zero"), sem("toep_loaded")
        bias_psum, bias_copied, bias_stored, bias_loaded = sem("bias_psum"), sem("bias_copied"), sem("bias_stored"), sem("bias_loaded")
        u_act, u_dve, ut_psum, ut_act, ut_dve = sem("u_act"), sem("u_dve"), sem("ut_psum"), sem("ut_act"), sem("ut_dve")
        x_psum, state_ready, y_psum, y_act, y_dve = sem("x_psum"), sem("state_ready"), sem("y_psum"), sem("y_act"), sem("y_dve")
        zt_psum, z_ready, sig_ready, sig_used = sem("zt_psum"), sem("z_ready"), sem("sig_ready"), sem("sig_used")
        copied_act, copied_dve = sem("copied_act"), sem("copied_dve")
        rel_psum, relu_ready, rel_used = sem("rel_psum"), sem("relu_ready"), sem("rel_used")
        lg_psum, lg_ready, p_exp, p_norm = sem("lg_psum"), sem("lg_ready"), sem("p_exp"), sem("p_norm")
        lg_read, pt_psum, pt_ready, pv_psum, pv_read = sem("lg_read"), sem("pt_psum"), sem("pt_ready"), sem("pv_psum"), sem("pv_read")
        x_reload, x1_done, x1_stored, x1_back = sem("x_reload"), sem("x1_done"), sem("x1_stored"), sem("x1_back")
        sc_psum, a_ready, o_psum, o_copied = sem("sc_psum"), sem("a_ready"), sem("o_psum"), sem("o_copied")
        mean_psum, oc_ready, on_ready, dec_loaded = sem("mean_psum"), sem("oc_ready"), sem("on_ready"), sem("dec_loaded")
        gz_psum, gz_ready, gsp_ready, gb_ready, gexp_ready = sem("gz_psum"), sem("gz_ready"), sem("gsp_ready"), sem("gb_ready"), sem("gexp_ready")
        gkd_ready, gkdT_psum, gkdT_ready, gla_loaded = sem("gkd_ready"), sem("gkdT_psum"), sem("gkdT_ready"), sem("gla_loaded")
        kv_psum, kv_read = sem("kv_psum"), sem("kv_read")
        merged_ready, mo_ready, x2_ready, dn_ready = sem("merged_ready"), sem("mo_ready"), sem("x2_ready"), sem("dn_ready")
        y_tile, out_ready, out_stored = sem("y_tile"), sem("out_ready"), sem("out_stored")
        block = ctx.enter_context(nc.Block())

        STATS = ["norm0"] + [f"qk{i}" for i in range(8)] + ["norm1"] + \
            [f"ret{h}" for h in range(4)] + [f"gla{h}" for h in range(4)] + ["post1", "norm2", "post2"]
        sizes = {"norm0": 8, "norm1": 8, "norm2": 8, "post1": 8, "post2": 8}
        sizes.update({f"qk{i}": 1 for i in range(8)})
        sizes.update({f"{b}{h}": 2 for b in ("ret", "gla") for h in range(4)})
        SQ0, ROOT = {}, {}
        for i, name in enumerate(STATS):
            SQ0[name] = sum(sizes[n] for n in STATS[:i])
            ROOT[name] = i

        def v(name, m):
            a, _ = VEC[name]
            return vec[:, a + m:a + m + 1]

        def done(name, i, b=2):
            return 2 * G[name][i].g + b

        def pbanks(gr):
            return 2 * (gr.g % 2), 2 * (gr.g % 2) + 1

        def all_groups():
            for name, _ in STAGES:
                if name not in RAW_STAGES:
                    for gr in G[name]:
                        yield gr

        def tile_used(s):
            inner = 0
            for gr in all_groups():
                n = len(gr.kts)
                if gr.s + n - 1 == s:
                    return group_done, 2 * gr.g + 2
                if gr.s <= s:
                    if s < gr.s + n - 1:
                        return w_used, inner + s - gr.s + 1
                inner += n - 1

        LG_BANKS, PT_BANKS, PV_BANKS = (4, 5, 0), (6, 1), (7, 2)
        SC_BANKS, O_BANKS = (5, 0, 1), ((6, 7), (2, 3))

        def kv_tile(n):
            return bank[2 * (n % 2) + n // 4][:, (n // 2 % 2) * 256:(n // 2 % 2) * 256 + 256]

        SL_BANKS, ST_BANKS, SV_BANKS = ((4, 5), (0, 1)), (6, 2), (7, 3)

        def prob(i, qt):
            return (sgb, sqb)[i % 4 // 2][:, i % 2, 0:P * (qt + 1)]

        SIG, n_sig = {}, 0
        for name, n in (("glu", 4), ("ret_g", 8), ("merge0", 8), ("gla_g", 8), ("merge1", 8),
                        ("merge2", 8), ("ffn_up", FT)):
            SIG[name] = n_sig
            n_sig += n
        PT_END = [32 + sum(1 if m % TT == 0 else 2 for m in range(n + 1)) for n in range(16)]

        @block.sync
        def _(sp):
            for t, src in ((vec[:, :], vecs), (cst[:, :], consts), (oh[:, :], onehot),
                           (rb[:, :], rel_bias), (dsk[:, :], d_skip)):
                sp.dma_start(t, src).then_inc(in_small, 16)
            for t, src in ((sv[:, 0:3, :], ssm_vec), (b_re[:, :, :], ssm_b[0]), (b_im[:, :, :], ssm_b[1]),
                           (c_re[:, :, :], ssm_c[0]), (c_im[:, :, :], ssm_c[1])):
                sp.dma_start(t, src).then_inc(in_ssm, 16)
            sp.dma_start(xr[:, :, :], xT).then_inc(in_x, 16)

            def aside(i):
                kind, n, _ = STREAM[i]
                if i == 10:
                    sp.wait_ge(strip_ready, 1)
                    sp.wait_ge(toep_zero, 1)
                    for s in range(STEPS):
                        r = (STEPS - 1 - s) * GCH
                        sp.dma_start(toep[r:r + GCH, :, s * GCH:P],
                                     strip[:, :, 0:P - s * GCH]).then_inc(toep_loaded, 16)

            for i, (kind, n, (_, _, kt, _)) in enumerate(STREAM):
                aside(i)
                if kind == "split" and n == G["out1"][1].s:
                    sp.wait_ge(lg_ready, 32)
                    sp.dma_start(xr[:, :, :], xT).then_inc(x_reload, 16)
                if i >= RAW_SLOTS:
                    was, k, _ = STREAM[i - RAW_SLOTS]
                    if was == "split":
                        sp.wait_ge(w_low, k + 1)
                    else:
                        sp.wait_ge(raw_used, k + 1)
                sp.dma_start(w_raw[:, i % RAW_SLOTS, 0:kt, :],
                             wstream[i][:, 0:kt * WC].rearrange("p (t c) -> p t c", c=WC)
                             ).then_inc(raw_loaded[i % RAW_SLOTS], 16)
            sp.wait_ge(toep_loaded, 16 * STEPS)
            sp.wait_ge(x1_stored, 16)
            for m in range(KT):
                sp.wait_ge(out_ready, m + 1)
                sp.dma_start(outT[:, m, :], down[:, m, :]).then_inc(out_stored, 16)
            sp.wait_ge(out_stored, 16 * KT)

        @block.gpsimd
        def _(pool):
            pool.memset(ones[:, :], 1.0).then_inc(consts_set, 1)
            pool.memset(eps[:, 0:1], EPS_RMS).then_inc(consts_set, 1)
            pool.memset(eps[:, 1:2], EPS_GN).then_inc(consts_set, 1)
            pool.memset(cl_re[:, :, :, :], 0.0).then_inc(cl_zero, 1)
            pool.memset(cl_im[:, :, :, :], 0.0).then_inc(cl_zero, 1)
            pool.memset(toep[:, :, :], 0.0).then_inc(toep_zero, 1)
            pool.wait_ge(bias_copied, 1)
            pool.dma_start(bias_dram.ap(), btab[:, :]).then_inc(bias_stored, 16)
            pool.wait_ge(bias_stored, 16)
            pool.dma_start(bias_rows.ap(), bass.AP(bias_dram, 0, [[0, P], [1, HEADS * BIAS_LEN]])
                           ).then_inc(bias_spread, 16)
            pool.wait_ge(bias_spread, 16)
            pool.wait_ge(y_psum, 8)
            pool.dma_start(bias[:, :, :], bass.AP(
                bias_rows, P - 1, [[HEADS * BIAS_LEN - 1, P], [BIAS_LEN, HEADS], [1, SEQ]])
                           ).then_inc(bias_loaded, 16)
            for h in range(4):
                if h == 0:
                    pool.wait_ge(pv_read, 4)
                    pool.wait_ge(act_low, AT["y_attn"] + 4)
                    pool.dma_start(dec[:, :, :], decay).then_inc(dec_loaded, 16)
            pool.wait_ge(x1_done, KT)
            pool.dma_start(x1_dram, xr[:, :, :].rearrange("p t n -> p (t n)")).then_inc(x1_stored, 16)
            pool.wait_ge(on_ready, 8)
            pool.wait_ge(o_psum, 8)
            pool.dma_start(rst[:, :], reset).then_inc(gla_loaded, 16)
            pool.dma_start(al2[:, :], alpha2).then_inc(gla_loaded, 16)
            pool.wait_ge(x1_stored, 16)
            pool.wait_ge(act_low, AT["merged"] + 8)
            pool.dma_start(xr[:, :, :].rearrange("p t n -> p (t n)"), x1_dram).then_inc(x1_back, 16)
            pool.wait_ge(x1_back, 16)

        @block.tensor
        def _(pe):
            def mm(out, lhsT, rhs, start, stop):
                return pe.matmul(out, lhsT, rhs, start=start, stop=stop)

            def gemm(gr, kind, hi, lo, k0=0, cols=WC, permuted=False, need=None, between=None):
                b = pbanks(gr)
                if gr.g >= 2:
                    for x in b:
                        pe.wait_ge(bank_free[x], gr.g // 2)
                n_tiles = len(gr.kts)
                k_all = sum(gr.kts)
                k_at = 0
                for j, kt in enumerate(gr.kts):
                    s = gr.s + j
                    pe.wait_ge(w_low, s + 1)
                    wh, wl = w_hi[:, s % 2], w_lo[:, s % 2]
                    for half in range(2):
                        if kind == "fm":
                            c = slice(half * P, half * P + P)
                            out = bank[b[half]][:, :]
                            for k in range(kt):
                                a = k0 + k_at + k
                                if need is not None and half == 0:
                                    pe.wait_ge(act_low, need + k_at + k + 1)
                                first, last = k_at + k == 0, k_at + k == k_all - 1
                                mm(out, wh[:, k, c], hi[:, a, :], first, False)
                                mm(out, wh[:, k, c], lo[:, a, :], False, False)
                                ins = mm(out, wl[:, k, c], hi[:, a, :], False, last)
                        else:
                            for t in (2 * half, 2 * half + 1):
                                out = bank[b[half]][:, (t % 2) * WC:(t % 2) * WC + cols]
                                for k in range(kt):
                                    a = k0 + k
                                    if need is not None and t == 0:
                                        pe.wait_ge(act_low, need + k + 1)
                                    if permuted:
                                        ah, al = (x[:, a, t:SEQ:4] for x in (hi, lo))
                                    else:
                                        ah, al = (x[:, a, t * P:t * P + P] for x in (hi, lo))
                                    mm(out, ah, wh[:, k, 0:cols], k == 0, False)
                                    mm(out, ah, wl[:, k, 0:cols], False, False)
                                    ins = mm(out, al, wh[:, k, 0:cols], False, k == kt - 1)
                        if j == n_tiles - 1:
                            ins.then_inc(group_done, 1)
                        elif half == 1:
                            ins.then_inc(w_used, 1)
                        if between is not None and half == 0:
                            between()
                    k_at += kt

            def all_banks(gr):
                for x in range(4):
                    last = gr.g if x // 2 == gr.g % 2 else gr.g - 1
                    pe.wait_ge(bank_free[x], last // 2 + 1)

            def ada(name, m0):
                for i, (tile, raw) in enumerate(G[name]):
                    pe.wait_ge(raw_loaded[tile % RAW_SLOTS], 16 * (tile // RAW_SLOTS + 1))
                    for half in range(2):
                        m = m0 + 2 * i + half
                        for k in range(KT):
                            ins = mm(bank[7][:, m:m + 1],
                                     w_raw[:, tile % RAW_SLOTS, k, half * P:half * P + P],
                                     silu_c[:, k:k + 1], k == 0, k == KT - 1)
                    ins.then_inc(raw_used, 1)

            def ada_complete(name):
                pe.wait_ge(raw_used, G[name][-1][1] + 1)
                pe.nop().then_inc(ada_done, 1)

            def stats(name, lhsT):
                stats_of(name, lhsT, 0, sizes[name])

            def stats_of(name, lhsT, m0, m1):
                n, s0, r = sizes[name], SQ0[name], ROOT[name]
                if r and m0 == 0:
                    pe.wait_ge(root_ready, r)
                for m in range(m0, m1):
                    pe.wait_ge(sq_ready, s0 + m + 1)
                    mm(bank[4][:, :], lhsT, sqb[:, (s0 + m) % 2, :], m == 0, m == n - 1).then_inc(sq_used, 1)

            pe.wait_ge(in_small, 80)
            pe.wait_ge(consts_set, 3)
            mm(bank[4][0:HEADS, 0:320], rb[:, :], oh[:, 0:320], True, True)
            mm(bank[5][0:HEADS, 0:320], rb[:, :], oh[:, 320:640], True, True).then_inc(bias_psum, 1)
            pe.wait_ge(c_ready, 1)
            ada("ada_shift_scale", 0)
            ada_complete("ada_shift_scale")
            pe.wait_ge(win_ready, 1)
            pe.wait_ge(bias_copied, 1)
            for b in range(8):
                src = (win_re, win_im)[b // 4]
                if b >= 2:
                    pe.wait_ge(wint_act if b % 2 == 0 else wint_dve, b // 2)
                for i in range(4):
                    ins = pe.transpose(bank[4 + b % 2][:, i * P:i * P + P],
                                       src[:, 4 * (b % 4) + i, :], ident)
                ins.then_inc(wint_psum, 1)
            pe.wait_ge(cl_ready, 1)
            pe.wait_ge(wint_act, 4)
            pe.wait_ge(wint_dve, 4)
            for b in range(8):
                if b >= 2:
                    pe.wait_ge(strip_act if b % 2 == 0 else strip_dve, b // 2)
                for i in range(2):
                    j = 2 * b + i
                    out = bank[4 + b % 2][0:GCH, i * 2 * P:(i + 1) * 2 * P]
                    mm(out, bb_re[:, j, :], cl_re[:, j, :, 0:P], True, False)
                    ins = mm(out, bb_im[:, j, :], cl_im[:, j, :, 0:P], False, True)
                ins.then_inc(strip_psum, 1)
            pe.wait_ge(strip_act, 4)
            pe.wait_ge(strip_dve, 4)

            stats("norm0", ones[:, :])
            for gr in G["ssm_u"]:
                gemm(gr, "tm", h_hi, h_lo, permuted=True, need=AT["norm0"])
            pe.wait_ge(u_act, 4)
            pe.wait_ge(u_dve, 4)
            pe.wait_ge(root_ready, 1)
            pe.wait_ge(mod_ready, 1)
            for b in range(8):
                if b >= 4:
                    pe.wait_ge(ut_act if b % 2 == 0 else ut_dve, (b - 4) // 2 + 1)
                for i in range(4):
                    ins = pe.transpose(bank[4 + b % 4][0:64, i * P:i * P + P], u4[:, 4 * b + i, :, :], ident)
                ins.then_inc(ut_psum, 1)
            pe.wait_ge(ut_act, 4)
            pe.wait_ge(ut_dve, 4)
            for half in range(2):
                for w, bk in ((wint_re, 4 + half), (wint_im, 6 + half)):
                    for j in range(8 * half, 8 * half + 8):
                        for gp in range(2):
                            ins = mm(bank[bk][gp * 64:gp * 64 + 64, (j % 8) * CHUNKS:(j % 8 + 1) * CHUNKS],
                                     w[:, j, gp * 64:gp * 64 + 64], ut[:, 2 * j + gp, :], True, True)
                    ins.then_inc(x_psum, 1)
            for gr in G["ssm_z"]:
                gemm(gr, "fm", h_hi, h_lo)
            pe.wait_ge(state_ready, 1)
            pe.wait_ge(toep_loaded, 16 * STEPS)
            for b in range(8):
                if b >= 4:
                    pe.wait_ge(y_act if b % 2 == 0 else y_dve, (b - 4) // 2 + 1)
                for i in range(2):
                    j = 2 * b + i
                    c = i * 2 * P
                    out = bank[4 + b % 4][0:64, c:c + 2 * P]
                    mm(out, ga_[:, j, :], cl_re[:, j, :, GCH:GCH + P], True, False)
                    mm(out, gb_[:, j, :], cl_im[:, j, :, GCH:GCH + P], False, False)
                    mm(out[:, 0:P], ut[:, 2 * j, :], toep[:, 2 * j, :], False, False)
                    ins = mm(out[:, P:2 * P], ut[:, 2 * j + 1, :], toep[:, 2 * j + 1, :], False, True)
                ins.then_inc(y_psum, 1)
            pe.wait_ge(y_act, 4)
            pe.wait_ge(y_dve, 4)
            for ct in range(4):
                for t in range(STEPS):
                    ins = pe.transpose(bank[4 + ct][:, t * CHUNKS:(t + 1) * CHUNKS],
                                       u[:, t, ct * P:ct * P + P], ident[0:64, 0:64])
                ins.then_inc(zt_psum, 1)
            for gr in G["glu"]:
                gemm(gr, "fm", y_hi, y_lo, k0=4, need=AT["z"])
            for gr in G["q_idx"]:
                gemm(gr, "fm", h_hi, h_lo)
            gr = G["k_idx"][0]
            b = pbanks(gr)
            for x in b:
                pe.wait_ge(bank_free[x], gr.g // 2)
            pe.wait_ge(w_low, gr.s + 1)
            wh, wl = w_hi[:, gr.s % 2], w_lo[:, gr.s % 2]
            for k in range(KT):
                mm(bank[b[0]][:, :], wh[:, k, 0:P], h_hi[:, k, :], k == 0, False)
                mm(bank[b[0]][:, :], wh[:, k, 0:P], h_lo[:, k, :], False, False)
                ins = mm(bank[b[0]][:, :], wl[:, k, 0:P], h_hi[:, k, :], False, k == KT - 1)
            ins.then_inc(group_done, 1)
            for t in range(TT):
                out = bank[b[1]][:, t * HEADS:(t + 1) * HEADS]
                for k in range(KT):
                    ah, al = h_hi[:, k, t * P:t * P + P], h_lo[:, k, t * P:t * P + P]
                    mm(out, ah, wh[:, k, P:P + HEADS], k == 0, False)
                    mm(out, ah, wl[:, k, P:P + HEADS], False, False)
                    ins = mm(out, al, wh[:, k, P:P + HEADS], False, k == KT - 1)
            ins.then_inc(group_done, 1)
            pe.wait_ge(copied_act, 1)
            pe.wait_ge(copied_dve, 1)
            for i in range(32):
                qt, h = i // 8, i % 8
                hp = slice((h % 2) * 64, (h % 2) * 64 + 64)
                if i >= 3:
                    pe.wait_ge(relu_ready, i - 2)
                mm(bank[5 + i % 3][:, 0:P * (qt + 1)], qi[hp, h // 2, qt * P:qt * P + P],
                   ki[hp, 0:P * (qt + 1)], True, True).then_inc(rel_psum, 1)
            for w, gr in enumerate(G["q"] + G["k"] + G["v"][0:1]):
                gemm(gr, "fm" if w < 4 else "tm", h_hi, h_lo,
                     between=(lambda w=w: stats(f"qk{2 * w - 2}", head_ones)) if w else None)
                if w:
                    stats(f"qk{2 * w - 1}", head_ones)
                if w == 1:
                    pe.wait_ge(relu_ready, 32)
                    ada("ada_gate0", 16)
                if w == 3:
                    ada("ada_gate1", 18)
            gemm(G["v"][1], "tm", h_hi, h_lo)
            ada("ada_gate2", 20)
            for gr in G["attn_z"]:
                gemm(gr, "fm", h_hi, h_lo)
            ada("ada_gate3", 22)
            ada_complete("ada_gate3")
            pe.wait_ge(mod_ready, 2)
            pe.wait_ge(copied_act, 3)
            pe.wait_ge(copied_dve, 3)
            pe.wait_ge(root_ready, ROOT["qk7"] + 1)

            all_banks(G["attn_z"][-1])

            def logits(i):
                h, qt = i // TT, i % TT
                hp = slice((h % 2) * 64, (h % 2) * 64 + 64)
                if i >= 3:
                    pe.wait_ge(lg_read, i - 2)
                mm(bank[LG_BANKS[i % 3]][:, 0:P * (qt + 1)], q32[hp, h // 2, qt * P:qt * P + P],
                   k32[hp, h // 2, 0:P * (qt + 1)], True, True).then_inc(lg_psum, 1)

            def transposes(i):
                qt = i % TT
                pe.wait_ge(p_norm, i + 1)
                if i >= 2:
                    pe.wait_ge(pt_ready, i - 1)
                for s in range(qt + 1):
                    ins = pe.transpose(bank[PT_BANKS[i % 2]][:, s * P:s * P + P], prob(i, qt)[:, s * P:s * P + P],
                                       ident)
                ins.then_inc(pt_psum, 1)

            def values(i):
                h, qt = i // TT, i % TT
                pe.wait_ge(pt_ready, i + 1)
                if h % 2 == 0 and qt == 0 and h >= 4:
                    pe.wait_ge(pv_read, h // 2 - 1)
                out = bank[PV_BANKS[h // 2 % 2]][(h % 2) * 64:(h % 2) * 64 + 64, qt * P:qt * P + P]
                for s in range(qt + 1):
                    ins = mm(out, v32[:, s, h * 64:h * 64 + 64], pT[:, i % 2, s, :], s == 0, s == qt)
                ins.then_inc(pv_psum, 1)

            for i in range(3):
                logits(i)
            for i in range(32):
                if i + 3 < 32:
                    logits(i + 3)
                transposes(i)
                if i:
                    values(i - 1)
            values(31)
            pe.wait_ge(pv_read, 4)
            pe.wait_ge(act_low, AT["y_attn"] + 4)
            for w, gr in enumerate(G["out1"]):
                gemm(gr, "fm", y_hi, y_lo)
                if w:
                    stats_of("norm1", ones[:, :], 2 * w - 2, 2 * w)
            stats_of("norm1", ones[:, :], 6, 8)

            for name in ("ret_q", "ret_k"):
                for gr in G[name]:
                    gemm(gr, "fm", h_hi, h_lo, need=AT["norm1"])
            for gr in G["ret_v"]:
                gemm(gr, "tm", h_hi, h_lo)
            pe.wait_ge(copied_act, 5)
            pe.wait_ge(copied_dve, 5)
            all_banks(G["ret_v"][-1])

            def scores(i):
                h, jb = i // TT, i % TT
                if i >= 3:
                    pe.wait_ge(a_ready, i - 2)
                mm(bank[SC_BANKS[i % 3]][:, P * jb:SEQ], rk[:, h, P * jb:P * jb + P], rq[:, h, P * jb:SEQ],
                   True, True).then_inc(sc_psum, 1)

            def head_stats(h):
                pe.wait_ge(o_copied, 2 * h + 2)
                pe.wait_ge(root_ready, ROOT[f"ret{h}"])
                mm(bank[4][:, :], ones[:, :], o32[:, 0, :], True, False)
                mm(bank[4][:, :], ones[:, :], o32[:, 1, :], False, True).then_inc(mean_psum, 1)

            for i in range(3):
                scores(i)
            for h in range(4):
                for jb in range(TT):
                    i = 4 * h + jb
                    pe.wait_ge(a_ready, i + 1)
                    if i + 3 < 16:
                        scores(i + 3)
                    if jb == 0 and h >= 2:
                        pe.wait_ge(o_copied, 2 * h - 2)
                    for e in range(2):
                        c = h * 256 + e * P
                        ins = mm(bank[O_BANKS[h % 2][e]][:, P * jb:SEQ], rv[:, jb, c:c + P],
                                 ra[:, i % 4, 0:SEQ - P * jb], jb == 0, jb == TT - 1)
                        if jb == TT - 1:
                            ins.then_inc(o_psum, 1)
                    if jb == 0 and h:
                        head_stats(h - 1)
                    if jb == 2 and h:
                        pe.wait_ge(oc_ready, 2 * h)
                        stats(f"ret{h - 1}", ones[:, :])
            head_stats(3)
            pe.wait_ge(oc_ready, 8)
            stats("ret3", ones[:, :])
            pe.wait_ge(a_ready, 16)
            pe.wait_ge(o_copied, 8)
            for gr in G["ret_g"]:
                gemm(gr, "fm", h_hi, h_lo)

            def merge(n):
                for i, gr in enumerate(G[f"merge{n}"]):
                    if i % 2 == 0:
                        gemm(gr, "fm", h_hi, h_lo)
                    else:
                        gemm(gr, "fm", y_hi, y_lo, need=AT[f"y{n}"])

            merge(0)
            for name in ("gla_q", "gla_k"):
                for gr in G[name]:
                    gemm(gr, "fm", h_hi, h_lo)
            gemm(G["gla_a"][0], "fm", h_hi, h_lo)
            pe.wait_ge(copied_act, 6)
            pe.wait_ge(copied_dve, 6)
            pe.wait_ge(gla_loaded, 32)
            pe.wait_ge(root_ready, ROOT["gla0"])
            for h, gr in enumerate(G["gla_v"]):
                if h:
                    pe.wait_ge(gz_ready, h)
                mm(bank[4][:, :], al2[:, h * P:h * P + P], ga[:, :], True, True).then_inc(gz_psum, 1)
                gemm(gr, "tm", h_hi, h_lo)
                pe.wait_ge(gkd_ready, h + 1)
                if h:
                    pe.wait_ge(gkdT_ready, h)
                for t in range(TT):
                    ins = pe.transpose(bank[5][:, t * P:t * P + P], kd[:, t * P:t * P + P], ident)
                ins.then_inc(gkdT_psum, 1)
            all_banks(G["gla_v"][-1])
            pe.wait_ge(copied_act, 7)
            pe.wait_ge(copied_dve, 7)

            def chunk_states(h):
                for n in range(7):
                    pr = slice((n % 2) * 64, (n % 2) * 64 + 64)
                    ins = mm(kv_tile(n), kdT[pr, 4 * h + n // 2, :], gv[pr, n // 2, h * 256:h * 256 + 256],
                             True, True)
                ins.then_inc(kv_psum, 1)

            def chunk_scores(h):
                for t in range(TT):
                    ins = mm(bank[5][:, t * P:t * P + P], gk[:, h, t * P:t * P + P],
                             gq[:, h, t * P:t * P + P], True, True)
                ins.then_inc(sc_psum, 1)

            pe.wait_ge(gkdT_ready, 4)
            chunk_states(0)
            chunk_scores(0)
            for h in range(4):
                pe.wait_ge(a_ready, 16 + h + 1)
                pe.wait_ge(kv_read, 7 * (h + 1))
                pe.wait_ge(o_copied, 8 + 2 * h)
                for e in range(2):
                    c = h * 256 + e * P
                    for t in range(TT):
                        mm(bank[6 + e][:, t * P:t * P + P], gv[:, t, c:c + P], am[:, t, :], t == 0, False)
                    for n in range(7):
                        ins = mm(bank[6 + e][:, (n + 1) * 64:(n + 2) * 64], st[:, n, e * P:e * P + P],
                                 gq[:, h, (n + 1) * 64:(n + 2) * 64], False, n == 6)
                    ins.then_inc(o_psum, 1)
                if h + 1 < 4:
                    chunk_states(h + 1)
                    chunk_scores(h + 1)
                stats(f"gla{h}", ones[:, :])
            for gr in G["gla_g"]:
                gemm(gr, "fm", h_hi, h_lo)
            merge(1)
            gemm(G["swa_k"][0], "fm", h_hi, h_lo)
            gemm(G["swa_v"][0], "tm", h_hi, h_lo)
            for gr in G["swa_q"]:
                gemm(gr, "fm", h_hi, h_lo)
            pe.wait_ge(copied_act, 9)
            pe.wait_ge(copied_dve, 9)
            pe.wait_ge(root_ready, ROOT["gla3"] + 1)
            pe.wait_ge(o_copied, 16)

            all_banks(G["swa_q"][-1])

            def swa_logits(n):
                kvh, qb = n // TT, n % TT
                if n >= 2:
                    pe.wait_ge(lg_read, 32 + 4 * (n - 1))
                k0 = max(qb - 1, 0) * P
                w = (qb + 1) * P - k0
                for i in range(4):
                    hp = slice((i % 2) * 64, (i % 2) * 64 + 64)
                    ins = mm(bank[SL_BANKS[n % 2][i % 2]][:, (i // 2) * 256:(i // 2) * 256 + w],
                             sq[hp, 2 * kvh + i // 2, qb * P:qb * P + P], sk[hp, kvh, k0:k0 + w],
                             True, True)
                ins.then_inc(lg_psum, 1)

            def swa_transposes(n):
                pe.wait_ge(p_norm, 32 + n + 1)
                for kb in range(1 if n % TT == 0 else 2):
                    t = PT_END[n - 1] + kb if n else 32
                    if t >= 34:
                        pe.wait_ge(pt_ready, t - 1)
                    for i in range(4):
                        ins = pe.transpose(bank[ST_BANKS[t % 2]][:, i * P:i * P + P],
                                           lg[:, n % 3, i, kb * P:kb * P + P], ident)
                    ins.then_inc(pt_psum, 1)

            def swa_values(n):
                kvh, qb = n // TT, n % TT
                blocks = 1 if qb == 0 else 2
                for kb in range(blocks):
                    t = PT_END[n] - blocks + kb
                    pe.wait_ge(pt_ready, t + 1)
                    if kb == 0 and n >= 2:
                        pe.wait_ge(pv_read, 4 + n - 1)
                    mm(bank[SV_BANKS[n % 2]][:, :], svd[:, qb - blocks + 1 + kb, kvh, :],
                       spT[:, t % 4, :], kb == 0, kb == blocks - 1).then_inc(pv_psum, 1)

            swa_logits(0)
            swa_logits(1)
            for n in range(16):
                if n + 2 < 16:
                    swa_logits(n + 2)
                swa_transposes(n)
                if n:
                    swa_values(n - 1)
            swa_values(15)
            pe.wait_ge(pv_read, 4 + 16)
            merge(2)
            for w, gr in enumerate(G["out2"]):
                gemm(gr, "fm", h_hi, h_lo, need=AT["merged"])
                if w:
                    stats_of("post1", ones[:, :], 2 * w - 2, 2 * w)
            stats_of("post1", ones[:, :], 6, 8)
            stats("norm2", ones[:, :])
            for gr in G["ffn_up"]:
                gemm(gr, "fm", h_hi, h_lo, need=AT["norm2"])
            for w, gr in enumerate(G["ffn_down"]):
                gemm(gr, "fm", f_hi, f_lo, need=AT["f"])
                if w:
                    stats_of("post2", ones[:, :], 2 * w - 2, 2 * w)
            stats_of("post2", ones[:, :], 6, 8)

        @block.scalar
        def _(act):
            steps = 0

            def settle(ins):
                nonlocal steps
                steps += 1
                ins.then_inc(act_step, 1)
                act.wait_ge(act_step, steps)

            def split_high(s):
                if s >= SPLIT_TILES:
                    return
                i = SPLIT_AT[s]
                kt = STREAM[i][2][2]
                act.wait_ge(raw_loaded[i % RAW_SLOTS], 16 * (i // RAW_SLOTS + 1))
                if s >= 2:
                    act.wait_ge(*tile_used(s - 2))
                act.copy(w_hi[:, s % 2, 0:kt, :], w_raw[:, i % RAW_SLOTS, 0:kt, :]).then_inc(w_high, 1)

            def ahead(gr):
                for j in range(len(gr.kts)):
                    split_high(gr.s + j + 1)

            def high(a, dst, src=None):
                act.wait_ge(act_val, a + 1)
                act.copy(dst, tval[:, a % 2, :] if src is None else src).then_inc(act_high, 1)

            def square(name, m, src):
                i = SQ0[name] + m
                if i >= 2:
                    act.wait_ge(sq_used, i - 1)
                act.activation(sqb[:, i % 2, :], src, ACT.Square).then_inc(sq_ready, 1)

            def root_of(name, n, e=0):
                act.wait_ge(sq_used, SQ0[name] + sizes[name])
                if ROOT[name]:
                    act.wait_ge(rstd_ready, ROOT[name])
                act.activation(root[:, :], bank[4][:, :], ACT.Sqrt, bias=eps[:, e:e + 1],
                               scale=1.0 / n).then_inc(root_ready, 1)

            def norm(name, src, ready=None, ready0=0):
                for m in range(KT):
                    if ready is not None:
                        act.wait_ge(ready, ready0 + m + 1)
                    square(name, m, src[:, m, :])
                root_of(name, D)

            act.wait_ge(in_small, 80)
            act.activation(silu_c[:, :], vec[:, VEC["c"][0]:VEC["c"][1]], ACT.Silu).then_inc(c_ready, 1)
            act.wait_ge(bias_psum, 1)
            settle(act.copy(btab[:, 0:320], bank[4][0:HEADS, 0:320]))
            act.copy(btab[:, 320:640], bank[5][0:HEADS, 0:320]).then_inc(bias_copied, 1)
            act.wait_ge(setup_trig, 1)
            act.activation(sv[:, 10, :], sv[:, 9, :], ACT.Sin).then_inc(trig_ready, 1)
            act.activation(sv[:, 11, :], sv[:, 9, :], ACT.Sin, scale=0.5).then_inc(trig_ready, 1)
            for b in range(0, 8, 2):
                act.wait_ge(wint_psum, b + 1)
                dst = (wint_re, wint_im)[b // 4]
                act.copy(dst[:, 4 * (b % 4):4 * (b % 4) + 4, :],
                         bank[4][:, :].rearrange("p (i c) -> p i c", c=P)).then_inc(wint_act, 1)
            for b in range(0, 8, 2):
                act.wait_ge(strip_psum, b + 1)
                act.copy(strip[:, 4 * b:4 * b + 4, :],
                         bank[4][0:GCH, :].rearrange("p (i c) -> p i c", c=P)).then_inc(strip_act, 1)
            act.wait_ge(in_x, 16)
            act.wait_ge(consts_set, 3)
            norm("norm0", xr)
            split_high(0)
            act.wait_ge(strip_psum, 8)
            act.wait_ge(bias_stored, 16)
            for m in range(KT):
                high(AT["norm0"] + m, h_hi[:, m, :])
            for w, gr in enumerate(G["ssm_u"]):
                ahead(gr)
                act.wait_ge(group_done, 2 * gr.g + 1)
                act.wait_ge(toep_loaded, 16 * STEPS)
                for t in range(2):
                    act.copy(u4[:, 16 * w:16 * w + 16, 3 - t, :],
                             bank[pbanks(gr)[0]][:, t * WC:(t + 1) * WC]
                             .rearrange("p (g c) -> p g c", c=GCH)).then_inc(u_act, 1)
                act.wait_ge(u_act, 2 * w + 2)
                act.nop().then_inc(bank_free[pbanks(gr)[0]], 1)
            for b in range(0, 8, 2):
                act.wait_ge(ut_psum, b + 1)
                x = bank[4 + b % 4][0:64, :].rearrange("p (i k r) -> p i r k", i=4, r=2)
                settle(act.copy(ut[0:64, 4 * b:4 * b + 4, :], x[:, :, 1, :]))
                act.copy(ut[64:128, 4 * b:4 * b + 4, :], x[:, :, 0, :]).then_inc(ut_act, 1)
            for w, gr in enumerate(G["ssm_z"]):
                ahead(gr)
                for half in range(2):
                    act.wait_ge(group_done, 2 * gr.g + half + 1)
                    bk = pbanks(gr)[half]
                    act.activation(sz[:, 2 * w + half, :], bank[bk][:, :], ACT.Silu).then_inc(bank_free[bk], 1)
            for b in range(0, 8, 2):
                act.wait_ge(y_psum, b + 1)
                if b == 0:
                    act.wait_ge(ut_psum, 8)
                act.copy(u[:, :, 64 * b:64 * b + 64].rearrange("p t (i c) -> p i t c", c=GCH),
                         bank[4 + b % 4][0:64, :].rearrange("p (i t c) -> p i t c", i=4, t=STEPS)).then_inc(y_act, 1)
            for ct in range(4):
                act.wait_ge(zt_psum, ct + 1)
                act.activation(z32[:, ct, :].rearrange("p (k t) -> p k t", t=STEPS),
                               bank[4 + ct][:, :].rearrange("p (t k) -> p k t", t=STEPS),
                               ACT.Gelu_apprx_tanh).then_inc(z_ready, 1)
            for m in range(4):
                act.wait_ge(z_ready, m + 1)
                act.copy(y_hi[:, 4 + m, :], z32[:, m, :]).then_inc(act_high, 1)
            for w, gr in enumerate(G["glu"]):
                ahead(gr)
                for half in range(2):
                    m = 2 * w + half
                    bk = pbanks(gr)[half]
                    act.wait_ge(group_done, 2 * gr.g + half + 1)
                    if m >= 2:
                        act.wait_ge(sig_used, m - 1)
                    settle(act.activation(sgb[:, m % 2, :], bank[bk][:, :], ACT.Sigmoid, bias=v("b_glu", m)))
                    act.nop().then_inc(sig_ready, 1)
                    act.nop().then_inc(bank_free[bk], 1)
                for half in range(2):
                    m = 2 * w + half
                    high(AT["y_ssm"] + m, y_hi[:, m, :])
            for w, gr in enumerate(G["q_idx"]):
                ahead(gr)
                for half in range(2):
                    act.wait_ge(group_done, 2 * gr.g + half + 1)
                    bk = pbanks(gr)[half]
                    act.copy(qi[:, 2 * w + half, :], bank[bk][:, :]).then_inc(bank_free[bk], 1)
                    act.wait_ge(bank_free[bk], gr.g // 2 + 1)
            gr = G["k_idx"][0]
            ahead(gr)
            act.wait_ge(group_done, 2 * gr.g + 1)
            act.copy(ki[:, :], bank[pbanks(gr)[0]][:, :]).then_inc(bank_free[pbanks(gr)[0]], 1)
            act.wait_ge(bank_free[pbanks(gr)[0]], gr.g // 2 + 1)
            act.nop().then_inc(copied_act, 1)
            for i in range(32):
                qt = i // 8
                act.wait_ge(rel_psum, i + 1)
                if i >= 2:
                    act.wait_ge(rel_used, i - 1)
                else:
                    act.wait_ge(sig_used, 4)
                act.activation(sgb[:, i % 2, 0:P * (qt + 1)], bank[5 + i % 3][:, 0:P * (qt + 1)],
                               ACT.Relu).then_inc(relu_ready, 1)
            for i in range(8):
                name, m = ("q", i) if i < 4 else ("k", i - 4)
                gr = G[name][m // 2]
                if i % 2 == 0:
                    ahead(gr)
                if i >= 2:
                    root_of(f"qk{i - 2}", 64)
                bk = pbanks(gr)[m % 2]
                act.wait_ge(group_done, 2 * gr.g + m % 2 + 1)
                settle(act.copy((q32 if i < 4 else k32)[:, m, :], bank[bk][:, :]))
                square(f"qk{i}", 0, bank[bk][:, :])
                act.wait_ge(sq_ready, SQ0[f"qk{i}"] + 1)
                act.nop().then_inc(bank_free[bk], 1)
            for w, gr in enumerate(G["v"]):
                ahead(gr)
                if w == 0:
                    root_of("qk6", 64)
                bk = pbanks(gr)[0]
                act.wait_ge(group_done, 2 * gr.g + 1)
                settle(act.copy(v32[:, 0:2, w * WC:(w + 1) * WC],
                                bank[bk][:, :].rearrange("p (t c) -> p t c", c=WC)))
                act.nop().then_inc(bank_free[bk], 1)
                if w == 0:
                    root_of("qk7", 64)
            act.nop().then_inc(copied_act, 1)
            for w, gr in enumerate(G["attn_z"]):
                ahead(gr)
                for half in range(2):
                    act.wait_ge(group_done, 2 * gr.g + half + 1)
                    bk = pbanks(gr)[half]
                    settle(act.activation(az[:, 2 * w + half, :], bank[bk][:, :], ACT.Silu))
                    act.nop().then_inc(bank_free[bk], 1)
            act.nop().then_inc(copied_act, 1)
            for i in range(33):
                if i < 32:
                    qt = i % TT
                    act.wait_ge(lg_ready, i + 1)
                    act.activation(prob(i, qt), prob(i, qt), ACT.Exp,
                                   bias=stat[:, 1, i:i + 1], accum_out=stat[:, 2, i:i + 1]).then_inc(p_exp, 1)
                if i >= 1:
                    j = i - 1
                    qt = j % TT
                    act.wait_ge(pt_psum, j + 1)
                    if j >= 2:
                        act.wait_ge(pv_psum, j - 1)
                    act.copy(pT[:, j % 2, 0:qt + 1, :],
                             bank[PT_BANKS[j % 2]][:, 0:P * (qt + 1)].rearrange("p (s c) -> p s c", c=P))\
                       .then_inc(pt_ready, 1)
                    if j >= 8 and j % 8 == 1:
                        high(AT["y_attn"] + j // 8 - 1, y_hi[:, 3 + j // 8, :])
            high(AT["y_attn"] + 3, y_hi[:, 7, :])
            for w, gr in enumerate(G["out1"]):
                ahead(gr)
                for m in (2 * w, 2 * w + 1):
                    act.wait_ge(x1_done, m + 1)
                    square("norm1", m, xr[:, m, :])
            root_of("norm1", D)
            act.wait_ge(group_done, done("out1", 3))
            for m in range(KT):
                high(AT["norm1"] + m, h_hi[:, m, :])

            def copies(name, dst, scale=None):
                for w, gr in enumerate(G[name]):
                    ahead(gr)
                    bk = pbanks(gr)[0]
                    act.wait_ge(group_done, 2 * gr.g + 1)
                    act.activation(dst[:, 2 * w, :], bank[bk][:, :], ACT.Copy, scale=scale or 1.0)\
                       .then_inc(bank_free[bk], 1)
                    act.wait_ge(bank_free[bk], gr.g // 2 + 1)

            def copies_tm(name, dst):
                for w, gr in enumerate(G[name]):
                    ahead(gr)
                    bk = pbanks(gr)[0]
                    act.wait_ge(group_done, 2 * gr.g + 1)
                    act.copy(dst[:, 0:2, w * WC:(w + 1) * WC],
                             bank[bk][:, :].rearrange("p (t c) -> p t c", c=WC)).then_inc(bank_free[bk], 1)
                    act.wait_ge(bank_free[bk], gr.g // 2 + 1)

            def gated(name, n):
                act.wait_ge(on_ready, 8 * (n + 1))
                for w, gr in enumerate(G[name]):
                    ahead(gr)
                    for half in range(2):
                        m = 2 * w + half
                        bk = pbanks(gr)[half]
                        act.wait_ge(group_done, 2 * gr.g + half + 1)
                        act.wait_ge(sig_used, SIG[name] + m - 1)
                        act.activation(sgb[:, m % 2, :], bank[bk][:, :], ACT.Silu).then_inc(bank_free[bk], 1)
                        act.wait_ge(bank_free[bk], gr.g // 2 + 1)
                        act.nop().then_inc(sig_ready, 1)
                    for half in range(2):
                        m = 2 * w + half
                        high(AT[f"y{n}"] + m, y_hi[:, m, :])

            def merge(n):
                for i, gr in enumerate(G[f"merge{n}"]):
                    ahead(gr)
                    if i % 2 == 0:
                        for half in range(2):
                            m = i + half
                            bk = pbanks(gr)[half]
                            act.wait_ge(group_done, 2 * gr.g + half + 1)
                            act.wait_ge(sig_used, SIG[f"merge{n}"] + m - 1)
                            act.activation(sgb[:, m % 2, :], bank[bk][:, :], ACT.Sigmoid)\
                               .then_inc(bank_free[bk], 1)
                            act.wait_ge(bank_free[bk], gr.g // 2 + 1)
                            act.nop().then_inc(sig_ready, 1)

            copies("ret_q", rq)
            copies("ret_k", rk)
            copies_tm("ret_v", rv)
            act.nop().then_inc(copied_act, 2)
            for h in range(4):
                if h:
                    act.wait_ge(oc_ready, 2 * h)
                for e in range(2):
                    act.wait_ge(o_psum, 2 * h + e + 1)
                    act.copy(o32[:, e, :], bank[O_BANKS[h % 2][e]][:, :]).then_inc(o_copied, 1)
                for e in range(2):
                    act.wait_ge(oc_ready, 2 * h + e + 1)
                    square(f"ret{h}", e, oc[:, e, :])
                root_of(f"ret{h}", 256, e=1)
            gated("ret_g", 0)
            merge(0)
            copies("gla_q", gq)
            copies("gla_k", gk)
            gr = G["gla_a"][0]
            ahead(gr)
            bk = pbanks(gr)
            act.wait_ge(group_done, 2 * gr.g + 1)
            settle(act.copy(ga[:, :], bank[bk[0]][0:GCH, :]))
            act.wait_ge(group_done, 2 * gr.g + 2)
            act.nop().then_inc(bank_free[bk[0]], 1)
            act.nop().then_inc(bank_free[bk[1]], 1)
            act.nop().then_inc(copied_act, 1)
            for h, gr in enumerate(G["gla_v"]):
                act.wait_ge(gz_ready, h + 1)
                settle(act.activation(lb[:, :], la[:, :], ACT.Abs))
                settle(act.activation(lb[:, :], lb[:, :], ACT.Exp, scale=-1.0))
                act.activation(lb[:, :], lb[:, :], ACT.Ln, bias=1.0).then_inc(gsp_ready, 1)
                act.wait_ge(gb_ready, h + 1)
                act.activation(eb[:, :], lb[:, :], ACT.Exp).then_inc(gexp_ready, 1)
                act.activation(la[:, :], lb[:, :], ACT.Exp, scale=-1.0).then_inc(gexp_ready, 1)
                ahead(gr)
                bk = pbanks(gr)[0]
                act.wait_ge(group_done, 2 * gr.g + 1)
                act.copy(gv[:, 0:2, h * WC:(h + 1) * WC],
                         bank[bk][:, :].rearrange("p (t c) -> p t c", c=WC)).then_inc(bank_free[bk], 1)
                act.wait_ge(bank_free[bk], gr.g // 2 + 1)
                act.wait_ge(gkdT_psum, h + 1)
                act.copy(kdT[:, 4 * h:4 * h + 4, :], bank[5][:, :].rearrange("p (t c) -> p t c", c=P))\
                   .then_inc(gkdT_ready, 1)
            act.nop().then_inc(copied_act, 1)
            for h in range(4):
                dst = (sgb, og)[h % 2]
                if h == 0:
                    act.wait_ge(sig_used, SIG["gla_g"])
                if h >= 2:
                    act.wait_ge(on_ready, 8 + 2 * h - 2)
                for e in range(2):
                    act.wait_ge(o_psum, 8 + 2 * h + e + 1)
                    act.copy(dst[:, e, :], bank[6 + e][:, :]).then_inc(o_copied, 1)
                for e in range(2):
                    act.wait_ge(o_copied, 8 + 2 * h + e + 1)
                    square(f"gla{h}", e, dst[:, e, :])
                root_of(f"gla{h}", 256)
            gated("gla_g", 1)
            merge(1)
            gr = G["swa_k"][0]
            ahead(gr)
            for half in range(2):
                bk = pbanks(gr)[half]
                act.wait_ge(group_done, 2 * gr.g + half + 1)
                settle(act.copy(sk[0:64, 2 * half, :], bank[bk][0:64, :]))
                settle(act.copy(sk[64:128, 2 * half, :], bank[bk][0:64, :]))
                settle(act.copy(sk[0:64, 2 * half + 1, :], bank[bk][64:128, :]))
                settle(act.copy(sk[64:128, 2 * half + 1, :], bank[bk][64:128, :]))
                act.nop().then_inc(bank_free[bk], 1)
            ahead(G["swa_v"][0])
            copies("swa_q", sq, 0.125)
            act.nop().then_inc(copied_act, 2)

            def window_copies(n, pt):
                kvh, qb = n // TT, n % TT
                for _ in range(1 if qb == 0 else 2):
                    act.wait_ge(pt_psum, 32 + pt + 1)
                    if pt >= 4:
                        act.wait_ge(pv_psum, 32 + pt - 3)
                    act.copy(spT[:, pt % 4, :], bank[ST_BANKS[pt % 2]][:, :]).then_inc(pt_ready, 1)
                    pt += 1
                return pt

            def window_high(n):
                kvh = n // TT
                for i in range(2):
                    high(AT["y2"] + 2 * kvh + i, y_hi[:, 2 * kvh + i, :], yb[:, i, :])

            pt = 0
            for n in range(17):
                if n == 16:
                    pt = window_copies(15, pt)
                    window_high(15)
                    break
                kvh, qb = n // TT, n % TT
                blocks = 1 if qb == 0 else 2
                w = blocks * P
                c = 4 * n
                act.wait_ge(lg_ready, 32 + n + 1)
                for i in range(4):
                    ins = act.activation(lg[:, n % 3, i, 0:w], lg[:, n % 3, i, 0:w], ACT.Exp,
                                         bias=sst[:, 1, c + i:c + i + 1], accum_out=sst[:, 2, c + i:c + i + 1])
                settle(ins)
                settle(act.activation(sst[:, 4, c:c + 4], sst[:, 3, c:c + 4], ACT.Exp))
                act.nop().then_inc(p_exp, 1)
                if n:
                    pt = window_copies(n - 1, pt)
                if n > 1 and n % TT == 1:
                    window_high(n - 2)
            merge(2)
            for m in range(KT):
                act.wait_ge(group_done, done("merge2", 7))
                act.wait_ge(merged_ready, m + 1)
                act.copy(h_hi[:, m, :], merged[:, m, :]).then_inc(act_high, 1)
            for w, gr in enumerate(G["out2"]):
                ahead(gr)
                bk = pbanks(gr)[0]
                act.wait_ge(group_done, 2 * gr.g + 1)
                act.copy(mo[:, 2 * w, :], bank[bk][:, :]).then_inc(bank_free[bk], 1)
                act.wait_ge(bank_free[bk], gr.g // 2 + 1)
                square("post1", 2 * w, mo[:, 2 * w, :])
                act.wait_ge(mo_ready, w + 1)
                square("post1", 2 * w + 1, mo[:, 2 * w + 1, :])
            root_of("post1", D)
            norm("norm2", xr, x2_ready)
            act.wait_ge(group_done, done("out2", 3))
            for m in range(KT):
                high(AT["norm2"] + m, h_hi[:, m, :])
            for i, gr in enumerate(G["ffn_up"]):
                ahead(gr)
                if i % 2 == 0:
                    for half in range(2):
                        m = i + half
                        bk = pbanks(gr)[half]
                        act.wait_ge(group_done, 2 * gr.g + half + 1)
                        act.wait_ge(sig_used, SIG["ffn_up"] + m - 1)
                        act.activation(sgb[:, m % 2, :], bank[bk][:, :], ACT.Silu).then_inc(bank_free[bk], 1)
                        act.wait_ge(bank_free[bk], gr.g // 2 + 1)
                        act.nop().then_inc(sig_ready, 1)
                else:
                    for half in range(2):
                        high(AT["f"] + i - 1 + half, f_hi[:, i - 1 + half, :])
            for w, gr in enumerate(G["ffn_down"]):
                ahead(gr)
                bk = pbanks(gr)[0]
                act.wait_ge(group_done, 2 * gr.g + 1)
                act.copy(down[:, 2 * w, :], bank[bk][:, :]).then_inc(bank_free[bk], 1)
                act.wait_ge(bank_free[bk], gr.g // 2 + 1)
                square("post2", 2 * w, down[:, 2 * w, :])
                act.wait_ge(dn_ready, w + 1)
                square("post2", 2 * w + 1, down[:, 2 * w + 1, :])
            root_of("post2", D)

        @block.vector
        def _(dve):
            steps = 0

            def settle(ins):
                nonlocal steps
                steps += 1
                ins.then_inc(dve_step, 1)
                dve.wait_ge(dve_step, steps)

            def tt(out, a, b, op):
                settle(dve.tensor_tensor(out, a, b, op))

            def ts(out, a, s1, s2, op0, op1=None):
                settle(dve.tensor_scalar(out, a, s1, s2, op0, op1) if op1 is not None
                       else dve.tensor_scalar(out, a, s1, None, op0))

            def stt(out, a, s, b, op0, op1):
                settle(dve.scalar_tensor_tensor(out=out, in0=a, scalar=s, in1=b, op0=op0, op1=op1))

            def cmul(o, a, b, t, negative=False):
                tt(o[0], a[0], b[0], ALU.mult)
                tt(t, a[1], b[1], ALU.mult)
                tt(o[0], o[0], t, ALU.subtract)
                tt(t, a[0], b[1], ALU.mult)
                tt(o[1], a[1], b[0], ALU.mult)
                if negative:
                    stt(o[1], t, -1.0, o[1], ALU.mult, ALU.subtract)
                else:
                    tt(o[1], o[1], t, ALU.add)

            def exponential(out, x, t):
                n, f, p = sv[:, t, :], sv[:, t + 1, :], sv[:, t + 2, :]
                ts(out, x, -87.0, 88.0, ALU.max, ALU.min)
                ts(n, out, 1.4426950408889634, 12582912.0, ALU.mult, ALU.add)
                ts(n, n, 12582912.0, None, ALU.subtract)
                stt(f, n, -0.693359375, out, ALU.mult, ALU.add)
                stt(f, n, 2.12194440e-4, f, ALU.mult, ALU.add)
                ts(p, f, 1.0 / 40320, None, ALU.mult)
                for c in (1.0 / 5040, 1.0 / 720, 1.0 / 120, 1.0 / 24, 1.0 / 6, 0.5, 1.0):
                    stt(p, p, c, f, ALU.add, ALU.mult)
                ts(p, p, 1.0, None, ALU.add)
                ts(f.bitcast(i32), n, 127.0, None, ALU.add)
                ts(f.bitcast(i32), f.bitcast(i32), 23, None, ALU.logical_shift_left)
                tt(out, p, f, ALU.mult)

            def split_low(s):
                if s >= SPLIT_TILES:
                    return
                i = SPLIT_AT[s]
                kt = STREAM[i][2][2]
                dve.wait_ge(w_high, s + 1)
                dve.tensor_tensor(w_lo[:, s % 2, 0:kt, :], w_raw[:, i % RAW_SLOTS, 0:kt, :],
                                  w_hi[:, s % 2, 0:kt, :].bitcast(f32), ALU.subtract).then_inc(w_low, 1)

            def ahead(gr):
                for j in range(len(gr.kts)):
                    split_low(gr.s + j + 1)

            def new_val(a):
                if a >= 2:
                    dve.wait_ge(act_low, a - 1)
                return tval[:, a % 2, :]

            def low(a, dst, hi, src=None):
                dve.wait_ge(act_high, a + 1)
                dve.tensor_tensor(dst, tval[:, a % 2, :] if src is None else src, hi.bitcast(f32),
                                  ALU.subtract).then_inc(act_low, 1)

            def rstd_of(name):
                dve.wait_ge(root_ready, ROOT[name] + 1)
                dve.reciprocal(rstd[:, :], root[:, :]).then_inc(rstd_ready, 1)
                dve.wait_ge(rstd_ready, ROOT[name] + 1)

            def norm(name, src, gain, shift=None):
                rstd_of(name)
                for m in range(KT + 1):
                    if m < KT:
                        a = AT[name] + m
                        t = new_val(a)
                        if shift is None:
                            dve.scalar_tensor_tensor(out=t, in0=src[:, m, :], scalar=gain(m), in1=rstd[:, :],
                                                     op0=ALU.mult, op1=ALU.mult).then_inc(act_val, 1)
                        else:
                            stt(t, src[:, m, :], gain(m), rstd[:, :], ALU.mult, ALU.mult)
                            dve.tensor_scalar(t, t, shift(m), None, ALU.add).then_inc(act_val, 1)
                    if m:
                        low(AT[name] + m - 1, h_lo[:, m - 1, :], h_hi[:, m - 1, :])

            dve.wait_ge(in_ssm, 80)
            log_dt, are, aim = sv[:, 0, :], sv[:, 1, :], sv[:, 2, :]
            dt, arg = sv[:, 3, :], sv[:, 9, :]
            exponential(dt, log_dt, 4)
            re, im, mag = sv[:, 12, :], sv[:, 13, :], sv[:, 14, :]
            tt(re, are, dt, ALU.mult)
            tt(im, aim, dt, ALU.mult)
            exponential(mag, re, 4)
            turns = sv[:, 4, :]
            ts(turns, im, 0.15915494309189535, 12582912.0, ALU.mult, ALU.add)
            ts(turns, turns, 12582912.0, None, ALU.subtract)
            stt(arg, turns, -6.28125, im, ALU.mult, ALU.add)
            stt(arg, turns, -1.9350051879882812e-3, arg, ALU.mult, ALU.add)
            stt(arg, turns, -3.0199159819e-7, arg, ALU.mult, ALU.add)
            ts(arg, arg, -3.1415925, 3.1415925, ALU.max, ALU.min)
            dve.nop().then_inc(setup_trig, 1)
            dve.wait_ge(trig_ready, 2)
            sin, half_sin, cos = sv[:, 10, :], sv[:, 11, :], sv[:, 15, :]
            tt(cos, half_sin, half_sin, ALU.mult)
            ts(cos, cos, -2.0, 1.0, ALU.mult, ALU.add)
            lre, lim = sv[:, 16, :], sv[:, 17, :]
            tt(lre, mag, cos, ALU.mult)
            tt(lim, mag, sin, ALU.mult)
            lm1, den, fre, fim, t0 = (sv[:, i, :] for i in (18, 19, 20, 21, 5))
            ts(lm1, lre, 1.0, None, ALU.subtract)
            tt(den, are, are, ALU.mult)
            tt(t0, aim, aim, ALU.mult)
            tt(den, den, t0, ALU.add)
            settle(dve.reciprocal(den, den))
            tt(fre, lm1, are, ALU.mult)
            tt(t0, lim, aim, ALU.mult)
            tt(fre, fre, t0, ALU.add)
            tt(fim, lim, are, ALU.mult)
            tt(t0, lm1, aim, ALU.mult)
            tt(fim, fim, t0, ALU.subtract)
            tt(fre, fre, den, ALU.mult)
            tt(fim, fim, den, ALU.mult)

            def over_c(x):
                return x[:, :, None].to_broadcast([P, PAIRS, GCH])

            tb = tmp[:, 0:PAIRS * GCH].rearrange("p (j c) -> p j c", c=GCH)
            cmul((bb_re[:, :, :], bb_im[:, :, :]), (over_c(fre), over_c(fim)),
                 (b_re[:, :, :], b_im[:, :, :]), tb)
            settle(dve.memset(pw_re[:, 0, :], 1.0))
            settle(dve.memset(pw_im[:, 0, :], 0.0))
            settle(dve.tensor_copy(pw_re[:, 1, :], lre))
            settle(dve.tensor_copy(pw_im[:, 1, :], lim))
            n = 1
            while n < STEPS:
                top = (pw_re[:, n:n + 1, :].to_broadcast([P, n, PAIRS]),
                       pw_im[:, n:n + 1, :].to_broadcast([P, n, PAIRS]))
                cmul((pw_re[:, n + 1:2 * n + 1, :], pw_im[:, n + 1:2 * n + 1, :]),
                     (pw_re[:, 1:n + 1, :], pw_im[:, 1:n + 1, :]), top,
                     tmp[:, 0:n * PAIRS].rearrange("p (t j) -> p t j", j=PAIRS))
                n *= 2
            for half in range(2):
                js = slice(8 * half, 8 * half + 8)
                shape = [P, 8, STEPS, GCH]
                tw = tmp[:, 0:1024].rearrange("p (j t c) -> p j t c", j=8, t=STEPS)

                def power(x, t0, t1, n):
                    return x[:, t0:t1, js].rearrange("p t j -> p j t")[:, :, :, None]\
                        .to_broadcast([P, 8, n, GCH])

                cmul(tuple(w[:, js, :].rearrange("p j (t c) -> p j t c", c=GCH) for w in (win_re, win_im)),
                     tuple(x[:, js, None, :].to_broadcast(shape) for x in (bb_re, bb_im)),
                     (power(pw_re, 0, STEPS, STEPS), power(pw_im, 0, STEPS, STEPS)), tw)
            dve.nop().then_inc(win_ready, 1)
            n = STEPS + 1
            dve.wait_ge(cl_zero, 2)
            for q in range(4):
                js = slice(4 * q, 4 * q + 4)
                sh = "p (j t c) -> p j t c"
                p1 = tmp[:, 0:576].rearrange(sh, j=4, t=n)
                p2 = tmp[:, 576:1152].rearrange(sh, j=4, t=n)
                ca, cb = (x[:, js, None, :].to_broadcast([P, 4, n, GCH]) for x in (c_re, c_im))
                wa, wb = (x[:, :, js].rearrange("p t j -> p j t")[:, :, :, None].to_broadcast([P, 4, n, GCH])
                          for x in (pw_re, pw_im))
                for out, x, y, z, w, op in ((cl_re, ca, wa, cb, wb, ALU.subtract),
                                            (cl_im, ca, wb, cb, wa, ALU.add)):
                    tt(p1, x, y, ALU.mult)
                    tt(p2, z, w, ALU.mult)
                    for r in range(2):
                        rows = slice(64 * r, 64 * r + 64)
                        o = out[rows, js, r, :].rearrange("p j (t c) -> p j t c", c=GCH)
                        if op == ALU.add:
                            ts(p1[rows], p1[rows], -1.0, None, ALU.mult)
                            tt(o, p1[rows], p2[rows], ALU.subtract)
                        else:
                            tt(o, p1[rows], p2[rows], ALU.subtract)
            dve.nop().then_inc(cl_ready, 1)
            for b in range(1, 8, 2):
                dve.wait_ge(wint_psum, b + 1)
                dst = (wint_re, wint_im)[b // 4]
                dve.tensor_copy(dst[:, 4 * (b % 4):4 * (b % 4) + 4, :],
                                bank[5][:, :].rearrange("p (i c) -> p i c", c=P)).then_inc(wint_dve, 1)
            pa, pb_ = [(sv[:, 4, :], sv[:, 5, :]), (sv[:, 6, :], sv[:, 7, :])], sv[:, 8, :]
            cmul(pa[0], (cos, sin), (cos, sin), pb_)
            cmul(pa[1], pa[0], pa[0], pb_)
            cmul(pa[0], pa[1], pa[1], pb_)
            tt(rho[:, :], mag, mag, ALU.mult)
            tt(rho[:, :], rho[:, :], rho[:, :], ALU.mult)
            tt(rho[:, :], rho[:, :], rho[:, :], ALU.mult)
            settle(dve.memset(cos_t[:, :, 0:1], 1.0))
            settle(dve.memset(sin_t[:, :, 0:1], 0.0))
            n, at = 1, 0
            while n < CHUNKS:
                by = tuple(x[:, :, None].to_broadcast([P, PAIRS, n]) for x in pa[at])
                cmul((cos_t[:, :, n:2 * n], sin_t[:, :, n:2 * n]), (cos_t[:, :, 0:n], sin_t[:, :, 0:n]), by,
                     tmp[:, 0:n * PAIRS].rearrange("p (j k) -> p j k", j=PAIRS))
                n *= 2
                if n < CHUNKS:
                    cmul(pa[1 - at], pa[at], pa[at], pb_)
                    at = 1 - at
            for b in range(1, 8, 2):
                dve.wait_ge(strip_psum, b + 1)
                dve.tensor_copy(strip[:, 4 * b:4 * b + 4, :],
                                bank[5][0:GCH, :].rearrange("p (i c) -> p i c", c=P)).then_inc(strip_dve, 1)
            dve.wait_ge(strip_act, 4)
            dve.wait_ge(strip_dve, 4)
            diag = tmp[0:GCH, 0:GROUPS * GCH].rearrange("p (g c) -> p g c", c=GCH)
            tt(diag, ident[0:GCH, None, 0:GCH].to_broadcast([GCH, GROUPS, GCH]),
               dsk[:, :, None].to_broadcast([GCH, GROUPS, GCH]), ALU.mult)
            dve.tensor_tensor(strip[:, :, 0:GCH], strip[:, :, 0:GCH], diag, ALU.add).then_inc(strip_ready, 1)
            a0 = VEC["b_ada"][0]
            dve.wait_ge(ada_done, 1)
            tt(modv[:, 0:16], bank[7][:, 0:16], vec[:, a0:a0 + 16], ALU.add)
            g0 = VEC["norm_g"][0]
            dve.scalar_tensor_tensor(out=gs[:, :], in0=modv[:, 8:16], scalar=1.0, in1=vec[:, g0:g0 + 8],
                                     op0=ALU.add, op1=ALU.mult).then_inc(mod_ready, 1)
            dve.wait_ge(mod_ready, 1)
            norm("norm0", xr, lambda m: gs[:, m:m + 1], lambda m: modv[:, m:m + 1])
            split_low(0)
            for w, gr in enumerate(G["ssm_u"]):
                ahead(gr)
                dve.wait_ge(group_done, 2 * gr.g + 2)
                dve.wait_ge(toep_loaded, 16 * STEPS)
                for t in range(2):
                    dve.tensor_copy(u4[:, 16 * w:16 * w + 16, 1 - t, :],
                                    bank[pbanks(gr)[1]][:, t * WC:(t + 1) * WC]
                                    .rearrange("p (g c) -> p g c", c=GCH)).then_inc(u_dve, 1)
                dve.wait_ge(u_dve, 2 * w + 2)
                dve.nop().then_inc(bank_free[pbanks(gr)[1]], 1)
            for b in range(1, 8, 2):
                dve.wait_ge(ut_psum, b + 1)
                x = bank[4 + b % 4][0:64, :].rearrange("p (i k r) -> p i r k", i=4, r=2)
                settle(dve.tensor_copy(ut[0:64, 4 * b:4 * b + 4, :], x[:, :, 1, :]))
                dve.tensor_copy(ut[64:128, 4 * b:4 * b + 4, :], x[:, :, 0, :]).then_inc(ut_dve, 1)
            t1 = tval[:, 0, :].rearrange("p (j k) -> p j k", k=CHUNKS)
            t2 = tval[:, 1, :].rearrange("p (j k) -> p j k", k=CHUNKS)
            for half in range(2):
                js = slice(8 * half, 8 * half + 8)
                dve.wait_ge(x_psum, 2 * half + 2)
                zr = bank[4 + half][:, :].rearrange("p (j k) -> p j k", k=CHUNKS)
                zi = bank[6 + half][:, :].rearrange("p (j k) -> p j k", k=CHUNKS)
                tt(t1, zr, cos_t[:, js, :], ALU.mult)
                tt(t2, zi, sin_t[:, js, :], ALU.mult)
                tt(xa[:, js, :], t1, t2, ALU.add)
                tt(t1, zi, cos_t[:, js, :], ALU.mult)
                tt(t2, zr, sin_t[:, js, :], ALU.mult)
                tt(xb[:, js, :], t1, t2, ALU.subtract)
                for j in range(8 * half, 8 * half + 8):
                    for x in (xa, xb):
                        ins = dve.tensor_tensor_scan(x[:, j, :], rho[:, j:j + 1].to_broadcast([P, CHUNKS]),
                                                     x[:, j, :], 0.0, ALU.mult, ALU.add)
                settle(ins)
                a, b, n = xa[:, js, 0:CHUNKS - 1], xb[:, js, 0:CHUNKS - 1], CHUNKS - 1
                cs, sn = cos_t[:, js, 0:n], sin_t[:, js, 0:n]
                cmul((ga_[:, js, 1:CHUNKS], gb_[:, js, 1:CHUNKS]), (a, b), (cs, sn), t1[:, :, 0:n])
            settle(dve.memset(ga_[:, :, 0:1], 0.0))
            dve.memset(gb_[:, :, 0:1], 0.0).then_inc(state_ready, 1)
            for gr in G["ssm_z"]:
                ahead(gr)
            for b in range(1, 8, 2):
                dve.wait_ge(y_psum, b + 1)
                dve.tensor_copy(u[:, :, 64 * b:64 * b + 64].rearrange("p t (i c) -> p i t c", c=GCH),
                                bank[4 + b % 4][0:64, :].rearrange("p (i t c) -> p i t c", i=4, t=STEPS))\
                   .then_inc(y_dve, 1)
            for m in range(4):
                dve.wait_ge(z_ready, m + 1)
                dve.nop().then_inc(act_val, 1)
                low(AT["z"] + m, y_lo[:, 4 + m, :], y_hi[:, 4 + m, :], z32[:, m, :])
            for w, gr in enumerate(G["glu"]):
                ahead(gr)
                for half in range(2):
                    m = 2 * w + half
                    dve.wait_ge(sig_ready, m + 1)
                    tt(sgb[:, m % 2, :], sgb[:, m % 2, :], z32[:, m, :], ALU.mult)
                    a = AT["y_ssm"] + m
                    dve.tensor_tensor(new_val(a), sgb[:, m % 2, :], sz[:, m, :], ALU.mult).then_inc(act_val, 1)
                    dve.wait_ge(act_val, a + 1)
                    dve.nop().then_inc(sig_used, 1)
                for half in range(2):
                    m = 2 * w + half
                    low(AT["y_ssm"] + m, y_lo[:, m, :], y_hi[:, m, :])
            for gr in G["q_idx"]:
                ahead(gr)
            gr = G["k_idx"][0]
            ahead(gr)
            bk = pbanks(gr)[1]
            dve.wait_ge(group_done, 2 * gr.g + 2)
            ts(wi[:, :, :], bank[bk][:, 0:TT * HEADS].rearrange("p (t h) -> p t h", h=HEADS),
               float(HEADS) ** -0.5, None, ALU.mult)
            dve.nop().then_inc(bank_free[bk], 1)
            dve.nop().then_inc(copied_dve, 1)
            m8 = small[:, 0:8]
            rounds = 0

            def select_keys(n):
                nonlocal rounds
                for _ in range(n):
                    qt = 1 + rounds // (TOPK // 8)
                    if qt >= TT:
                        return
                    s = score[:, qt, 0:P * (qt + 1)]
                    settle(dve.max(m8, s))
                    settle(dve.match_replace(s, m8, s, NEG_TAKEN))
                    rounds += 1
                    if rounds % (TOPK // 8) == 0:
                        ts(s, s, NEG_BETWEEN, NEG_LOGIT, ALU.is_ge, ALU.mult)

            for i in range(32):
                qt, h = i // 8, i % 8
                w = P * (qt + 1)
                dve.wait_ge(relu_ready, i + 1)
                if h == 0:
                    dve.tensor_scalar(score[:, qt, 0:w], sgb[:, i % 2, 0:w], wi[:, qt, h:h + 1], None,
                                      ALU.mult).then_inc(rel_used, 1)
                else:
                    dve.scalar_tensor_tensor(out=score[:, qt, 0:w], in0=sgb[:, i % 2, 0:w],
                                             scalar=wi[:, qt, h:h + 1], in1=score[:, qt, 0:w],
                                             op0=ALU.mult, op1=ALU.add).then_inc(rel_used, 1)
                dve.wait_ge(rel_used, i + 1)
                if h == 7 and qt:
                    tt(score[:, qt, qt * P:w], score[:, qt, qt * P:w], causal, ALU.add)
                if i >= 16:
                    select_keys(1)
            ts(score[:, 0, 0:P], causal, NEG_BETWEEN / 2, NEG_LOGIT, ALU.is_lt, ALU.mult)
            ts(qg[:, :], v("q_gain", 0), 0.125, None, ALU.mult)

            def normalise_qk(i):
                rstd_of(f"qk{i}")
                x = (q32 if i < 4 else k32)[:, i % 4, :]
                stt(x, x, qg[:, 0:1] if i < 4 else v("k_gain", 0), rstd[:, :], ALU.mult, ALU.mult)

            for w, gr in enumerate(G["q"] + G["k"]):
                ahead(gr)
                select_keys(3)
                for i in (2 * w - 2, 2 * w - 1):
                    if i >= 0:
                        normalise_qk(i)
                        select_keys(1)
            for w, gr in enumerate(G["v"]):
                ahead(gr)
                if w == 0:
                    normalise_qk(6)
                    select_keys(4)
                    normalise_qk(7)
                bk = pbanks(gr)[1]
                dve.wait_ge(group_done, 2 * gr.g + 2)
                settle(dve.tensor_copy(v32[:, 2:4, w * WC:(w + 1) * WC],
                                       bank[bk][:, :].rearrange("p (t c) -> p t c", c=WC)))
                dve.nop().then_inc(bank_free[bk], 1)
                select_keys(4)
            for gr in G["attn_z"]:
                ahead(gr)
                select_keys(4)
            dve.wait_ge(ada_done, 2)
            dve.tensor_tensor(modv[:, 16:24], bank[7][:, 16:24], vec[:, a0 + 16:a0 + 24], ALU.add)\
               .then_inc(mod_ready, 1)
            dve.wait_ge(mod_ready, 2)
            dve.nop().then_inc(copied_dve, 2)
            dve.wait_ge(bias_loaded, 16)

            def masked_logits(i):
                h, qt = i // TT, i % TT
                w = P * (qt + 1)
                s = prob(i, qt)
                dve.wait_ge(lg_psum, i + 1)
                if i >= 4:
                    dve.wait_ge(pt_psum, i - 3)
                dve.tensor_tensor(s, bank[LG_BANKS[i % 3]][:, 0:w], bias[:, h, SEQ - w:SEQ], ALU.add)\
                   .then_inc(lg_read, 1)
                dve.wait_ge(lg_read, i + 1)
                settle(dve.tensor_tensor_reduce(s, s, score[:, qt, 0:w], 1.0, -3e38, ALU.add, ALU.max,
                                                stat[:, 0, i:i + 1]))
                dve.tensor_scalar(stat[:, 1, i:i + 1], stat[:, 0, i:i + 1], -1.0, None, ALU.mult)\
                   .then_inc(lg_ready, 1)

            def attn_out(j):
                m = j // 8
                a = AT["y_attn"] + m
                dve.wait_ge(pv_psum, j + 1)
                dve.tensor_tensor(new_val(a), bank[PV_BANKS[m % 2]][:, :], az[:, m, :], ALU.mult)\
                   .then_inc(act_val, 1)
                dve.wait_ge(act_val, a + 1)
                dve.nop().then_inc(pv_read, 1)
                low(a, y_lo[:, 4 + m, :], y_hi[:, 4 + m, :])

            masked_logits(0)
            masked_logits(1)
            for i in range(32):
                if i + 2 < 32:
                    masked_logits(i + 2)
                qt = i % TT
                dve.wait_ge(p_exp, i + 1)
                settle(dve.reciprocal(stat[:, 3, i:i + 1], stat[:, 2, i:i + 1]))
                dve.tensor_scalar(prob(i, qt), prob(i, qt), stat[:, 3, i:i + 1], None,
                                  ALU.mult).then_inc(p_norm, 1)
                if i >= 8 and i % 8 == 1:
                    attn_out(i - 2)
            attn_out(31)
            dve.wait_ge(x_reload, 16)
            for w, gr in enumerate(G["out1"]):
                ahead(gr)
                for half in range(2):
                    m = 2 * w + half
                    bk = pbanks(gr)[half]
                    dve.wait_ge(group_done, 2 * gr.g + half + 1)
                    dve.scalar_tensor_tensor(out=xr[:, m, :], in0=bank[bk][:, :], scalar=modv[:, 16 + m:17 + m],
                                             in1=xr[:, m, :], op0=ALU.mult, op1=ALU.add).then_inc(x1_done, 1)
                    dve.wait_ge(x1_done, m + 1)
                    dve.nop().then_inc(bank_free[bk], 1)
            norm("norm1", xr, lambda m: v("norm_mix_pre", m))

            def copies(name, dst, signal=None, scale=None):
                for w, gr in enumerate(G[name]):
                    ahead(gr)
                    bk = pbanks(gr)[1]
                    dve.wait_ge(group_done, 2 * gr.g + 2)
                    if scale is None:
                        ins = dve.tensor_copy(dst[:, 2 * w + 1, :], bank[bk][:, :])
                    else:
                        ins = dve.tensor_scalar(dst[:, 2 * w + 1, :], bank[bk][:, :], scale, None, ALU.mult)
                    ins.then_inc(bank_free[bk], 1)
                    dve.wait_ge(bank_free[bk], gr.g // 2 + 1)
                    if signal is not None:
                        dve.nop().then_inc(signal, 1)

            def copies_tm(name, dst):
                for w, gr in enumerate(G[name]):
                    ahead(gr)
                    bk = pbanks(gr)[1]
                    dve.wait_ge(group_done, 2 * gr.g + 2)
                    dve.tensor_copy(dst[:, 2:4, w * WC:(w + 1) * WC],
                                    bank[bk][:, :].rearrange("p (t c) -> p t c", c=WC)).then_inc(bank_free[bk], 1)
                    dve.wait_ge(bank_free[bk], gr.g // 2 + 1)

            def gated(name, n, bias_name=None):
                for w, gr in enumerate(G[name]):
                    ahead(gr)
                    for half in range(2):
                        m = 2 * w + half
                        a = AT[f"y{n}"] + m
                        t = new_val(a)
                        dve.wait_ge(sig_ready, SIG[name] + m + 1)
                        if bias_name:
                            ins = dve.scalar_tensor_tensor(out=t, in0=on[:, m, :], scalar=v(bias_name, m),
                                                           in1=sgb[:, m % 2, :], op0=ALU.add, op1=ALU.mult)
                        else:
                            ins = dve.tensor_tensor(t, on[:, m, :], sgb[:, m % 2, :], ALU.mult)
                        ins.then_inc(act_val, 1)
                        dve.wait_ge(act_val, a + 1)
                        dve.nop().then_inc(sig_used, 1)
                    for half in range(2):
                        m = 2 * w + half
                        low(AT[f"y{n}"] + m, y_lo[:, m, :], y_hi[:, m, :])

            def merge(n):
                for i, gr in enumerate(G[f"merge{n}"]):
                    ahead(gr)
                    if i % 2 == 0:
                        continue
                    for half in range(2):
                        m = i - 1 + half
                        bk = pbanks(gr)[half]
                        dve.wait_ge(sig_ready, SIG[f"merge{n}"] + m + 1)
                        dve.wait_ge(group_done, 2 * gr.g + half + 1)
                        g = sgb[:, m % 2, :]
                        if n == 0:
                            tt(merged[:, m, :], g, bank[bk][:, :], ALU.mult)
                        else:
                            tt(g, g, bank[bk][:, :], ALU.mult)
                            tt(merged[:, m, :], merged[:, m, :], g, ALU.add)
                        dve.nop().then_inc(bank_free[bk], 1)
                        dve.nop().then_inc(sig_used, 1)
                        if n == 2:
                            dve.nop().then_inc(merged_ready, 1)

            copies("ret_q", rq)
            copies("ret_k", rk)
            copies_tm("ret_v", rv)
            dve.nop().then_inc(copied_dve, 2)
            dve.wait_ge(dec_loaded, 16)
            dve.wait_ge(group_done, done("out1", 3))
            def decayed(i):
                h, jb = i // TT, i % TT
                dve.wait_ge(sc_psum, i + 1)
                dve.tensor_tensor(ra[:, i % 4, 0:SEQ - P * jb], bank[SC_BANKS[i % 3]][:, P * jb:SEQ],
                                  dec[:, h, 0:SEQ - P * jb], ALU.mult).then_inc(a_ready, 1)

            def centred(h):
                dve.wait_ge(mean_psum, h + 1)
                for e in range(2):
                    dve.scalar_tensor_tensor(out=oc[:, e, :], in0=bank[4][:, :], scalar=-1.0 / 256,
                                             in1=o32[:, e, :], op0=ALU.mult, op1=ALU.add).then_inc(oc_ready, 1)
                dve.wait_ge(oc_ready, 2 * h + 2)

            def normed(h):
                rstd_of(f"ret{h}")
                for e in range(2):
                    dve.scalar_tensor_tensor(out=on[:, 2 * h + e, :], in0=oc[:, e, :],
                                             scalar=v("ret_w", 2 * h + e), in1=rstd[:, :],
                                             op0=ALU.mult, op1=ALU.mult).then_inc(on_ready, 1)
                dve.wait_ge(on_ready, 2 * h + 2)

            for h in range(4):
                for jb in range(TT):
                    decayed(4 * h + jb)
                    if jb == 1 and h:
                        centred(h - 1)
                    if jb == 3 and h:
                        normed(h - 1)
            centred(3)
            normed(3)
            gated("ret_g", 0, "ret_b")
            dve.wait_ge(x1_stored, 16)
            merge(0)
            copies("gla_q", gq)
            copies("gla_k", gk)
            ahead(G["gla_a"][0])
            dve.nop().then_inc(copied_dve, 1)
            dve.wait_ge(gla_loaded, 32)
            chunks = "p (n c) -> p n c"
            for h, gr in enumerate(G["gla_v"]):
                dve.wait_ge(gz_psum, h + 1)
                dve.tensor_scalar(la[:, :], bank[4][:, :], v("gla_b", h), None, ALU.add).then_inc(gz_ready, 1)
                dve.wait_ge(gsp_ready, h + 1)
                stt(la[:, :], la[:, :], 0.0, lb[:, :], ALU.min, ALU.subtract)
                ts(la[:, :], la[:, :], 1.0 / 16, -1.0, ALU.mult, ALU.max)
                dve.tensor_tensor_scan(lb[:, :], rst[:, :], la[:, :], 0.0, ALU.mult, ALU.add).then_inc(gb_ready, 1)
                dve.wait_ge(gexp_ready, 2 * h + 2)
                ends = eb[:, :].rearrange(chunks, c=GLA_CHUNK)[:, :, GLA_CHUNK - 1:GLA_CHUNK]
                dve.scalar_tensor_tensor(out=gq[:, h, :], in0=gq[:, h, :], scalar=float(P) ** -0.5,
                                         in1=eb[:, :], op0=ALU.mult, op1=ALU.mult)
                dve.tensor_copy(ebl[:, h, :, None], ends)
                tt(gk[:, h, :], gk[:, h, :], la[:, :], ALU.mult)
                if h:
                    dve.wait_ge(gkdT_psum, h)
                dve.tensor_tensor(kd[:, :].rearrange(chunks, c=GLA_CHUNK),
                                  gk[:, h, :].rearrange(chunks, c=GLA_CHUNK),
                                  ends.to_broadcast([P, SEQ // GLA_CHUNK, GLA_CHUNK]), ALU.mult).then_inc(gkd_ready, 1)
                ahead(gr)
                bk = pbanks(gr)[1]
                dve.wait_ge(group_done, 2 * gr.g + 2)
                dve.tensor_copy(gv[:, 2:4, h * WC:(h + 1) * WC],
                                bank[bk][:, :].rearrange("p (t c) -> p t c", c=WC)).then_inc(bank_free[bk], 1)
                dve.wait_ge(bank_free[bk], gr.g // 2 + 1)
            dve.wait_ge(gkd_ready, 4)
            dve.nop().then_inc(copied_dve, 1)
            dve.wait_ge(group_done, done("merge0", 7))

            def gla_normed(h):
                rstd_of(f"gla{h}")
                for e in range(2):
                    dve.scalar_tensor_tensor(out=on[:, 2 * h + e, :], in0=(sgb, og)[h % 2][:, e, :],
                                             scalar=v("gla_w", 2 * h + e), in1=rstd[:, :],
                                             op0=ALU.mult, op1=ALU.mult).then_inc(on_ready, 1)
                dve.wait_ge(on_ready, 8 + 2 * h + 2)

            for h in range(4):
                dve.wait_ge(kv_psum, h + 1)
                for n in range(7):
                    if n == 0:
                        ins = dve.tensor_copy(st[:, 0, :], kv_tile(0))
                    else:
                        ins = dve.scalar_tensor_tensor(out=st[:, n, :], in0=st[:, n - 1, :],
                                                       scalar=ebl[:, h, n:n + 1], in1=kv_tile(n),
                                                       op0=ALU.mult, op1=ALU.add)
                    ins.then_inc(kv_read, 1)
                    dve.wait_ge(kv_read, 7 * h + n + 1)
                dve.wait_ge(sc_psum, 16 + h + 1)
                dve.tensor_tensor(am[:, :, :], bank[5][:, :].rearrange("p (t c) -> p t c", c=P),
                                  gla_mask[:, None, :].to_broadcast([P, TT, P]), ALU.mult).then_inc(a_ready, 1)
                if h:
                    gla_normed(h - 1)
            gla_normed(3)
            gated("gla_g", 1)
            merge(1)
            ahead(G["swa_k"][0])
            gr = G["swa_v"][0]
            ahead(gr)
            for half in range(2):
                bk = pbanks(gr)[half]
                dve.wait_ge(group_done, 2 * gr.g + half + 1)
                for t in range(2):
                    settle(dve.tensor_copy(
                        svd[:, 2 * half + t, :, :].rearrange("p k (r c) -> p k r c", r=2),
                        bank[bk][:, t * WC:(t + 1) * WC].rearrange("p (k c) -> p k c", c=64)
                        [:, :, None, :].to_broadcast([P, 4, 2, 64])))
                dve.nop().then_inc(bank_free[bk], 1)
            copies("swa_q", sq, scale=0.125)
            dve.nop().then_inc(copied_dve, 2)

            def window_logits(n):
                kvh, qb = n // TT, n % TT
                w = P if qb == 0 else 2 * P
                c = 4 * n
                dve.wait_ge(lg_psum, 32 + n + 1)
                if n >= 3:
                    dve.wait_ge(pt_psum, PT_END[n - 3])
                for i in range(4):
                    slope = float(np.float32(2.0 ** (-8.0 * (4 * kvh + i + 1) / 16)))
                    dve.scalar_tensor_tensor(out=lg[:, n % 3, i, 0:w], in0=swa_dist[:, 256 - w:256], scalar=-slope,
                                             in1=bank[SL_BANKS[n % 2][i % 2]][:, (i // 2) * 256:(i // 2) * 256 + w],
                                             op0=ALU.mult, op1=ALU.add).then_inc(lg_read, 1)
                dve.wait_ge(lg_read, 32 + 4 * n + 4)
                mx, nmx, dsink = sst[:, 0, c:c + 4], sst[:, 1, c:c + 4], sst[:, 3, c:c + 4]
                s0 = VEC["sinks"][0] + 4 * kvh
                settle(dve.tensor_reduce(mx, lg[:, n % 3, :, 0:w], AX.X, ALU.max))
                tt(mx, mx, vec[:, s0:s0 + 4], ALU.max)
                ts(nmx, mx, -1.0, None, ALU.mult)
                dve.tensor_tensor(dsink, vec[:, s0:s0 + 4], mx, ALU.subtract).then_inc(lg_ready, 1)

            def window_norm(n):
                w = P if n % TT == 0 else 2 * P
                c = 4 * n
                dve.wait_ge(p_exp, 32 + n + 1)
                tt(sst[:, 5, c:c + 4], sst[:, 2, c:c + 4], sst[:, 4, c:c + 4], ALU.add)
                settle(dve.reciprocal(sst[:, 6, c:c + 4], sst[:, 5, c:c + 4]))
                dve.tensor_tensor(lg[:, n % 3, :, 0:w], lg[:, n % 3, :, 0:w],
                                  sst[:, 6, c:c + 4][:, :, None].to_broadcast([P, 4, w]), ALU.mult)\
                   .then_inc(p_norm, 1)

            def window_out(n):
                kvh, qb = n // TT, n % TT
                dve.wait_ge(pv_psum, PT_END[n])
                o = bank[SV_BANKS[n % 2]][:, :].rearrange("p (m r q) -> p m r q", m=2, r=2)
                for r in range(2):
                    rows = slice(64 * r, 64 * r + 64)
                    settle(dve.tensor_copy(yb[rows, :, qb * P:qb * P + P], o[rows, :, r, :]))
                dve.nop().then_inc(pv_read, 1)
                if qb == TT - 1:
                    dve.nop().then_inc(act_val, 2)
                    for i in range(2):
                        m = 2 * kvh + i
                        low(AT["y2"] + m, y_lo[:, m, :], y_hi[:, m, :], yb[:, i, :])
                    dve.wait_ge(act_low, AT["y2"] + 2 * kvh + 2)

            window_logits(0)
            for n in range(16):
                if n + 1 < 16:
                    window_logits(n + 1)
                window_norm(n)
                if n > 1:
                    window_out(n - 2)
            window_out(14)
            window_out(15)
            merge(2)
            for m in range(KT):
                dve.nop().then_inc(act_val, 1)
                low(AT["merged"] + m, h_lo[:, m, :], h_hi[:, m, :], merged[:, m, :])
            copies("out2", mo, signal=mo_ready)
            rstd_of("post1")
            dve.wait_ge(x1_back, 16)
            for m in range(KT):
                stt(sgb[:, m % 2, :], mo[:, m, :], v("norm_mix_post", m), rstd[:, :], ALU.mult, ALU.mult)
                dve.tensor_tensor(xr[:, m, :], xr[:, m, :], sgb[:, m % 2, :], ALU.add).then_inc(x2_ready, 1)
            dve.wait_ge(x2_ready, KT)
            norm("norm2", xr, lambda m: v("norm_ffn_pre", m))
            for i, gr in enumerate(G["ffn_up"]):
                ahead(gr)
                if i % 2 == 0:
                    continue
                for half in range(2):
                    m = i - 1 + half
                    bk = pbanks(gr)[half]
                    a = AT["f"] + m
                    t = new_val(a)
                    dve.wait_ge(sig_ready, SIG["ffn_up"] + m + 1)
                    dve.wait_ge(group_done, 2 * gr.g + half + 1)
                    dve.tensor_tensor(t, sgb[:, m % 2, :], bank[bk][:, :], ALU.mult).then_inc(act_val, 1)
                    dve.wait_ge(act_val, a + 1)
                    dve.nop().then_inc(bank_free[bk], 1)
                    dve.nop().then_inc(sig_used, 1)
                for half in range(2):
                    m = i - 1 + half
                    low(AT["f"] + m, f_lo[:, m, :], f_hi[:, m, :])
            copies("ffn_down", down, signal=dn_ready)
            rstd_of("post2")
            for m in range(KT):
                stt(sgb[:, m % 2, :], down[:, m, :], v("norm_ffn_post", m), rstd[:, :], ALU.mult, ALU.mult)
                dve.tensor_tensor(down[:, m, :], xr[:, m, :], sgb[:, m % 2, :], ALU.add).then_inc(out_ready, 1)


def shape_constants():
    q, s = np.arange(P)[:, None], np.arange(P)[None, :]
    k2 = np.arange(256)[None, :]
    dist = P + q - k2
    cst = np.concatenate([
        np.eye(P), np.where(s <= q, 0.0, NEG_MASKED),
        (s >= q) & (s // GLA_CHUNK == q // GLA_CHUNK),
        np.where((dist >= 0) & (dist < P), dist, 1e30),
        q // 64 == s // 64], axis=1).astype(np.float32)
    m = np.arange(BIAS_LEN)
    bucket = np.searchsorted(np.array(BUCKET_STARTS), np.maximum(SEQ - 1 - m, 0), side="right") - 1
    onehot = (np.arange(32)[:, None] == bucket[None, :]).astype(np.float32)
    log_g = np.log1p(-np.exp2(-5.0 - np.arange(4)))
    rel = np.arange(SEQ)[None, :] - np.arange(P)[:, None]
    decay = np.exp(np.maximum(rel, 0)[:, None, :] * log_g[None, :, None]) * (rel >= 0)[:, None, :] * P ** -0.5
    reset = np.broadcast_to((np.arange(SEQ) % GLA_CHUNK != 0), (P, SEQ)).astype(np.float32)
    return cst, onehot, decay.astype(np.float32), np.ascontiguousarray(reset)


def lay_out(inputs):
    a = {k: np.asarray(x) for k, x in inputs.items()}
    mats = {"w_ada": a["w_ada"][0], "w_in": a["w_in"][0], "w_glu": a["w_glu"][0], "w_out": a["w_out"][0],
            "w_in2": a["w_in_2"][0], "w_out2": a["w_out_2"][0], "w_gate": a["ffn_w_gate_2"][0],
            "w_up": a["ffn_w_up_2"][0], "w_down": a["ffn_w_down_2"][0]}
    for n in range(3):
        mats[f"w_branch{n}"] = a["w_branch_2"][0, n]
    ws = np.zeros((len(TILES), P, KT, WC), np.float32)
    for i, (name, row0, kt, cols) in enumerate(TILES):
        at = 0
        for c0, n in cols:
            ws[i, :, 0:kt, at:at + n] = mats[name][row0:row0 + kt * P, c0:c0 + n].reshape(kt, P, n).transpose(1, 0, 2)
            at += n

    def col(x):
        return x.reshape(-1, P).T

    vecs = np.concatenate([
        col(a["c"]), col(a["norm_g"]), col(a["b_ada"]), np.tile(a["q_gain"].reshape(64, 1), (2, 1)),
        np.tile(a["k_gain"].reshape(64, 1), (2, 1)), col(a["b_glu"]), col(a["norm_mix_pre_2"]),
        col(a["norm_mix_post_2"]), col(a["ret_norm_w_2"]), col(a["ret_norm_b_2"]),
        col(a["gla_b_alpha_2"]), col(a["gla_norm_w_2"]), col(a["norm_ffn_pre_2"]),
        col(a["norm_ffn_post_2"]), np.broadcast_to(a["attn_sinks_2"].reshape(1, 16), (P, 16))], axis=1)

    def states(x):
        x = x.reshape((PAIRS, 2) + x.shape[1:])
        return np.moveaxis(x, 0, 2).reshape((P, PAIRS) + x.shape[3:])

    log_dt = np.broadcast_to(a["log_dt"][0][:, None], (GROUPS, NSTATE))
    ssm_vec = np.stack([states(x) for x in (log_dt, a["a_re"][0], a["a_im"][0])], axis=1)
    ssm_b = np.stack([states(a["b_re"][0]), states(a["b_im"][0])])
    ssm_c = np.stack([states(a[n][0].transpose(0, 2, 1)) for n in ("c_re", "c_im")])
    cst, onehot, decay, reset = shape_constants()
    return {
        "wstream": ws.reshape(len(TILES), P, KT * WC),
        "xT": a["x"][0].T.reshape(KT, P, SEQ).transpose(1, 0, 2),
        "vecs": vecs, "consts": cst, "onehot": onehot, "rel_bias": a["rel_bias"],
        "ssm_vec": ssm_vec, "ssm_b": ssm_b, "ssm_c": ssm_c,
        "d_skip": a["d_skip"][0].reshape(GROUPS, GCH).T, "alpha2": a["gla_w_alpha2_2"][0],
        "decay": decay, "reset": reset,
    }


def kernel(**inputs):
    import concourse.bacc as bacc
    from concourse.bass_utils import run_bass_kernel_spmd

    nc = bacc.Bacc("TRN2", target_bir_lowering=False, num_devices=1)
    arrays = {n: np.ascontiguousarray(x) for n, x in lay_out(inputs).items()}
    args = [nc.dram_tensor(n, x.shape, mybir.dt.from_np(x.dtype), kind="ExternalInput").ap()
            for n, x in arrays.items()]
    outT = nc.dram_tensor("outT", (P, KT, SEQ), mybir.dt.float32, kind="ExternalOutput").ap()
    hybrid_blocks(nc, *args, outT)
    r = run_bass_kernel_spmd(nc, [arrays], core_ids=[0])
    got = np.asarray(r.results[0]["outT"])
    return np.ascontiguousarray(got.transpose(1, 0, 2).reshape(D, SEQ).T[None])
```
